# Optimizing a Trainium2 kernel written in Bass

```python
import jax, jax.numpy as jnp
from jax import lax
import numpy as np
import math

D_MODEL = 1024
BATCH = 1
SEQ = 512
DEPTH = 1

HEAD_DIM = 64
NSA_HEADS = 8
NSA_KV_HEADS = 2
SWA_HEADS = 8
SWA_KV_HEADS = 2
N_HEADS = NSA_HEADS + SWA_HEADS
MIX_WIDTH = N_HEADS * HEAD_DIM
CMP_LEN = 32
CMP_STRIDE = 16
CMP_HIDDEN = 128
SEL_LEN = 64
N_SEL = 16
NSA_WINDOW = 512
NSA_Q_BLOCK = 64
SWA_WINDOW = 128
SWA_Q_BLOCK = 128
D_FF = 2816
CONV_W = 3
PLE_DIM = 256
RMS_EPS = 1e-6
NEG_INF = -1e30
FORCE_BONUS = 1e6

NSA_Q_W = NSA_HEADS * HEAD_DIM
NSA_KV_W = NSA_KV_HEADS * HEAD_DIM
NSA_GATE_W = 3 * NSA_HEADS
SWA_Q_W = SWA_HEADS * HEAD_DIM
SWA_KV_W = SWA_KV_HEADS * HEAD_DIM
IN_SPLITS = [NSA_Q_W] + [NSA_KV_W] * 6 + [NSA_GATE_W, SWA_Q_W, SWA_KV_W, SWA_KV_W]
IN_WIDTH = sum(IN_SPLITS)
IN_SPLIT_POINTS = [int(v) for v in np.cumsum(IN_SPLITS)[:-1]]


def rmsnorm(x, g):
    xf = x.astype(jnp.float32)
    y = xf * lax.rsqrt(jnp.mean(xf * xf, axis=-1, keepdims=True) + RMS_EPS)
    return (y * g.astype(jnp.float32)).astype(x.dtype)

def alibi_slopes():
    h = jnp.arange(N_HEADS, dtype=jnp.float32)
    return jnp.exp2(-8.0 * (h + 1.0) / N_HEADS)

def compress_kv(kv, pe, w1, w2):
    B, S, G, hd = kv.shape
    r = CMP_LEN // CMP_STRIDE
    seg = kv.reshape(B, S // CMP_STRIDE, CMP_STRIDE, G, hd)
    n_cmp = S // CMP_STRIDE - r + 1
    blocks = jnp.concatenate([seg[:, i:i + n_cmp] for i in range(r)], axis=2)
    blocks = blocks + pe.astype(kv.dtype)[:, None, :]
    flat = jnp.transpose(blocks, (0, 1, 3, 2, 4)).reshape(B, n_cmp, G, CMP_LEN * hd)
    hid = jax.nn.gelu(flat @ w1.astype(kv.dtype))
    return hid @ w2.astype(kv.dtype)

def nsa_attention(q, k_cmp, v_cmp, k_slc, v_slc, k_win, v_win, gates, slopes):
    B, S, H, hd = q.shape
    G = k_slc.shape[2]
    R = H // G
    C = NSA_Q_BLOCK
    n_cmp = k_cmp.shape[1]
    n_sb = S // SEL_LEN
    n_top = min(N_SEL, n_sb)
    scale = hd ** -0.5
    slopes_g = slopes.reshape(G, R)
    cmp_start = jnp.arange(n_cmp) * CMP_STRIDE
    cmp_end = cmp_start + CMP_LEN - 1
    sel_start = jnp.arange(n_sb) * SEL_LEN
    overlap = ((cmp_start[:, None] < sel_start[None, :] + SEL_LEN)
               & (cmp_end[:, None] >= sel_start[None, :])).astype(jnp.float32)
    kb = jnp.transpose(k_slc.reshape(B, n_sb, SEL_LEN, G, hd), (0, 3, 1, 2, 4))
    vb = jnp.transpose(v_slc.reshape(B, n_sb, SEL_LEN, G, hd), (0, 3, 1, 2, 4))
    pad = ((0, 0), (NSA_WINDOW, 0), (0, 0), (0, 0))
    k_wp = jnp.pad(k_win, pad)
    v_wp = jnp.pad(v_win, pad)
    bi = jnp.arange(B)[:, None, None, None]
    gi = jnp.arange(G)[None, :, None, None]
    blk = jnp.arange(n_sb)

    def one_block(c):
        t0 = c * C
        t = t0 + jnp.arange(C)
        qc = lax.dynamic_slice_in_dim(q, t0, C, axis=1).reshape(B, C, G, R, hd)
        gc = lax.dynamic_slice_in_dim(gates, t0, C, axis=1).reshape(B, C, G, R, 3)
        dist_c = (t[:, None] - cmp_end[None, :]).astype(jnp.float32)
        valid_c = dist_c >= 0
        s_c = jnp.einsum('bcgrd,bngd->bgrcn', qc, k_cmp).astype(jnp.float32) * scale
        s_c = jnp.where(valid_c, s_c - slopes_g[:, :, None, None] * dist_c, NEG_INF)
        p_c = jax.nn.softmax(s_c, axis=-1) * valid_c
        o_c = jnp.einsum('bgrcn,bngd->bcgrd', p_c.astype(v_cmp.dtype), v_cmp)
        imp = jnp.einsum('bgrcn,nj->bgcj', p_c, overlap)
        jt = t // SEL_LEN
        forced = (blk[None, :] == 0) | (blk[None, :] == jt[:, None]) | (blk[None, :] == jt[:, None] - 1)
        imp = jnp.where(forced, FORCE_BONUS, imp)
        imp = jnp.where(blk[None, :] <= jt[:, None], imp, NEG_INF)
        _, idx = lax.top_k(imp, n_top)
        ks = kb[bi, gi, idx]
        vs = vb[bi, gi, idx]
        pos = idx[..., None] * SEL_LEN + jnp.arange(SEL_LEN)
        dist_s = (t[:, None, None] - pos).astype(jnp.float32)[:, :, None]
        s_s = jnp.einsum('bcgrd,bgcnld->bgrcnl', qc, ks).astype(jnp.float32) * scale
        s_s = jnp.where(dist_s >= 0, s_s - slopes_g[None, :, :, None, None, None] * dist_s, NEG_INF)
        p_s = jax.nn.softmax(s_s, axis=(-2, -1))
        o_s = jnp.einsum('bgrcnl,bgcnld->bcgrd', p_s.astype(vs.dtype), vs)
        kw = lax.dynamic_slice_in_dim(k_wp, t0, C + NSA_WINDOW, axis=1)
        vw = lax.dynamic_slice_in_dim(v_wp, t0, C + NSA_WINDOW, axis=1)
        s_pos = t0 - NSA_WINDOW + jnp.arange(C + NSA_WINDOW)
        dist_w = t[:, None] - s_pos[None, :]
        valid_w = (dist_w >= 0) & (dist_w < NSA_WINDOW) & (s_pos[None, :] >= 0)
        s_w = jnp.einsum('bcgrd,bkgd->bgrck', qc, kw).astype(jnp.float32) * scale
        s_w = jnp.where(valid_w, s_w - slopes_g[:, :, None, None] * dist_w.astype(jnp.float32), NEG_INF)
        p_w = jax.nn.softmax(s_w, axis=-1)
        o_w = jnp.einsum('bgrck,bkgd->bcgrd', p_w.astype(vw.dtype), vw)
        o = gc[..., 0:1] * o_c + gc[..., 1:2] * o_s + gc[..., 2:3] * o_w
        return o.reshape(B, C, H * hd)

    out = lax.map(one_block, jnp.arange(S // C))
    return jnp.transpose(out, (1, 0, 2, 3)).reshape(B, S, H * hd)

def swa_attention(q, k, v, sinks, slopes):
    B, S, H, hd = q.shape
    G = k.shape[2]
    R = H // G
    C = SWA_Q_BLOCK
    n_q = S // C
    scale = hd ** -0.5
    qb = q.reshape(B, n_q, C, G, R, hd)
    pad = ((0, 0), (C, 0), (0, 0), (0, 0))
    kp = jnp.pad(k, pad).reshape(B, n_q + 1, C, G, hd)
    vp = jnp.pad(v, pad).reshape(B, n_q + 1, C, G, hd)
    kb = jnp.concatenate([kp[:, :-1], kp[:, 1:]], axis=2)
    vb = jnp.concatenate([vp[:, :-1], vp[:, 1:]], axis=2)
    i = jnp.arange(C)[:, None]
    j = jnp.arange(2 * C)[None, :]
    dist = C + i - j
    kpos = jnp.arange(n_q)[:, None, None] * C - C + j[None]
    valid = (dist >= 0) & (dist < SWA_WINDOW) & (kpos >= 0)
    slopes_g = slopes.reshape(G, R)
    s = jnp.einsum('bnqgrd,bnkgd->bngrqk', qb, kb).astype(jnp.float32) * scale
    s = s - slopes_g[:, :, None, None] * dist.astype(jnp.float32)
    s = jnp.where(valid[:, None, None], s, NEG_INF)
    sg = sinks.astype(jnp.float32).reshape(G, R)[:, :, None, None]
    m = jnp.maximum(jnp.max(s, axis=-1, keepdims=True), sg)
    e = jnp.exp(s - m)
    prob = e / (jnp.sum(e, axis=-1, keepdims=True) + jnp.exp(sg - m))
    o = jnp.einsum('bngrqk,bnkgd->bnqgrd', prob.astype(vb.dtype), vb)
    return o.reshape(B, S, H * hd)

def causal_dwconv(a, w, b):
    y = lax.conv_general_dilated(a, w[:, None, :].astype(a.dtype), window_strides=(1,),
                                 padding=[(CONV_W - 1, 0)],
                                 dimension_numbers=('NWC', 'WIO', 'NWC'),
                                 feature_group_count=a.shape[-1])
    return y + b.astype(a.dtype)

def first_inputs(seed: int = 0) -> dict:
    key = jax.random.key(seed)
    ks = jax.random.split(key, 24)
    f32 = jnp.float32
    L = DEPTH

    def nrm(k, shape, scale):
        return jax.random.normal(k, shape, f32) * scale

    def gain(k):
        return 1.0 + 0.02 * jax.random.normal(k, (L, D_MODEL), f32)

    return {
        'x': nrm(ks[0], (BATCH, SEQ, D_MODEL), 1.0),
        'p': nrm(ks[1], (DEPTH, BATCH, SEQ, PLE_DIM), 1.0),
        'attn_pre_g': gain(ks[2]),
        'w_in': nrm(ks[3], (L, D_MODEL, IN_WIDTH), D_MODEL ** -0.5),
        'cmp_pe_k': nrm(ks[4], (L, CMP_LEN, HEAD_DIM), 0.02),
        'cmp_w1_k': nrm(ks[5], (L, CMP_LEN * HEAD_DIM, CMP_HIDDEN), (CMP_LEN * HEAD_DIM) ** -0.5),
        'cmp_w2_k': nrm(ks[6], (L, CMP_HIDDEN, HEAD_DIM), CMP_HIDDEN ** -0.5),
        'cmp_pe_v': nrm(ks[7], (L, CMP_LEN, HEAD_DIM), 0.02),
        'cmp_w1_v': nrm(ks[8], (L, CMP_LEN * HEAD_DIM, CMP_HIDDEN), (CMP_LEN * HEAD_DIM) ** -0.5),
        'cmp_w2_v': nrm(ks[9], (L, CMP_HIDDEN, HEAD_DIM), CMP_HIDDEN ** -0.5),
        'sinks': nrm(ks[10], (L, SWA_HEADS), 1.0),
        'w_o': nrm(ks[11], (L, MIX_WIDTH, D_MODEL), MIX_WIDTH ** -0.5),
        'attn_post_g': gain(ks[12]),
        'mlp_pre_g': gain(ks[13]),
        'w_gate_up': nrm(ks[14], (L, D_MODEL, 2 * D_FF), D_MODEL ** -0.5),
        'conv_w': nrm(ks[15], (L, CONV_W, D_FF), CONV_W ** -0.5),
        'conv_b': nrm(ks[16], (L, D_FF), 0.01),
        'w_down': nrm(ks[17], (L, D_FF, D_MODEL), D_FF ** -0.5),
        'mlp_post_g': gain(ks[18]),
        'w_ple': nrm(ks[19], (L, PLE_DIM, D_MODEL), PLE_DIM ** -0.5),
        'w_ple_gate': nrm(ks[20], (L, D_MODEL, D_MODEL), D_MODEL ** -0.5),
    }

def first_block(x, p, attn_pre_g, w_in, cmp_pe_k, cmp_w1_k, cmp_w2_k, cmp_pe_v, cmp_w1_v, cmp_w2_v,
              sinks, w_o, attn_post_g, mlp_pre_g, w_gate_up, conv_w, conv_b, w_down, mlp_post_g,
              w_ple, w_ple_gate):
    B, S, _ = x.shape
    slopes = alibi_slopes()
    swa_slopes = slopes[:SWA_HEADS]
    nsa_slopes = slopes[SWA_HEADS:]
    for i in range(DEPTH):
        h = rmsnorm(x, attn_pre_g[i])
        proj = h @ w_in[i].astype(h.dtype)
        (q_n, kc, vc, ksl, vsl, kwn, vwn, g_n, q_s, k_s, v_s) = jnp.split(proj, IN_SPLIT_POINTS, axis=-1)
        kv_shape = (B, S, NSA_KV_HEADS, HEAD_DIM)
        k_cmp = compress_kv(kc.reshape(kv_shape), cmp_pe_k[i], cmp_w1_k[i], cmp_w2_k[i])
        v_cmp = compress_kv(vc.reshape(kv_shape), cmp_pe_v[i], cmp_w1_v[i], cmp_w2_v[i])
        gates = jax.nn.sigmoid(g_n).reshape(B, S, NSA_HEADS, 3)
        o_nsa = nsa_attention(q_n.reshape(B, S, NSA_HEADS, HEAD_DIM), k_cmp, v_cmp,
                              ksl.reshape(kv_shape), vsl.reshape(kv_shape),
                              kwn.reshape(kv_shape), vwn.reshape(kv_shape), gates, nsa_slopes)
        o_swa = swa_attention(q_s.reshape(B, S, SWA_HEADS, HEAD_DIM),
                              k_s.reshape(B, S, SWA_KV_HEADS, HEAD_DIM),
                              v_s.reshape(B, S, SWA_KV_HEADS, HEAD_DIM), sinks[i], swa_slopes)
        mix = jnp.concatenate([o_nsa, o_swa], axis=-1) @ w_o[i].astype(x.dtype)
        x = x + rmsnorm(mix, attn_post_g[i])
        h = rmsnorm(x, mlp_pre_g[i])
        gu = h @ w_gate_up[i].astype(h.dtype)
        a, u = jnp.split(gu, [D_FF], axis=-1)
        a = causal_dwconv(a, conv_w[i], conv_b[i])
        y = (jax.nn.gelu(a, approximate=True) * u) @ w_down[i].astype(h.dtype)
        x = x + rmsnorm(y, mlp_post_g[i])
        e = p[i] @ w_ple[i].astype(x.dtype)
        x = x + e * jax.nn.sigmoid(x @ w_ple_gate[i].astype(x.dtype))
    return x


DEPTH_2 = 2

CTX_LEN = 256
GRID_W = 64
N_MIXERS = 2
N_LAYERS_A = (DEPTH_2 + 1) // 2
N_LAYERS_B = DEPTH_2 // 2
BRANCH_WIDTH = D_MODEL
DA_HEAD_DIM = 64
DA_HEADS = BRANCH_WIDTH // (2 * DA_HEAD_DIM)
DA_QK_WIDTH = DA_HEADS * 2 * DA_HEAD_DIM
DA_IN_WIDTH = 2 * DA_QK_WIDTH + 2 * BRANCH_WIDTH
GQ_HEAD_DIM = 128
GQ_HEADS = BRANCH_WIDTH // GQ_HEAD_DIM
GQ_KV_HEADS = 2
GQ_Q_WIDTH = GQ_HEADS * GQ_HEAD_DIM
GQ_KV_WIDTH = GQ_KV_HEADS * GQ_HEAD_DIM
GQ_IN_WIDTH = GQ_Q_WIDTH + 2 * GQ_KV_WIDTH + BRANCH_WIDTH
ROPE_THETA = 10000.0
Q_BLOCK = 128
NORM_EPS = 1e-6


def rms_norm(x, g):
    xf = x.astype(jnp.float32)
    y = xf * lax.rsqrt(jnp.mean(xf * xf, axis=-1, keepdims=True) + NORM_EPS)
    return (y * g.astype(jnp.float32)).astype(x.dtype)

def adaln(cvec, w, b):
    m = jax.nn.silu(cvec) @ w + b
    return jnp.split(m, 3, axis=-1)

def axial_rope_tables(rows, cols, head_dim):
    axis_dim = head_dim // 2
    freqs = ROPE_THETA ** (-jnp.arange(0, axis_dim, 2, dtype=jnp.float32) / axis_dim)
    ang = jnp.concatenate([rows.astype(jnp.float32)[:, None] * freqs,
                           cols.astype(jnp.float32)[:, None] * freqs], axis=-1)
    return jnp.cos(ang), jnp.sin(ang)

def apply_rope(x, cos, sin):
    S, half = cos.shape
    shp = (1, S) + (1,) * (x.ndim - 3) + (half,)
    cs = cos.reshape(shp).astype(x.dtype)
    sn = sin.reshape(shp).astype(x.dtype)
    x1, x2 = jnp.split(x, 2, axis=-1)
    return jnp.concatenate([x1 * cs - x2 * sn, x2 * cs + x1 * sn], axis=-1)

def sweep_attention(q, k, v):
    B, Sq, Hq, Dh = q.shape
    Hkv = k.shape[2]
    G = Hq // Hkv
    Dv = v.shape[-1]
    scale = Dh ** -0.5
    k32 = k.astype(jnp.float32)
    qb = q.reshape(B, Sq // Q_BLOCK, Q_BLOCK, Hkv, G, Dh).transpose(1, 0, 2, 3, 4, 5)

    def one_block(qblk):
        s = jnp.einsum('bqhgd,bkhd->bhgqk', qblk.astype(jnp.float32), k32) * scale
        p = jax.nn.softmax(s, axis=-1)
        return jnp.einsum('bhgqk,bkhd->bqhgd', p.astype(v.dtype), v)

    out = lax.map(one_block, qb)
    return out.transpose(1, 0, 2, 3, 4, 5).reshape(B, Sq, Hq, Dv)

def lambda_init_fn(layer_idx):
    return 0.8 - 0.6 * math.exp(-0.3 * layer_idx)

def diff_attention_mixer(h, hc, w_in, w_out, lam_p, subln_g, lam_init, cos, sin, with_ctx_out):
    B, S, _ = h.shape

    def project(t):
        L = t.shape[1]
        p = t @ w_in
        q, k, v, z = jnp.split(p, [DA_QK_WIDTH, 2 * DA_QK_WIDTH, 2 * DA_QK_WIDTH + BRANCH_WIDTH], axis=-1)
        q = q.reshape(B, L, DA_HEADS, 2, DA_HEAD_DIM)
        k = k.reshape(B, L, DA_HEADS, 2, DA_HEAD_DIM)
        v = v.reshape(B, L, DA_HEADS, 2 * DA_HEAD_DIM)
        return q, k, v, z

    q, k, v, z = project(h)
    qc, kc, vc, zc = project(hc)
    q = apply_rope(q, cos, sin)
    k = apply_rope(k, cos, sin)
    k_all = jnp.concatenate([k, kc], axis=1)
    v_all = jnp.concatenate([v, vc], axis=1)

    lp = lam_p.astype(jnp.float32)
    lam = jnp.exp(jnp.sum(lp[0] * lp[1])) - jnp.exp(jnp.sum(lp[2] * lp[3])) + lam_init

    def diff(qq, kk, vv, gate):
        o1 = sweep_attention(qq[..., 0, :], kk[..., 0, :], vv)
        o2 = sweep_attention(qq[..., 1, :], kk[..., 1, :], vv)
        o = o1 - lam.astype(o1.dtype) * o2
        o = rms_norm(o, subln_g) * (1.0 - lam_init)
        o = o.reshape(o.shape[0], o.shape[1], BRANCH_WIDTH)
        return (o * jax.nn.silu(gate)) @ w_out

    y = diff(q, k_all, v_all, z)
    yc = diff(qc, kc, vc, zc) if with_ctx_out else None
    return y, yc

def gqa_mixer(h, hc, w_in, w_out, qk_g, cos, sin, with_ctx_out):
    B, S, _ = h.shape

    def project(t):
        L = t.shape[1]
        p = t @ w_in
        q, k, v, z = jnp.split(p, [GQ_Q_WIDTH, GQ_Q_WIDTH + GQ_KV_WIDTH, GQ_Q_WIDTH + 2 * GQ_KV_WIDTH], axis=-1)
        q = rms_norm(q.reshape(B, L, GQ_HEADS, GQ_HEAD_DIM), qk_g[0])
        k = rms_norm(k.reshape(B, L, GQ_KV_HEADS, GQ_HEAD_DIM), qk_g[1])
        v = v.reshape(B, L, GQ_KV_HEADS, GQ_HEAD_DIM)
        return q, k, v, z

    q, k, v, z = project(h)
    qc, kc, vc, zc = project(hc)
    q = apply_rope(q, cos, sin)
    k = apply_rope(k, cos, sin)
    k_all = jnp.concatenate([k, kc], axis=1)
    v_all = jnp.concatenate([v, vc], axis=1)

    def attend(qq, kk, vv, gate):
        o = sweep_attention(qq, kk, vv)
        o = o.reshape(o.shape[0], o.shape[1], BRANCH_WIDTH)
        return (o * jax.nn.silu(gate)) @ w_out

    y = attend(q, k_all, v_all, z)
    yc = attend(qc, kc, vc, zc) if with_ctx_out else None
    return y, yc

def second_inputs(seed: int = 0) -> dict:
    key = jax.random.key(seed)
    ks = jax.random.split(key, 16)
    f32 = jnp.float32
    D = D_MODEL
    s_in = D ** -0.5
    return {
        "x": jax.random.normal(ks[0], (BATCH, SEQ, D), f32),
        "c": jax.random.normal(ks[1], (BATCH, D), f32),
        "ctx": jax.random.normal(ks[2], (BATCH, CTX_LEN, D), f32),
        "c_ctx": jax.random.normal(ks[3], (D,), f32),
        "ada_w": jax.random.normal(ks[4], (DEPTH_2, D, 3 * D), f32) * (0.5 * s_in),
        "ada_b": jax.random.normal(ks[5], (DEPTH_2, 3 * D), f32) * 0.01,
        "pre_g": 1.0 + 0.05 * jax.random.normal(ks[6], (DEPTH_2, D), f32),
        "post_g": 1.0 + 0.05 * jax.random.normal(ks[7], (DEPTH_2, D), f32),
        "w_out": jax.random.normal(ks[8], (DEPTH_2, BRANCH_WIDTH, D), f32) * (BRANCH_WIDTH ** -0.5),
        "a_w_in": jax.random.normal(ks[9], (N_LAYERS_A, D, DA_IN_WIDTH), f32) * s_in,
        "a_lambda": jax.random.normal(ks[10], (N_LAYERS_A, 4, DA_HEAD_DIM), f32) * 0.1,
        "a_subln_g": 1.0 + 0.05 * jax.random.normal(ks[11], (N_LAYERS_A, 2 * DA_HEAD_DIM), f32),
        "b_w_in": jax.random.normal(ks[12], (N_LAYERS_B, D, GQ_IN_WIDTH), f32) * s_in,
        "b_qk_g": 1.0 + 0.05 * jax.random.normal(ks[13], (N_LAYERS_B, 2, GQ_HEAD_DIM), f32),
    }

def second_block(x, c, ctx, c_ctx, ada_w, ada_b, pre_g, post_g, w_out, a_w_in, a_lambda, a_subln_g, b_w_in, b_qk_g):
    n_tokens = x.shape[1]
    n_rows = n_tokens // GRID_W
    rows = jnp.repeat(jnp.arange(n_rows, dtype=jnp.int32), GRID_W)
    cols = jnp.tile(jnp.arange(GRID_W, dtype=jnp.int32), n_rows)
    cos_a, sin_a = axial_rope_tables(rows, cols, DA_HEAD_DIM)
    cos_b, sin_b = axial_rope_tables(rows, cols, GQ_HEAD_DIM)

    xc = ctx
    for i in range(DEPTH_2):
        last = i == DEPTH_2 - 1
        shift, scale, gate = adaln(c, ada_w[i], ada_b[i])
        shift, scale, gate = shift[:, None, :], scale[:, None, :], gate[:, None, :]
        cshift, cscale, cgate = adaln(c_ctx, ada_w[i], ada_b[i])
        h = rms_norm(x, pre_g[i]) * (1.0 + scale) + shift
        hc = rms_norm(xc, pre_g[i]) * (1.0 + cscale) + cshift
        j = i // N_MIXERS
        if i % N_MIXERS == 0:
            y, yc = diff_attention_mixer(h, hc, a_w_in[j], w_out[i], a_lambda[j], a_subln_g[j],
                                         lambda_init_fn(i), cos_a, sin_a, not last)
        else:
            y, yc = gqa_mixer(h, hc, b_w_in[j], w_out[i], b_qk_g[j], cos_b, sin_b, not last)
        x = x + gate * rms_norm(y, post_g[i])
        if not last:
            xc = xc + cgate * rms_norm(yc, post_g[i])
    return x


def setup_inputs(seed=0):
    out = dict(first_inputs(seed))
    for name, value in second_inputs(seed + 1).items():
        if name != "x":
            out[name + "_2"] = value
    return out


def reference(
    x, p, attn_pre_g, w_in, cmp_pe_k, cmp_w1_k, cmp_w2_k, cmp_pe_v, cmp_w1_v, cmp_w2_v, sinks,
    w_o, attn_post_g, mlp_pre_g, w_gate_up, conv_w, conv_b, w_down, mlp_post_g, w_ple,
    w_ple_gate, c_2, ctx_2, c_ctx_2, ada_w_2, ada_b_2, pre_g_2, post_g_2, w_out_2, a_w_in_2,
    a_lambda_2, a_subln_g_2, b_w_in_2, b_qk_g_2,
):
    x = first_block(
        x, p, attn_pre_g, w_in, cmp_pe_k, cmp_w1_k, cmp_w2_k, cmp_pe_v, cmp_w1_v, cmp_w2_v,
        sinks, w_o, attn_post_g, mlp_pre_g, w_gate_up, conv_w, conv_b, w_down, mlp_post_g,
        w_ple, w_ple_gate,
    )
    return second_block(
        x, c_2, ctx_2, c_ctx_2, ada_w_2, ada_b_2, pre_g_2, post_g_2, w_out_2, a_w_in_2,
        a_lambda_2, a_subln_g_2, b_w_in_2, b_qk_g_2,
    )


_drawn_inputs = setup_inputs


def setup_inputs(seed=0):
    import zlib

    import numpy as np

    out = dict(_drawn_inputs(seed))
    spreads = {}
    factors = {'cmp_pe_k': 8.0,
     'cmp_pe_v': 5.615,
     'attn_post_g': 3.562,
     'mlp_pre_g': 3.393,
     'conv_b': 8.0,
     'mlp_post_g': 5.152,
     'ada_b_2': 4.837,
     'pre_g_2': 3.731,
     'post_g_2': 4.706,
     'a_lambda_2': 3.996,
     'a_subln_g_2': 6.148,
     'b_qk_g_2': 8.0}
    for name, (base, spread) in spreads.items():
        noise = np.random.default_rng([zlib.crc32(name.encode()), seed]).standard_normal(out[name].shape)
        drawn = base * np.exp(spread * noise) if base else spread * noise
        out[name] = __import__('jax').numpy.asarray(drawn.astype(out[name].dtype))
    for name, factor in factors.items():
        out[name] = (out[name] * factor).astype(out[name].dtype)
    return out
```

```python
import math
from contextlib import ExitStack, contextmanager

import numpy as np
import concourse.bass as bass
from concourse import mybir

F32 = mybir.dt.float32
F32R = mybir.dt.float32r
ALU = mybir.AluOpType
ACT = mybir.ActivationFunctionType
AX = mybir.AxisListType

P = 128
S = 512
C = 256
D = 1024
KD = D // P
TX, TC = S // P, C // P
TA = TX + TC
HD = 64
GD = 128
GROUPS, PER_G = 2, 4
NCMP, CMP_W = 31, 32
CMP_L, CMP_ST = 32, 16
PE_IN = 256
FF = 2816
KF = FF // P
FT = 256
EPS = 1e-6
BIG = 1e30
HEAD = 1000
LAM_INIT = 0.8 - 0.6 * math.exp(-0.3 * 0)
GELU_C = math.sqrt(2.0 / math.pi)
GELU_A = math.sqrt(0.044715)
NSA_BIAS_W = S + TX * CMP_W
SWA_BIAS_W = 2 * P


class Mark:

    def __init__(self, sem, const, coeff=0, loop=None):
        self.sem, self.const, self.coeff, self.loop = sem, const, coeff, loop

    def value(self):
        if self.loop is None or self.coeff == 0:
            return self.const
        if self.loop.active:
            return self.loop.i * self.coeff + self.const
        return self.const + self.coeff * (self.loop.n - 1)


class Counter:

    def __init__(self, prog, name, start=0):
        self.h = prog.ctx.enter_context(prog.nc.semaphore(name))
        self.name, self.const, self.coeff, self.loop = name, start, 0, None
        prog.counters.append(self)

    def inc(self, instr, by=1):
        instr.then_inc(self.h, by)
        self.const += by
        return Mark(self, self.const, self.coeff, self.loop)


class Engine:

    def __init__(self, prog, e, name, compute=True):
        self.e, self.seen = e, {}
        self.settled = prog.ctx.enter_context(prog.nc.semaphore(name + "_settled"))
        self.done = Counter(prog, name + "_done", HEAD) if compute else None
        if compute:
            e.sem_inc(self.done.h, HEAD)
        prog.engines.append(self)

    def wait(self, *marks):
        for m in marks:
            if m is None:
                continue
            if isinstance(m, (list, tuple)):
                self.wait(*m)
                continue
            fixed = m.loop is None or m.coeff == 0 or not m.loop.active
            key = (m.sem.name, fixed)
            const = m.value() if fixed else m.const
            if self.seen.get(key, -1) >= const:
                continue
            self.seen[key] = const
            self.e.wait_ge(m.sem.h, m.value())

    def mark(self, instr):
        return self.done.inc(instr)

    def settle(self):
        self.e.sem_inc(self.settled, 1)

    def last(self):
        return Mark(self.done, self.done.const, self.done.coeff, self.done.loop)


class Last:

    def __init__(self, prog, name):
        self.prog, self.name, self.marks, self.fresh = prog, name, [], False
        prog.lasts.append(self)

    def set(self, *marks):
        self.marks, self.fresh = [m for m in marks if m is not None], True

    def get(self):
        loop = self.prog.loop_now
        if loop is None or self.fresh:
            return list(self.marks)
        before = []
        for cname, off in self.prog.counts.get((loop.name, self.name), []):
            c = self.prog.by_name(cname)
            before.append(Mark(c, loop.base[cname] + off - c.coeff, c.coeff, loop))
        return list(self.marks) + before


class Loop:
    def __init__(self, name, n):
        self.name, self.n, self.active, self.i, self.base = name, n, True, None, {}


class Prog:

    def __init__(self, nc, ctx, counts):
        self.nc, self.ctx, self.counts = nc, ctx, counts
        self.counters, self.engines, self.lasts, self.loop_now = [], [], [], None
        self.pe = Engine(self, nc.tensor, "pe")
        self.act = Engine(self, nc.scalar, "act")
        self.dve = Engine(self, nc.vector, "dve")
        self.pool = Engine(self, nc.gpsimd, "pool")
        self.sp = Engine(self, nc.sync, "sp", compute=False)

    def by_name(self, name):
        return [c for c in self.counters if c.name == name][0]

    def meet(self, *engines):
        for a in engines:
            a.wait(*[b.last() for b in engines if b.done is not None])

    @contextmanager
    def loop(self, name, n):
        loop = Loop(name, n)
        start = {c.name: c.const for c in self.counters}
        loop.base = start
        with self.nc.Fori(0, n) as i:
            loop.i = i
            for c in self.counters:
                c.coeff, c.loop = self.counts.get((name, c.name), 0), loop
            for e in self.engines:
                e.seen = {}
            for x in self.lasts:
                x.fresh = False
            self.loop_now = loop
            yield i
        for c in self.counters:
            self.counts[(name, c.name)] = c.const - start[c.name]
            c.const = start[c.name] + n * (c.const - start[c.name])
            c.coeff, c.loop = 0, None
        for x in self.lasts:
            if x.fresh:
                self.counts[(name, x.name)] = [(m.sem.name, m.const - start[m.sem.name]) for m in x.marks if m.loop is loop]
        for e in self.engines:
            e.seen = {}
        loop.active = False
        self.loop_now = None


class Weights:

    def __init__(self, prog):
        self.p = prog
        c, nc = prog.ctx, prog.nc
        self.raw = c.enter_context(nc.sbuf_tensor("w_raw", [P, 2, 2, 512], F32))
        self.hi = c.enter_context(nc.sbuf_tensor("w_hi", [P, 2, KD, 512], F32R))
        self.lo = c.enter_context(nc.sbuf_tensor("w_lo", [P, 2, KD, 512], F32R))
        self.loaded = [Counter(prog, f"w_loaded{s}") for s in range(2)]
        self.raw_read = [Last(prog, f"w_raw_read{s}") for s in range(2)]
        self.tile_read = [Last(prog, f"w_tile_read{s}") for s in range(2)]
        self.turn = 0

    def push(self, sources, row0=0, chunks=KD):
        p, slot = self.p, self.turn
        self.turn = 1 - self.turn
        width = max(c0 + n for c0, n, _ in sources)
        ready = []
        for q in range(0, chunks, 2):
            r = (q // 2) % 2
            p.sp.wait(self.raw_read[r].get())
            for c0, n, src in sources:
                rows = src[row0 + q * P:row0 + (q + 2) * P, :].rearrange("(c p) n -> p c n", p=P)
                loaded = self.loaded[r].inc(p.sp.e.dma_start(self.raw[:, r, :, c0:c0 + n], rows), 16)
            raw = self.raw[:, r, :, 0:width]
            hi, lo = self.hi[:, slot, q:q + 2, 0:width], self.lo[:, slot, q:q + 2, 0:width]
            p.pool.wait(loaded, self.tile_read[slot].get())
            p.pool.settle()
            a = p.pool.mark(p.pool.e.tensor_scalar(hi, raw, 1.0, 0.0, ALU.mult, ALU.add))
            p.pool.wait(a)
            b = p.pool.mark(p.pool.e.tensor_tensor(lo, raw, hi, ALU.subtract))
            self.raw_read[r].set(b)
            ready.append(b)
        return Tile(self, slot, ready)


class Tile:
    def __init__(self, w, slot, ready):
        self.w, self.slot, self.ready = w, slot, ready

    def hl(self, k, c0, n):
        return self.w.hi[:, self.slot, k, c0:c0 + n], self.w.lo[:, self.slot, k, c0:c0 + n]

    def release(self, mark):
        self.w.tile_read[self.slot].set(mark)


def three(e, out, a, b, start, stop):
    e.matmul(out, a[0], b[0], start=start, stop=False)
    e.matmul(out, a[0], b[1], start=False, stop=False)
    return e.matmul(out, a[1], b[0], start=False, stop=stop)


def split(prog, hi, lo, ps, ready, free, scale=None, gain=None, shift=None, tmp=None, tmp_free=None, twin=None):
    act, dve = prog.act, prog.dve
    act.wait(ready, free)
    if shift is not None:
        a = act.mark(act.e.activation(hi, ps, ACT.Identity, bias=shift, scale=gain))
    else:
        k = gain if gain is not None else (1.0 if scale is None else scale)
        a = act.mark(act.e.activation(hi, ps, ACT.Copy, scale=k))
    if twin is not None:
        a = act.mark(act.e.copy(twin, ps))
    dve.wait(ready, free, a)
    if shift is not None:
        dve.wait(tmp_free)
        t = dve.mark(dve.e.tensor_scalar(tmp, ps, gain, shift, ALU.mult, ALU.add))
        dve.wait(t, a)
        b = dve.mark(dve.e.tensor_tensor(lo, tmp, hi, ALU.subtract))
    elif gain is not None or scale is not None:
        dve.wait(a)
        b = dve.mark(dve.e.scalar_tensor_tensor(lo, ps, gain if gain is not None else scale, hi, ALU.mult, ALU.subtract))
    else:
        dve.wait(a)
        b = dve.mark(dve.e.tensor_tensor(lo, ps, hi, ALU.subtract))
    return a, b


class Kernel:
    def __init__(self, nc, ins, outs, counts):
        self.nc, self.ins, self.outs = nc, ins, outs
        self.ctx = ExitStack()
        with self.ctx:
            self.p = Prog(nc, self.ctx, counts)
            self.build()

    def sb(self, ctx, name, shape, dt=F32, side="left"):
        return ctx.enter_context(self.nc.sbuf_tensor(name, shape, dt, side=side))

    def load(self, out, src, sem=None):
        self.n_loads += 1
        c = sem or Counter(self.p, f"load{self.n_loads}")
        return c.inc(self.p.sp.e.dma_start(out, src), 16)

    def store(self, out, src, after):
        self.n_loads += 1
        c = Counter(self.p, f"store{self.n_loads}")
        self.p.sp.wait(after)
        m = c.inc(self.p.sp.e.dma_start(out, src), 16)
        self.stores.append(m)
        return m

    def row(self, v):
        return v.rearrange("(a n) -> a n", a=1).partition_broadcast(P)

    def rsqrt(self, out, ssq, n, count, ready):
        p = self.p
        p.dve.wait(ready)
        a = p.dve.mark(p.dve.e.tensor_scalar(ssq, ssq, 1.0 / count, EPS, ALU.mult, ALU.add))
        p.pool.wait(a, self.const_ready)
        return p.pool.mark(p.pool.e.tensor_tensor(out, ssq, self.minus_half[:, 0:n], ALU.pow))

    def to_columns(self, rows, nt, chunks, hi, lo, ready, gains=None, shifts=None, tmp=None):
        p, w = self.p, nt * P
        banks = 2 if w > 512 else 1
        half = w // banks
        parts = gains or [(0, nt, None, None)]
        marks = []
        for k in range(chunks):
            b0 = 2 * (k % 4)
            ps = self.ps[:, b0:b0 + banks, 0:half]
            p.pe.wait(ready, self.bank[b0].get(), self.const_ready)
            for t in range(nt):
                c = t * P
                m = p.pe.e.transpose(self.ps[:, b0 + c // half, c % half:c % half + P],
                                     rows[:, t, k * P:(k + 1) * P], self.ident[:, :])
            m = p.pe.mark(m)
            ends = []
            for t0, n, gain, shift in parts:
                for c0 in range(t0 * P, (t0 + n) * P, half):
                    c1 = min((t0 + n) * P, (c0 // half + 1) * half)
                    self.split_part(c0, c1, b0, half, k, hi, lo, m, gain, shift, tmp, ends)
            self.bank[b0].set(*ends[-1])
            marks.append(ends[-1])
        return marks[-1]

    def split_part(self, c0, c1, b0, half, k, hi, lo, m, gain, shift, tmp, ends):
        src = self.ps[:, b0 + c0 // half, c0 % half:c0 % half + c1 - c0]
        i = len(ends) % 2
        t = tmp[:, i, 0:c1 - c0] if tmp is not None else None
        ends.append(split(self.p, hi[:, k, c0:c1], lo[:, k, c0:c1], src, m, ends[-1] if ends else None,
                          gain=None if gain is None else gain[:, k:k + 1],
                          shift=None if shift is None else shift[:, k:k + 1],
                          tmp=t, tmp_free=self.p.dve.last()))

    def rms_rows(self, x, xn, nt, stat, ready):
        p = self.p
        for t in range(nt):
            p.act.wait(ready[t] if isinstance(ready, list) else ready)
            m = p.act.mark(p.act.e.activation(xn[:, t, :], x[:, t, :], ACT.Square, accum_out=stat[:, 0, t:t + 1]))
        r = self.rsqrt(stat[:, 1, 0:nt], stat[:, 0, 0:nt], nt, D, m)
        p.act.wait(r, m)
        for t in range(nt):
            m = p.act.mark(p.act.e.activation(xn[:, t, :], x[:, t, :], ACT.Copy, scale=stat[:, 1, t:t + 1]))
        return m

    def out_rows(self, jobs_ready, y, nt, nh, banks):
        p = self.p
        for t in range(nt):
            p.act.wait(jobs_ready[t])
            m = p.act.mark(p.act.e.copy(y[:, t, nh * 512:(nh + 1) * 512], self.ps[:, banks[t], :]))
            self.bank[banks[t]].set(m)
        return m

    def add_normed(self, x, y, gains, junk, ready):
        p, nt, stat = self.p, len(x), self.stat
        for t in range(nt):
            p.act.wait(ready, p.act.last())
            m = p.act.mark(p.act.e.activation(junk, y[:, t, :], ACT.Square, accum_out=stat[:, 0, t:t + 1]))
        r = self.rsqrt(stat[:, 1, 0:nt], stat[:, 0, 0:nt], nt, D, m)
        out = []
        for t in range(nt):
            p.dve.wait(r)
            a = p.dve.mark(p.dve.e.scalar_tensor_tensor(y[:, t, :], y[:, t, :], stat[:, 1, t:t + 1], gains[t],
                                                        ALU.mult, ALU.mult))
            p.dve.wait(a)
            out.append(p.dve.mark(p.dve.e.tensor_tensor(x[t], x[t], y[:, t, :], ALU.add)))
        return out

    def rows_product(self, cols, tile, chunks, t, bank, c0, n, ready, out_c0=0, start=True, stop=True, k0=0, fresh=True):
        p = self.p
        p.pe.wait(ready, self.bank[bank].get() if start and fresh else None)
        for k in range(chunks):
            p.pe.wait(tile.ready[k // 2])
            m = three(p.pe.e, self.ps[:, bank, out_c0:out_c0 + n],
                      (cols[0][:, k0 + k, t * P:(t + 1) * P], cols[1][:, k0 + k, t * P:(t + 1) * P]),
                      tile.hl(k, c0, n), start and k == 0, stop and k == chunks - 1)
        return p.pe.mark(m)

    def cols_product(self, cols, tile, chunks, bank, c0, ready, n=S):
        p = self.p
        p.pe.wait(ready, self.bank[bank].get())
        for k in range(chunks):
            p.pe.wait(tile.ready[k // 2])
            m = three(p.pe.e, self.ps[:, bank, 0:n], tile.hl(k, c0, P),
                      (cols[0][:, k, 0:n], cols[1][:, k, 0:n]), k == 0, k == chunks - 1)
        return p.pe.mark(m)

    def attention(self, units, st, pbuf, pthi, ptlo, depth, filler=None):
        p = self.p
        pe, act, dve = p.pe, p.act, p.dve
        state = {}

        def sbank(n, c):
            return (n % 2) if depth == 2 else c

        def banks_of(u):
            return (1, u["w"]) if u["w"] <= 512 else (2, u["w"] // 2)

        def scores(n):
            u = units[n]
            nb, half = banks_of(u)
            pe.wait(u.get("ready"))
            for c in range(nb):
                b = self.S0 + sbank(n, c)
                pe.wait(self.bank[b].get())
                for i, (q, k) in enumerate(u["qk"]):
                    m = pe.e.matmul(self.ps[:, b, 0:half], q, k(u["k0"] + c * half, u["k0"] + (c + 1) * half),
                                    start=i == 0, stop=i == len(u["qk"]) - 1)
            m = pe.mark(m)
            b = self.S0 + sbank(n, 0)
            sc = self.ps[:, b:b + nb, 0:half] if nb > 1 else self.ps[:, b, 0:half]
            s = st[:, n % 4, :]
            dve.wait(m)
            if u["bias"] is not None:
                dve.wait(u.get("bias_ready"))
                dve.settle()
                a = dve.mark(dve.e.tensor_tensor_reduce(sc, sc, u["bias"], 1.0, u.get("init", 3e38), ALU.add, ALU.min,
                                                        s[:, 0:1]))
            else:
                a = dve.mark(dve.e.tensor_reduce(s[:, 0:1], sc, AX.XY if nb > 1 else AX.X, ALU.min))
            pr = pbuf[:, n % depth, 0:u["w"]]
            act.wait(a)
            e = act.mark(act.e.activation(pr.rearrange("p (a b) -> p a b", a=nb) if nb > 1 else pr, sc, ACT.Exp,
                                          bias=s[:, 0:1], scale=-1.0, accum_out=s[:, 1:2]))
            if u.get("sink") is not None:
                e2 = act.mark(act.e.activation(s[:, 2:3], s[:, 0:1], ACT.Exp, bias=u["sink"]))
                state[n, "exp"] = e2
            else:
                state[n, "exp"] = e
            for c in range(nb):
                self.bank[self.S0 + sbank(n, c)].set(a, e)
            if u.get("valid") is not None:
                dve.wait(e)
                state[n, "exp"] = dve.mark(dve.e.tensor_tensor(pr, pr, u["valid"], ALU.mult))

        def turn(n):
            u = units[n]
            nk = -(-u["w"] // P)
            kw = min(P, u["w"])
            nb, per = (1, nk) if nk <= 4 else (2, nk // 2)
            pe.wait(state[n, "exp"])
            b0 = self.T0 + (n % 2 if depth == 2 else 0)
            for c in range(nb):
                pe.wait(self.bank[b0 + c].get())
            for j in range(nk):
                m = pe.e.transpose(self.ps[0:kw, b0 + j // per, (j % per) * P:(j % per + 1) * P],
                                   pbuf[:, n % depth, j * P:j * P + kw], self.ident[:, :])
            m = pe.mark(m)
            src = self.ps[0:kw, b0:b0 + nb, 0:per * P] if nb > 1 else self.ps[0:kw, b0, 0:per * P]
            hi, lo = (x[0:kw, n % depth, 0:nk * P] for x in (pthi, ptlo))
            if nb > 1:
                hi, lo = (x.rearrange("p (a b) -> p a b", a=nb) for x in (hi, lo))
            a, b = split(p, hi, lo, src, m, state.get((n - depth, "values")))
            for c in range(nb):
                self.bank[b0 + c].set(a, b)
            state[n, "turned"] = b

        def values(n):
            u = units[n]
            nk = -(-u["w"] // P)
            kw = min(P, u["w"])
            vw = u["vw"]
            o0 = (n % 4) * P
            pe.wait(state[n, "turned"], self.bank[self.O0].get())
            for j in range(nk):
                k = u["k0"] // P + j
                m = three(pe.e, self.ps[:, self.O0, o0:o0 + vw],
                          (pthi[0:kw, n % depth, j * P:(j + 1) * P], ptlo[0:kw, n % depth, j * P:(j + 1) * P]),
                          u["v"](k), j == 0, j == nk - 1)
            m = pe.mark(m)
            state[n, "values"] = m
            dve.wait(m, state[n, "exp"])
            state[n, "post"] = u["post"](self.ps[:, self.O0, o0:o0 + vw], st[:, n % 4, :])
            self.bank[self.O0].set(state[n, "post"])

        n_u = len(units)
        for n in range(n_u + depth):
            if n < n_u:
                scores(n)
            if filler is not None:
                filler(n)
            if depth == 1:
                if 0 < n:
                    values(n - 1)
                if n < n_u:
                    turn(n)
            else:
                if 0 < n <= n_u:
                    turn(n - 1)
                if n > 1:
                    values(n - 2)
        return state[n_u - 1, "post"]

    def build(self):
        nc, p, ins, ctx = self.nc, self.p, self.ins, self.ctx
        self.n_loads, self.stores = 0, []
        self.ps = ctx.enter_context(nc.psum_tensor("ps", [P, 8, 512], F32))
        self.bank = [Last(p, f"bank{b}") for b in range(8)]
        self.w = Weights(p)
        self.ident = self.sb(ctx, "ident", [P, P])
        self.minus_half = self.sb(ctx, "minus_half", [P, 8])
        self.ones = self.sb(ctx, "ones", [P, P])
        self.gx = self.sb(ctx, "gx", [P, 4, KD])
        self.cvec = self.sb(ctx, "cvec", [P, 2, KD])
        self.halves = self.sb(ctx, "halves", [P, 2, 8])
        self.gate_stored = None
        self.csil = self.sb(ctx, "csil", [P, 2, KD])
        self.adab = self.sb(ctx, "adab", [P, 2, 2 * KD])
        self.mod = self.sb(ctx, "mod", [P, 4, 2, KD])
        m = [p.pool.mark(p.pool.e.memset(self.minus_half[:, :], -0.5)), p.pool.mark(p.pool.e.memset(self.ones[:, :], 1.0))]
        loads = [self.load(self.ident[:, :], ins["ident"]),
                 self.load(self.gx[:, 0, :], ins["attn_pre_g"]), self.load(self.gx[:, 1, :], ins["mlp_pre_g"]),
                 self.load(self.gx[:, 2:4, :], ins["pre_g_2"]),
                 self.load(self.cvec[:, 0, :], ins["c_2"]), self.load(self.cvec[:, 1, :], ins["c_ctx_2"]),
                 self.load(self.adab[:, :, :], ins["ada_b_cols"])]
        self.const_ready = m + loads
        self.x_dram = nc.dram_tensor("x_scratch", [P, TX, D], F32).ap()
        self.gate_dram = nc.dram_tensor("gate_scratch", [3, D], F32).ap()
        self.engines4 = (p.pe, p.act, p.dve, p.pool)
        self.all_engines = (*self.engines4, p.sp)

        p.act.wait(self.const_ready)
        a = p.act.mark(p.act.e.activation(self.csil[:, :, :], self.cvec[:, :, :], ACT.Tanh, scale=0.5))
        p.dve.wait(a, self.const_ready)
        a = p.dve.mark(p.dve.e.scalar_tensor_tensor(self.csil[:, :, :], self.csil[:, :, :], 1.0, self.cvec[:, :, :],
                                                    ALU.add, ALU.mult))
        p.dve.wait(a)
        self.csil_ready = p.dve.mark(p.dve.e.tensor_scalar(self.csil[:, :, :], self.csil[:, :, :], 0.5, None, ALU.mult))

        with ExitStack() as s:
            self.stat = self.sb(ctx, "stat", [P, 2, 8])
            h = self.sb(s, "h_hi", [P, KD, S], F32R, "right"), self.sb(s, "h_lo", [P, KD, S], F32R, "right")
            h_ready = self.block_one_attention(h)
            self.block_one_mlp(h, h_ready, s)
        with ExitStack() as s:
            x = self.sb(s, "x", [P, TX, D], F32, "right")
            self.block_one_down(x)
            self.block_one_gate(x)
        self.differential()
        for m in self.stores:
            p.sp.wait(m)

    def xin(self):
        return self.ins["x"].rearrange("(t p) d -> p t d", p=P)

    def block_one_attention(self, h):
        p, ins = self.p, self.ins
        with ExitStack() as s:
            rows = self.sb(s, "rows1", [P, TX, D])
            lx = [self.load(rows[:, t, :], self.xin()[:, t, :]) for t in range(TX)]
            m = self.rms_rows_in_place(rows, TX, self.stat, lx)
            ready = self.to_columns(rows, TX, KD, h[0], h[1], m, gains=[(0, TX, self.gx[:, 0, :], None)])
            p.meet(*self.all_engines)
            with ExitStack() as s2:
                self.attention_groups(s2, h, ready, rows)
                p.meet(*self.all_engines)
            with ExitStack() as s2:
                ready = self.project_out(s2, h, rows)
                p.meet(*self.all_engines)
        return ready

    def attention_groups(self, s, h, h_ready, orow):
        p, nc, ins = self.p, self.nc, self.ins
        pe, act, dve, pool = self.engines4
        w_in = ins["w_in"]
        sb = lambda n, sh, dt=F32: self.sb(s, n, sh, dt)
        w1 = [sb(f"cmp_w1_{n}", [P, 16, P]) for n in "kv"]
        w2 = [sb(f"cmp_w2_{n}", [P, HD]) for n in "kv"]
        pe_t = sb("cmp_pe", [P, 2, 16])
        wg = sb("wg", [P, KD, 24])
        wg_hi, wg_lo = sb("wg_hi", [P, KD, 24], F32R), sb("wg_lo", [P, KD, 24], F32R)
        sink = sb("sink", [P, 8])
        nsink = sb("nsink", [P, 8])
        gates = sb("gates", [P, TX, 24])
        valid = sb("valid", [P, TX, CMP_W])
        small = [self.load(w1[0][:, :, :], ins["cmp_w1_k"].rearrange("(l r) h -> r l h", r=P)),
                 self.load(w1[1][:, :, :], ins["cmp_w1_v"].rearrange("(l r) h -> r l h", r=P)),
                 self.load(w2[0][:, :], ins["cmp_w2_k"]), self.load(w2[1][:, :], ins["cmp_w2_v"]),
                 self.load(pe_t[:, 0, :], ins["cmp_pe_k"]), self.load(pe_t[:, 1, :], ins["cmp_pe_v"]),
                 self.load(wg[:, :, :], w_in[:, 1280:1304].rearrange("(k p) n -> p k n", p=P)),
                 self.load(sink[:, :], self.row(ins["sinks"])), self.load(valid[:, :, :], ins["cmp_valid"])]
        dve.wait(small)
        a = dve.mark(dve.e.tensor_scalar(nsink[:, :], sink[:, :], -1.0, None, ALU.mult))
        a = dve.mark(dve.e.tensor_copy(wg_hi[:, :, :], wg[:, :, :]))
        dve.wait(a)
        wg_ready = dve.mark(dve.e.tensor_tensor(wg_lo[:, :, :], wg[:, :, :], wg_hi[:, :, :], ALU.subtract))
        pe.wait(wg_ready, h_ready, self.bank[0].get(), small)
        for t in range(TX):
            for k in range(KD):
                m = three(pe.e, self.ps[:, 0, t * 24:(t + 1) * 24],
                          (h[0][:, k, t * P:(t + 1) * P], h[1][:, k, t * P:(t + 1) * P]),
                          (wg_hi[:, k, :], wg_lo[:, k, :]), k == 0, k == KD - 1)
        m = pe.mark(m)
        act.wait(m, small)
        a = act.mark(act.e.activation(gates[:, :, :], self.ps[:, 0, 0:TX * 24].rearrange("p (t n) -> p t n", t=TX),
                                      ACT.Tanh, scale=0.5))
        self.bank[0].set(a)
        dve.wait(a)
        gates_ready = dve.mark(dve.e.tensor_scalar(gates[:, :, :], gates[:, :, :], 0.5, 0.5, ALU.mult, ALU.add))

        qst = sb("q_stacked", [P, 8, S], F32R)
        khh = sb("k_hi_twice", [P, 3, S], F32R)
        klo = sb("k_lo", [HD, 3, S], F32R)
        vhi, vlo = sb("v_hi", [P, TX, 192], F32R), sb("v_lo", [P, TX, 192], F32R)
        blocks = sb("cmp_blocks", [P, 2, 16, NCMP])
        ckhh, cklo = sb("ck_hi_twice", [P, CMP_W], F32R), sb("ck_lo", [HD, CMP_W], F32R)
        ckz = sb("ck_zero", [P, CMP_W])
        cvhi, cvlo = sb("cv_hi", [CMP_W, HD], F32R), sb("cv_lo", [CMP_W, HD], F32R)
        hid = sb("cmp_hid", [P, 3, NCMP])
        bias = sb("alibi", [P, PER_G, NSA_BIAS_W + SWA_BIAS_W])
        st = sb("st1", [P, 4, 8])
        pbuf = sb("p1", [P, 2, S])
        pthi, ptlo = sb("pt1_hi", [P, 2, S], F32R), sb("pt1_lo", [P, 2, S], F32R)
        part = sb("o_part", [P, 2, HD])
        self.S0, self.T0, self.O0 = 0, 2, 4
        bias_loaded = Counter(p, "alibi_loaded")
        attn_end = Last(p, "attn_end1")
        sink_g = sb("sink_g", [P, 2, PER_G])
        z = pool.mark(pool.e.memset(ckz[:, :], 0.0))
        dve.wait(z)
        zeroed = [dve.mark(dve.e.tensor_copy(ckhh[:, :], ckz[:, :])), dve.mark(dve.e.tensor_copy(cklo[:, :], ckz[0:HD, :])),
              dve.mark(dve.e.tensor_copy(cvhi[:, :], ckz[0:CMP_W, 0:1].to_broadcast([CMP_W, HD]))),
              dve.mark(dve.e.tensor_copy(cvlo[:, :], ckz[0:CMP_W, 0:1].to_broadcast([CMP_W, HD])))]

        with p.loop("groups", GROUPS) as g:
            at = (512, 640, 768, 1024, 1816, 1944, 896, 1152)
            kv = self.w.push([(HD * j, HD, w_in[:, bass.ds(g * HD + c0, HD)]) for j, c0 in enumerate(at)])
            qt = self.w.push([(0, 256, w_in[:, bass.ds(g * 256, 256)]), (256, 256, w_in[:, bass.ds(g * 256 + 1304, 256)])])
            p.sp.wait(attn_end.get())
            bias_ready = bias_loaded.inc(p.sp.e.dma_start(
                bias[:, :, :], ins["alibi"][bass.ds(g, 1)].rearrange("g p h n -> (g p) h n")), 16)
            ready = [self.cols_product(h, kv, KD, j, j * P, None) for j in range(3)]
            for t in range(TX):
                vm = self.rows_product(h, kv, KD, t, 3 + t // 2, 320, 192, None, out_c0=(t % 2) * 192, fresh=t % 2 == 0)
            kv.release(vm)
            dve.wait(ready[0], small)
            for j in range(2):
                for par in range(2):
                    src = self.ps[j * HD:(j + 1) * HD, 0, :]
                    src = bass.AP(src.tensor, src.offset + par, [src.ap[0], [2, 16], [CMP_ST, NCMP]])
                    vec = pe_t[par * HD:(par + 1) * HD, j, :].rearrange("p (l o) -> p l o", o=1)
                    bm = dve.mark(dve.e.tensor_tensor(blocks[par * HD:(par + 1) * HD, j, :, :], src,
                                                      vec.to_broadcast([HD, 16, NCMP]), ALU.add))
            self.bank[0].set(bm)
            for j in range(3):
                b, r0 = (1, j * HD) if j < 2 else (2, 0)
                src = self.ps[r0:r0 + HD, b, :]
                a, l = split(p, khh[0:HD, j, :], klo[:, j, :], src, ready[b], None, twin=khh[HD:P, j, :])
                self.bank[b].set(a, l)
            for b in range(2):
                src = self.ps[:, 3 + b, 0:384].rearrange("p (t n) -> p t n", t=2)
                a, l = split(p, vhi[:, 2 * b:2 * b + 2, :], vlo[:, 2 * b:2 * b + 2, :], src, vm, None)
                self.bank[3 + b].set(a, l)
            for j in range(4):
                b = 4 + j
                m = self.cols_product(h, qt, KD, b, j * P, None)
                for e in range(2):
                    a, l = split(p, qst[0:HD, 2 * j + e, :], qst[HD:P, 2 * j + e, :],
                                 self.ps[e * HD:(e + 1) * HD, b, :], m, None, scale=-(HD ** -0.5))
                self.bank[b].set(a, l)
            qt.release(m)
            for j in range(2):
                pe.wait(bm, small, self.bank[j].get())
                for l in range(16):
                    m = pe.e.matmul(self.ps[:, j, 0:NCMP], w1[j][:, l, :], blocks[:, j, l, :], start=l == 0, stop=l == 15)
                hm = self.gelu_small(hid, self.ps[:, j, 0:NCMP], pe.mark(m))
                pe.wait(hm)
                if j == 0:
                    src = self.ps[0:HD, j, 64:64 + NCMP]
                    m = pe.mark(pe.e.matmul(src, w2[0][:, :], hid[:, 0, :], start=True, stop=True))
                    a, l = split(p, ckhh[0:HD, 0:NCMP], cklo[:, 0:NCMP], src, m, zeroed, twin=ckhh[HD:P, 0:NCMP])
                else:
                    src = self.ps[0:NCMP, j, 64:128]
                    m = pe.mark(pe.e.matmul(src, hid[:, 0, :], w2[1][:, :], start=True, stop=True))
                    a, l = split(p, cvhi[0:NCMP, :], cvlo[0:NCMP, :], src, m, zeroed)
                self.bank[j].set(a, l)
            a = dve.mark(dve.e.tensor_copy(sink_g[:, 0, :], sink[:, bass.ds(g * PER_G, PER_G)]))
            dve.wait(a)
            dve.mark(dve.e.tensor_scalar(sink_g[:, 1, :], sink_g[:, 0, :], -1.0, None, ALU.mult))
            p.meet(pe, act, dve)

            def nsa_post(head, t, which):
                def post(o, s):
                    a = dve.mark(dve.e.reciprocal(s[:, 3:4], s[:, 1:2]))
                    dve.wait(a, gates_ready)
                    b = dve.mark(dve.e.tensor_tensor(s[:, 4:5], s[:, 3:4],
                                                     gates[:, t, bass.ds(g * 12 + (head * 3 + which), 1)], ALU.mult))
                    dve.wait(b)
                    if which == 0:
                        return dve.mark(dve.e.tensor_scalar(part[:, 0, :], o, s[:, 4:5], None, ALU.mult))
                    dst = part[:, 1, :] if which == 1 else orow[:, t, bass.ds(g * 256 + head * HD, HD)]
                    return dve.mark(dve.e.scalar_tensor_tensor(dst, o, s[:, 4:5], part[:, which - 1, :], ALU.mult, ALU.add))
                return post

            def swa_post(head, t):
                def post(o, s):
                    a = dve.mark(dve.e.tensor_tensor(s[:, 3:4], s[:, 1:2], s[:, 2:3], ALU.add))
                    dve.wait(a)
                    a = dve.mark(dve.e.reciprocal(s[:, 4:5], s[:, 3:4]))
                    dve.wait(a)
                    dst = orow[:, t, bass.ds(g * 256 + (512 + head * HD), HD)]
                    return dve.mark(dve.e.tensor_scalar(dst, o, s[:, 4:5], None, ALU.mult))
                return post

            def qk(head, t, hh, lo):
                return [(qst[:, head, t * P:(t + 1) * P], hh), (qst[0:HD, head, t * P:(t + 1) * P], lo)]

            units = []
            for e in range(PER_G):
                for t in range(TX):
                    units.append(dict(
                        qk=qk(e, t, lambda a, b: ckhh[:, a:b], lambda a, b: cklo[:, a:b]), k0=0, w=CMP_W,
                        bias=bias[:, e, S + t * CMP_W:S + (t + 1) * CMP_W], bias_ready=bias_ready,
                        valid=valid[:, t, :], vw=HD, v=lambda k: (cvhi[:, :], cvlo[:, :]), post=nsa_post(e, t, 0)))
                    for j in range(2):
                        c = HD * (1 + j)
                        units.append(dict(
                            qk=qk(e, t, lambda a, b, j=j: khh[:, j, a:b], lambda a, b, j=j: klo[:, j, a:b]), k0=0,
                            w=(t + 1) * P, bias=bias[:, e, (TX - 1 - t) * P:S], vw=HD,
                            v=lambda k, c=c: (vhi[:, k, c:c + HD], vlo[:, k, c:c + HD]), post=nsa_post(e, t, 1 + j)))
            for e in range(PER_G):
                for t in range(TX):
                    k0 = max(0, t - 1)
                    w = (t + 1 - k0) * P
                    units.append(dict(
                        qk=qk(4 + e, t, lambda a, b: khh[:, 2, a:b], lambda a, b: klo[:, 2, a:b]), k0=k0 * P, w=w,
                        bias=bias[:, e, NSA_BIAS_W + SWA_BIAS_W - w:NSA_BIAS_W + SWA_BIAS_W], vw=HD,
                        init=sink_g[:, 1, e:e + 1], sink=sink_g[:, 0, e:e + 1],
                        v=lambda k: (vhi[:, k, 0:HD], vlo[:, k, 0:HD]), post=swa_post(e, t)))
            attn_end.set(self.attention(units, st, pbuf, pthi, ptlo, 2))
            p.meet(pe, act, dve)

    def gelu_small(self, hid, x, ready):
        act, dve = self.p.act, self.p.dve
        act.wait(ready)
        a = act.mark(act.e.activation(hid[:, 1, :], x, ACT.Square, scale=GELU_A))
        dve.wait(a)
        b = dve.mark(dve.e.scalar_tensor_tensor(hid[:, 2, :], hid[:, 1, :], 1.0, x, ALU.add, ALU.mult))
        act.wait(b)
        a = act.mark(act.e.activation(hid[:, 1, :], hid[:, 2, :], ACT.Tanh, scale=GELU_C))
        dve.wait(a)
        b = dve.mark(dve.e.scalar_tensor_tensor(hid[:, 2, :], hid[:, 1, :], 1.0, x, ALU.add, ALU.mult))
        dve.wait(b, self.p.pe.last())
        return dve.mark(dve.e.tensor_scalar(hid[:, 0, :], hid[:, 2, :], 0.5, None, ALU.mult))

    def modulation_buffers(self, s, layer):
        m = dict(layer=layer, acc=self.sb(s, f"mod_acc{layer}", [P, 2, 3 * D]),
                 piece=self.sb(s, f"mod_piece{layer}", [P, 2, 3 * D]),
                 loaded=[Counter(self.p, f"mod_loaded{layer}{i}") for i in range(2)],
                 read=[Last(self.p, f"mod_read{layer}{i}") for i in range(2)])
        p = self.p
        z = p.pool.mark(p.pool.e.memset(m["acc"][:, :, :], 0.0))
        m["zero"] = z
        return m

    def modulation_step(self, m, i, k):
        p, layer = self.p, m["layer"]
        p.act.wait(m["read"][i].get())
        src = self.ins["ada_w_2"][layer].rearrange("(k p) n -> p k n", p=P)[:, bass.ds(k, 1), :]
        loaded = m["loaded"][i].inc(p.act.e.dma_start(m["piece"][:, i:i + 1, :], src), 16)
        p.dve.wait(loaded, m["zero"], self.csil_ready)
        for stream in range(2):
            n = 2 * D if (layer, stream) == (1, 1) else 3 * D
            acc = m["acc"][:, stream, 0:n]
            p.dve.wait(p.dve.last())
            r = p.dve.mark(p.dve.e.scalar_tensor_tensor(acc, m["piece"][:, i, 0:n],
                                                        self.csil[:, stream, bass.ds(k, 1)], acc, ALU.mult, ALU.add))
        m["read"][i].set(r)

    def modulation_end(self, s, m):
        p, layer, ins = self.p, m["layer"], self.ins
        rows = self.sb(s, f"mod_rows{layer}", [1, 3, D])
        lb = self.load(rows[:, 0, :], ins["ada_b_2"][layer:layer + 1, 2 * D:3 * D])
        lg = self.load(rows[:, 1, :], ins["post_g_2"][layer:layer + 1, :])
        p.pe.wait(p.dve.last(), self.const_ready)
        for stream in range(2):
            acc = m["acc"]
            b = 5 + stream
            p.pe.wait(self.bank[b].get())
            for j in range(2 * KD):
                t = p.pe.e.matmul(self.ps[:, b, j:j + 1], acc[:, stream, j * P:(j + 1) * P], self.ones[:, 0:1], start=True, stop=True)
            t = p.pe.mark(t)
            mod = self.mod[:, 2 * layer + stream, :, :]
            p.dve.wait(t)
            a = p.dve.mark(p.dve.e.tensor_tensor(mod, self.ps[:, b, 0:2 * KD].rearrange("p (a k) -> p a k", a=2),
                                                 self.adab[:, layer, :].rearrange("p (a k) -> p a k", a=2), ALU.add))
            self.bank[b].set(a)
            p.dve.wait(a)
            a = p.dve.mark(p.dve.e.scalar_tensor_tensor(mod[:, 1, :], mod[:, 1, :], 1.0, self.gx[:, 2 + layer, :], ALU.add, ALU.mult))
            if (layer, stream) == (1, 1):
                continue
            p.pe.wait(self.bank[7].get())
            for hf in range(2):
                p.pe.wait(self.bank[7].get())
                t = p.pe.mark(p.pe.e.matmul(self.ps[0:1, 7, :], self.ones[:, 0:1],
                                            acc[:, stream, 2 * D + hf * 512:2 * D + (hf + 1) * 512], start=True, stop=True))
                p.dve.wait(t, lb, lg, p.dve.last(), self.gate_stored)
                a = p.dve.mark(p.dve.e.tensor_tensor(rows[:, 2, hf * 512:(hf + 1) * 512], self.ps[0:1, 7, :],
                                                     rows[:, 0, hf * 512:(hf + 1) * 512], ALU.add))
                self.bank[7].set(a)
            p.dve.wait(a)
            a = p.dve.mark(p.dve.e.tensor_tensor(rows[:, 2, :], rows[:, 2, :], rows[:, 1, :], ALU.mult))
            self.gate_stored = self.store(self.gate_dram[2 * layer + stream:2 * layer + stream + 1, :], rows[:, 2, :], a)
        self.p.dve.wait(self.gate_stored)

    def project_out(self, s, h, rows):
        p, ins = self.p, self.ins
        x = self.sb(s, "x2", [P, TX, D])
        gain = self.sb(s, "post1", [P, D])
        junk = self.sb(s, "junk2", [P, D])
        mod = self.modulation_buffers(s, 0)
        lx = [self.load(x[:, :, :], self.xin()), self.load(gain[:, :], self.row(ins["attn_post_g"]))]
        ready = self.to_columns(rows, TX, KD, h[0], h[1], p.dve.last())
        done = []
        for nh in range(2):
            w = self.w.push([(0, 512, ins["w_o"][:, nh * 512:(nh + 1) * 512])])
            done.append([self.rows_product(h, w, KD, t, 4 * nh + t, 0, 512, ready) for t in range(TX)])
            w.release(done[-1][-1])
        with p.loop("modulation0", KD // 2) as i:
            for e in range(2):
                self.modulation_step(mod, e, i * 2 + e)
        for nh in range(2):
            m = self.out_rows(done[nh], rows, TX, nh, [4 * nh + t for t in range(TX)])
        self.modulation_end(s, mod)
        p.dve.wait(lx)
        a = self.add_normed([x[:, t, :] for t in range(TX)], rows, [gain[:, :]] * TX, junk[:, :], m)
        self.x_stored = self.store(self.x_dram[:, :, :], x[:, :, :], a[-1])
        m = self.rms_rows(x, rows, TX, self.stat, a)
        ready = self.to_columns(rows, TX, KD, h[0], h[1], m, gains=[(0, TX, self.gx[:, 1, :], None)])
        p.dve.wait(self.x_stored)
        return ready

    def block_one_mlp(self, h, h_ready, s_h):
        self.s_gated = ExitStack()
        s = self.s_gated
        self.gated = self.sb(s, "g_hi", [P, KF, S], F32R), self.sb(s, "g_lo", [P, KF, S], F32R)
        with ExitStack() as s2:
            self.gate_up(s2, h, h_ready, *self.gated)
            self.p.meet(*self.all_engines)

    def block_one_down(self, x):
        p, ins = self.p, self.ins
        pe, act, dve, pool = self.engines4
        with self.s_gated as s:
            y = self.sb(s, "y4", [P, TX, D])
            gain = self.sb(s, "post2", [P, D])
            junk = self.sb(s, "junk4", [P, D])
            p.sp.wait(dve.last(), act.last(), pe.last(), self.x_stored)
            lx = [self.load(x[:, :, :], self.x_dram[:, :, :]), self.load(gain[:, :], self.row(ins["mlp_post_g"]))]
            parts = (8, 6, 4, 4)
            with p.loop("w_down", 2) as nh:
                k0 = 0
                for c in parts:
                    w = self.w.push([(0, 512, ins["w_down"][:, bass.ds(nh * 512, 512)])], row0=k0 * P, chunks=c)
                    done = [self.rows_product(self.gated, w, c, t, t, 0, 512, None, start=k0 == 0, stop=k0 + c == KF, k0=k0)
                            for t in range(TX)]
                    w.release(done[-1])
                    k0 += c
                for t in range(TX):
                    act.wait(done[t])
                    m = act.mark(act.e.copy(y[:, t, bass.ds(nh * 512, 512)], self.ps[:, t, :]))
                    self.bank[t].set(m)
            dve.wait(lx)
            self.x_ready = self.add_normed([x[:, t, :] for t in range(TX)], y, [gain[:, :]] * TX, junk[:, :], act.last())
            p.meet(*self.all_engines)

    def rms_rows_in_place(self, x, nt, stat, ready):
        p = self.p
        act = p.act
        act.wait(ready)
        for t in range(nt):
            for hf in range(2):
                act.wait(self.bank[hf].get())
                m = act.mark(act.e.activation(self.ps[:, hf, :], x[:, t, hf * 512:(hf + 1) * 512], ACT.Square,
                                              accum_out=self.halves[:, hf, t:t + 1]))
                self.bank[hf].set(m)
        p.dve.wait(m)
        a = p.dve.mark(p.dve.e.tensor_tensor(stat[:, 0, 0:nt], self.halves[:, 0, 0:nt], self.halves[:, 1, 0:nt], ALU.add))
        r = self.rsqrt(stat[:, 1, 0:nt], stat[:, 0, 0:nt], nt, D, a)
        act.wait(r, m)
        for t in range(nt):
            m = act.mark(act.e.activation(x[:, t, :], x[:, t, :], ACT.Copy, scale=stat[:, 1, t:t + 1]))
        return m

    def gate_up(self, s, h, h_ready, ghi, glo):
        p, ins = self.p, self.ins
        pe, act, dve, pool = self.engines4
        conv = self.sb(s, "conv_wb", [P, 4, KF])
        lc = [self.load(conv[:, 0:3, :], ins["conv_w"]), self.load(conv[:, 3, :], ins["conv_b"])]
        c = self.sb(s, "conv_out", [P, 2, S])
        v = self.sb(s, "gelu_mid", [P, S])
        g = self.sb(s, "gated", [P, S])
        g_read = Last(p, "gated_read")
        c_read = [Last(p, f"conv_read{i}") for i in range(2)]
        n_tiles = FF // FT
        act.wait(lc)
        dve.wait(lc)
        pe.wait(h_ready)

        def tile(col, col_u, j, b0):
            w = self.w.push([(0, FT, ins["w_gate_up"][:, col]), (FT, FT, ins["w_gate_up"][:, col_u])])
            m = [self.cols_product(h, w, KD, b0 + i, (i % 2) * FT + (i // 2) * P, None) for i in range(4)]
            w.release(m[-1])
            for e in range(2):
                a_ps, u_ps = self.ps[:, b0 + 2 * e, :], self.ps[:, b0 + 2 * e + 1, :]
                je = j + e
                col1 = (lambda r: conv[:, r, bass.ds(je, 1)]) if not isinstance(je, int) else (lambda r: conv[:, r, je:je + 1])
                row = (lambda x: x[:, bass.ds(je, 1), :].rearrange("p a n -> p (a n)")) if not isinstance(je, int) else (lambda x: x[:, je, :])
                ce = c[:, e, :]
                act.wait(m[2 * e], c_read[e].get())
                a = act.mark(act.e.activation(ce, a_ps, ACT.Identity, bias=col1(3), scale=col1(2)))
                for r in (1, 0):
                    d = 2 - r
                    dve.wait(a, dve.last())
                    b = dve.mark(dve.e.scalar_tensor_tensor(ce[:, d:S], a_ps[:, 0:S - d], col1(r), ce[:, d:S], ALU.mult, ALU.add))
                act.wait(b, g_read.get())
                a = act.mark(act.e.activation(v[:, :], ce, ACT.Square, scale=GELU_A))
                dve.wait(a)
                b = dve.mark(dve.e.scalar_tensor_tensor(v[:, :], v[:, :], 1.0, ce, ALU.add, ALU.mult))
                act.wait(b)
                a = act.mark(act.e.activation(v[:, :], v[:, :], ACT.Tanh, scale=GELU_C))
                dve.wait(a)
                b = dve.mark(dve.e.scalar_tensor_tensor(ce, v[:, :], 1.0, ce, ALU.add, ALU.mult))
                dve.wait(b, m[2 * e + 1], g_read.get())
                b = dve.mark(dve.e.scalar_tensor_tensor(g[:, :], ce, 0.5, u_ps, ALU.mult, ALU.mult))
                self.bank[b0 + 2 * e].set(b)
                self.bank[b0 + 2 * e + 1].set(b)
                c_read[e].set(b)
                act.wait(b)
                a = act.mark(act.e.copy(row(ghi), g[:, :]))
                dve.wait(a)
                b = dve.mark(dve.e.tensor_tensor(row(glo), g[:, :], row(ghi), ALU.subtract))
                g_read.set(b)

        with p.loop("gate_up", n_tiles // 2) as i:
            for e in range(2):
                tile(bass.ds(i * (2 * FT) + e * FT, FT), bass.ds(i * (2 * FT) + (FF + e * FT), FT), i * 4 + 2 * e, 4 * e)
        for t in range(n_tiles // 2 * 2, n_tiles):
            tile(slice(t * FT, (t + 1) * FT), slice(FF + t * FT, FF + (t + 1) * FT), 2 * t, 0)

    def block_one_gate(self, x):
        p, ins = self.p, self.ins
        pe, act, dve, pool = self.engines4
        KP = PE_IN // P
        with ExitStack() as s:
            hi, lo = self.sb(s, "x5_hi", [P, KD, S], F32R), self.sb(s, "x5_lo", [P, KD, S], F32R)
            phi, plo = self.sb(s, "p_hi", [P, KP, S], F32R), self.sb(s, "p_lo", [P, KP, S], F32R)
            prow = self.sb(s, "p_rows", [P, TX, PE_IN])
            th = self.sb(s, "gate_tanh", [P, 2, 512])
            mod = self.modulation_buffers(s, 1)
            lx = self.x_ready
            p.sp.wait(dve.last(), act.last(), pe.last())
            lp = self.load(prow[:, :, :], ins["p"].rearrange("(t p) d -> p t d", p=P))
            r1 = self.to_columns(x, TX, KD, hi, lo, lx)
            r2 = self.to_columns(prow, TX, KP, phi, plo, lp)
            th_read = [Last(p, f"tanh_read{i}") for i in range(2)]
            with p.loop("ple", 2) as nh:
                w = self.w.push([(0, 512, ins["w_ple_gate"][:, bass.ds(nh * 512, 512)])])
                we = self.w.push([(0, 512, ins["w_ple"][:, bass.ds(nh * 512, 512)])], chunks=KP)
                mg = [self.rows_product((hi, lo), w, KD, t, t, 0, 512, [r1, r2]) for t in range(TX)]
                w.release(mg[-1])
                me = [self.rows_product((phi, plo), we, KP, t, 4 + t, 0, 512, None) for t in range(TX)]
                we.release(me[-1])
                for k in range(4):
                    self.modulation_step(mod, k % 2, nh * 4 + k)
                for t in range(TX):
                    tt = th[:, t % 2, :]
                    act.wait(mg[t], th_read[t % 2].get())
                    a = act.mark(act.e.activation(tt, self.ps[:, t, :], ACT.Tanh, scale=0.5))
                    self.bank[t].set(a)
                    dve.wait(a, me[t])
                    b = dve.mark(dve.e.scalar_tensor_tensor(tt, tt, 1.0, self.ps[:, 4 + t, :], ALU.add, ALU.mult))
                    self.bank[4 + t].set(b)
                    dve.wait(b)
                    xs = x[:, t, bass.ds(nh * 512, 512)]
                    b = dve.mark(dve.e.scalar_tensor_tensor(xs, tt, 0.5, xs, ALU.mult, ALU.add))
                    th_read[t % 2].set(b)
            self.x_stored = self.store(self.x_dram[:, :, :], x[:, :, :], dve.last())
            self.modulation_end(s, mod)
            dve.wait(self.x_stored)
            p.meet(*self.all_engines)

    def differential(self):
        p, ins = self.p, self.ins
        pe, act, dve, pool = self.engines4
        with ExitStack() as s:
            h = (self.sb(s, "h6_hi", [P, KD, TA * P], F32R), self.sb(s, "h6_lo", [P, KD, TA * P], F32R))
            rows = self.sb(s, "rows6", [P, TA, D])
            stat = self.stat
            tmp = self.sb(s, "shift_tmp", [P, 2, 384])
            p.sp.wait(self.x_stored)
            ctx_in = ins["ctx_2"].rearrange("(t p) d -> p t d", p=P)
            lx = [self.load(rows[:, 0:TX, :], self.x_dram[:, :, :]), self.load(rows[:, TX:TA, :], ctx_in)]
            m = self.rms_rows_in_place(rows, TA, stat, lx)
            mod = lambda layer: [(0, TX, self.mod[:, 2 * layer, 1, :], self.mod[:, 2 * layer, 0, :]),
                                 (TX, TC, self.mod[:, 2 * layer + 1, 1, :], self.mod[:, 2 * layer + 1, 0, :])]
            ready = self.to_columns(rows, TA, KD, h[0], h[1], m, gains=mod(0), tmp=tmp)
            p.meet(*self.all_engines)
            with ExitStack() as s2:
                self.differential_heads(s2, h, ready, rows)
                p.meet(*self.all_engines)
            with ExitStack() as s2:
                x, c = self.sb(s2, "x7", [P, TX, D]), self.sb(s2, "c7", [P, TC, D])
                gain = self.sb(s2, "post7", [P, 2, D])
                junk = self.sb(s2, "junk7", [P, D])
                p.sp.wait(dve.last(), act.last(), pe.last())
                lx = [self.load(x[:, :, :], self.x_dram[:, :, :]), self.load(c[:, :, :], ctx_in),
                      self.load(gain[:, 0, :], self.row(self.gate_dram[0, :])),
                      self.load(gain[:, 1, :], self.row(self.gate_dram[1, :]))]
                ready = self.to_columns(rows, TA, KD, h[0], h[1], dve.last())
                for nh in range(2):
                    w = self.w.push([(0, 512, ins["w_out_2"][0][:, nh * 512:(nh + 1) * 512])])
                    banks = [(TA * nh + t) % 8 for t in range(TA)]
                    done = [self.rows_product(h, w, KD, t, banks[t], 0, 512, ready) for t in range(TA)]
                    w.release(done[-1])
                    m = self.out_rows(done, rows, TA, nh, banks)
                gains = [gain[:, 0, :]] * TX + [gain[:, 1, :]] * TC
                xc = [x[:, t, :] for t in range(TX)] + [c[:, t, :] for t in range(TC)]
                dve.wait(lx)
                a = self.add_normed(xc, rows, gains, junk[:, :], m)
                self.x_stored = self.store(self.x_dram[:, :, :], x[:, :, :], a[-1])
                for t in range(TA):
                    act.wait(a[t])
                    m = act.mark(act.e.activation(rows[:, t, :], xc[t], ACT.Square, accum_out=stat[:, 0, t:t + 1]))
                r = self.rsqrt(stat[:, 1, 0:TA], stat[:, 0, 0:TA], TA, D, m)
                act.wait(r, m)
                for t in range(TA):
                    m = act.mark(act.e.activation(rows[:, t, :], xc[t], ACT.Copy, scale=stat[:, 1, t:t + 1]))
                ready = self.to_columns(rows, TA, KD, h[0], h[1], m, gains=mod(1), tmp=tmp)
                dve.wait(self.x_stored)
                p.meet(*self.all_engines)
            self.grouped(s, h, ready, rows, stat)
            p.meet(*self.all_engines)

    def rope(self, out, t2, x, cos, sin, half, ready):
        dve = self.p.dve
        n = x.shape[1]
        shape = [P, n, half]
        dve.wait(ready, dve.last())
        dve.mark(dve.e.tensor_tensor(out, x, cos.rearrange("p (o n) -> p o n", o=1).to_broadcast([P, n, 2 * half]), ALU.mult))
        a = sin.rearrange("p (o n) -> p o n", o=1)
        dve.mark(dve.e.tensor_tensor(t2[:, :, 0:half], x[:, :, half:2 * half], a[:, :, 0:half].to_broadcast(shape), ALU.mult))
        m = dve.mark(dve.e.tensor_tensor(t2[:, :, half:2 * half], x[:, :, 0:half], a[:, :, half:2 * half].to_broadcast(shape), ALU.mult))
        dve.wait(m)
        return dve.mark(dve.e.tensor_tensor(out, out, t2, ALU.add)), m

    def differential_heads(self, s, h, h_ready, orow):
        p, ins = self.p, self.ins
        pe, act, dve, pool = self.engines4
        sb = lambda n, sh, dt=F32: self.sb(s, n, sh, dt)
        w_in = ins["a_w_in_2"][0]
        T6 = TA * P
        cos, sin = sb("cos_a", [P, TX, HD]), sb("sin_a", [P, TX, HD])
        lamb = sb("lambda", [P, 4, HD])
        lam = sb("lam", [P, 4])
        lj = sb("lam_junk", [P, 2, HD])
        gsub = sb("subln", [P, P])
        qst, khh, klo = sb("q6", [P, 2, T6], F32R), sb("k6_hi", [P, 2, T6], F32R), sb("k6_lo", [HD, 2, T6], F32R)
        vhi, vlo = sb("v6_hi", [P, TA, P], F32R), sb("v6_lo", [P, TA, P], F32R)
        zg, ot = sb("z6", [P, TA, P]), sb("o6", [P, TA, P])
        rot, rot2 = sb("rot6", [P, 2, 4, HD]), sb("rot6b", [P, 4, HD])
        st = sb("st6", [P, 4, 8])
        ss = sb("ss6", [P, 2, 8])
        o1 = sb("o1_6", [P, P])
        oj = sb("oj_6", [P, P])
        pbuf = sb("p6", [P, 1, T6])
        pthi, ptlo = sb("pt6_hi", [P, 1, T6], F32R), sb("pt6_lo", [P, 1, T6], F32R)
        small = [self.load(cos[:, :, :], ins["cos_a"]), self.load(sin[:, :, :], ins["sin_a"]),
                 self.load(lamb[:, :, :].rearrange("p a n -> p (a n)"), self.row(ins["a_lambda_2"])),
                 self.load(gsub[:, :], self.row(ins["a_subln_g_2"]))]
        dve.wait(small)
        for j in range(2):
            m = dve.mark(dve.e.tensor_tensor_reduce(lj[:, j, :], lamb[:, 2 * j, :], lamb[:, 2 * j + 1, :], 1.0, 0.0,
                                                    ALU.mult, ALU.add, lam[:, j:j + 1]))
        act.wait(m)
        a = act.mark(act.e.activation(lam[:, 2:4], lam[:, 0:2], ACT.Exp))
        dve.wait(a)
        lam_ready = dve.mark(dve.e.tensor_scalar(lam[:, 0:1], lam[:, 3:4], LAM_INIT, lam[:, 2:3], ALU.subtract, ALU.subtract))
        gsub_ready = dve.mark(dve.e.tensor_scalar(gsub[:, :], gsub[:, :], 0.5 * (1.0 - LAM_INIT), None, ALU.mult))
        self.S0, self.T0, self.O0 = 0, 2, 4
        GB, TB = 5, 7

        def head(hd):
            w = self.w.push([(P * j, P, w_in[:, bass.ds(hd * P + j * D, P)]) for j in range(4)])
            for t in range(TA):
                b = GB + t % 2
                m = self.rows_product(h, w, KD, t, b, 0, 512, h_ready)
                x = self.ps[:, b, 0:256].rearrange("p (v n) -> p v n", v=4)
                r = rot[:, t % 2, :, :]
                z = self.ps[:, b, 384:512]
                act.wait(m)
                c = act.mark(act.e.activation(zg[:, t, :], z, ACT.Tanh, scale=0.5))
                if t >= TX:
                    act.wait(pe.last())
                    a = act.mark(act.e.copy(r, x))
                va, vl = split(p, vhi[:, t, :], vlo[:, t, :], self.ps[:, b, 256:384], m, None)
                if t < TX:
                    a, _ = self.rope(r, rot2[:, :, :], x, cos[:, t, :], sin[:, t, :], HD // 2, [va, pe.last()])
                dve.wait(c)
                d = dve.mark(dve.e.scalar_tensor_tensor(zg[:, t, :], zg[:, t, :], 1.0, z, ALU.add, ALU.mult))
                self.bank[b].set(a, va, vl, d)
                e = t % 2
                pe.wait(a, self.bank[TB].get() if e == 0 else None)
                for j in range(2):
                    m2 = pe.e.transpose(self.ps[:, TB, j * 256 + e * P:j * 256 + (e + 1) * P],
                                        rot[:, e, 2 * j:2 * j + 2, :].rearrange("p a n -> p (a n)"), self.ident[:, :])
                m2 = pe.mark(m2)
                if e == 1:
                    c0, c1 = (t - 1) * P, (t + 1) * P
                    for sub in range(2):
                        q = self.ps[sub * HD:(sub + 1) * HD, TB, 0:256]
                        k = self.ps[sub * HD:(sub + 1) * HD, TB, 256:512]
                        _, b1 = split(p, qst[0:HD, sub, c0:c1], qst[HD:P, sub, c0:c1], q, m2, None, scale=-(HD ** -0.5))
                        split(p, khh[0:HD, sub, c0:c1], klo[:, sub, c0:c1], k, m2, b1, twin=khh[HD:P, sub, c0:c1])
                    self.bank[TB].set(act.last(), dve.last())
            w.release(m)
            pool.wait(d, gsub_ready)
            zm = pool.mark(pool.e.tensor_tensor(zg[:, :, :], zg[:, :, :],
                                                gsub[:, :].rearrange("p (o n) -> p o n", o=1).to_broadcast([P, TA, P]), ALU.mult))
            p.meet(pe, act, dve)

            def post(t, sub):
                def f(o, s_):
                    a = dve.mark(dve.e.reciprocal(s_[:, 3:4], s_[:, 1:2]))
                    dve.wait(a, lam_ready)
                    if sub == 0:
                        return dve.mark(dve.e.tensor_scalar(o1[:, :], o, s_[:, 3:4], None, ALU.mult))
                    a = dve.mark(dve.e.tensor_tensor(s_[:, 4:5], s_[:, 3:4], lam[:, 0:1], ALU.mult))
                    dve.wait(a)
                    a = dve.mark(dve.e.scalar_tensor_tensor(ot[:, t, :], o, s_[:, 4:5], o1[:, :], ALU.mult, ALU.add))
                    dve.wait(a)
                    dve.mark(dve.e.tensor_tensor_reduce(oj[:, :], ot[:, t, :], ot[:, t, :], 1.0, 0.0, ALU.mult, ALU.add,
                                                        ss[:, 0, t:t + 1]))
                    return a
                return f

            units = []
            for t in range(TA):
                for sub in range(2):
                    q0 = t * P
                    units.append(dict(
                        qk=[(qst[:, sub, q0:q0 + P], lambda a, b, sub=sub: khh[:, sub, a:b]),
                            (qst[0:HD, sub, q0:q0 + P], lambda a, b, sub=sub: klo[:, sub, a:b])],
                        k0=0 if t < TX else S, w=T6 if t < TX else C, bias=None, vw=P,
                        v=lambda k: (vhi[:, k, :], vlo[:, k, :]), post=post(t, sub)))
            self.attention(units, st, pbuf, pthi, ptlo, 1)
            r = self.rsqrt(ss[:, 1, 0:TA], ss[:, 0, 0:TA], TA, P, dve.last())
            dve.wait(r, zm)
            for t in range(TA):
                m = dve.mark(dve.e.scalar_tensor_tensor(orow[:, t, bass.ds(hd * P, P)], ot[:, t, :], ss[:, 1, t:t + 1],
                                                        zg[:, t, :], ALU.mult, ALU.mult))
            p.meet(pe, act, dve)

        with p.loop("diff_heads", 4) as i:
            for e in range(2):
                head(i * 2 + e)

    def grouped(self, s, h, h_ready, orow, stat):
        p, ins = self.p, self.ins
        pe, act, dve, pool = self.engines4
        w_in = ins["b_w_in_2"][0]
        T6 = TA * P
        with ExitStack() as s2:
            sb = lambda n, sh, dt=F32: self.sb(s2, n, sh, dt)
            cos, sin = sb("cos_b", [P, TX, GD]), sb("sin_b", [P, TX, GD])
            gq, gk = sb("gq", [P, GD]), sb("gk", [P, GD])
            khi, klo = sb("k8_hi", [P, 2, T6], F32R), sb("k8_lo", [P, 2, T6], F32R)
            vhi, vlo = sb("v8_hi", [P, TA, 256], F32R), sb("v8_lo", [P, TA, 256], F32R)
            qhi, qlo = sb("q8_hi", [P, 2, S], F32R), sb("q8_lo", [P, 2, S], F32R)
            zg = sb("z8", [P, TX, 256])
            nrm, rot, rot2 = sb("nrm8", [P, 2, GD]), sb("rot8", [P, 2, 2, GD]), sb("rot8b", [P, 2, GD])
            st = sb("st8", [P, 4, 8])
            ss = sb("ss8", [P, 2, 16])
            junk = sb("junk8", [P, GD])
            mh = sb("minus_half16", [P, 16])
            pbuf = sb("p8", [P, 1, T6])
            pthi, ptlo = sb("pt8_hi", [P, 1, T6], F32R), sb("pt8_lo", [P, 1, T6], F32R)
            mh_ready = pool.mark(pool.e.memset(mh[:, :], -0.5))
            small = [self.load(cos[:, :, :], ins["cos_b"]), self.load(sin[:, :, :], ins["sin_b"]),
                     self.load(gq[:, :], self.row(ins["b_qk_g_2"][0:GD])),
                     self.load(gk[:, :], self.row(ins["b_qk_g_2"][GD:2 * GD]))]
            dve.wait(small)
            g_ready = dve.mark(dve.e.tensor_scalar(gq[:, :], gq[:, :], -(GD ** -0.5), None, ALU.mult))
            self.S0, self.T0, self.O0 = 0, 2, 4

            def normed(done, banks, gain, hi, lo, tb, nt, beside):
                for t in range(nt):
                    act.wait(done[t])
                    for e in range(2):
                        act.wait(act.last())
                        m = act.mark(act.e.activation(junk[:, :], self.ps[:, banks[t], e * GD:(e + 1) * GD], ACT.Square,
                                                      accum_out=ss[:, 0, 2 * t + e:2 * t + e + 1]))
                    m = beside(t)
                dve.wait(m)
                a = dve.mark(dve.e.tensor_scalar(ss[:, 0, 0:2 * nt], ss[:, 0, 0:2 * nt], 1.0 / GD, EPS, ALU.mult, ALU.add))
                pool.wait(a, mh_ready)
                r = pool.mark(pool.e.tensor_tensor(ss[:, 1, 0:2 * nt], ss[:, 0, 0:2 * nt], mh[:, 0:2 * nt], ALU.pow))
                out = []
                for t in range(nt):
                    dve.wait(r, dve.last(), pe.last(), g_ready)
                    x = rot[:, t % 2, :, :]
                    dst = nrm if t < TX else x
                    for e in range(2):
                        m = dve.mark(dve.e.scalar_tensor_tensor(dst[:, e, :], self.ps[:, banks[t], e * GD:(e + 1) * GD],
                                                                ss[:, 1, 2 * t + e:2 * t + e + 1], gain[:, :], ALU.mult, ALU.mult))
                    if t < TX:
                        m, _ = self.rope(x, rot2[:, :, :], nrm[:, :, :], cos[:, t, :], sin[:, t, :], GD // 2, m)
                    pe.wait(m, self.bank[tb].get())
                    for e in range(2):
                        m2 = pe.e.transpose(self.ps[:, tb, e * P:(e + 1) * P], rot[:, t % 2, e, :], self.ident[:, :])
                    m2 = pe.mark(m2)
                    src = self.ps[:, tb, 0:256].rearrange("p (a n) -> p a n", a=2)
                    a, b = split(p, hi[:, :, t * P:(t + 1) * P], lo[:, :, t * P:(t + 1) * P], src, m2, None)
                    self.bank[tb].set(a, b)
                return b

            w = self.w.push([(0, 512, w_in[:, D:D + 512])])
            banks = list(range(TA))
            done = [self.rows_product(h, w, KD, t, banks[t], 0, 512, h_ready) for t in range(TA)]
            w.release(done[-1])
            normed(done, banks, gk, khi, klo, 7, TA,
                   lambda t: act.mark(act.e.copy(vhi[:, t, :], self.ps[:, banks[t], 256:512])))
            for t in range(TA):
                self.bank[banks[t]].set(dve.mark(dve.e.tensor_tensor(vlo[:, t, :], self.ps[:, banks[t], 256:512],
                                                                     vhi[:, t, :], ALU.subtract)))
            p.meet(pe, act, dve)

            with p.loop("gqa_groups", 2) as g:
                for pair in range(2):
                    col = g * 512 + pair * 256
                    w = self.w.push([(0, 256, w_in[:, bass.ds(col, 256)]), (256, 256, w_in[:, bass.ds(col + (D + 512), 256)])])
                    banks = [3, 4, 5, 6]
                    done = [self.rows_product(h, w, KD, t, banks[t], 0, 512, None) for t in range(TX)]
                    w.release(done[-1])
                    normed(done, banks, gq, qhi, qlo, 7, TX,
                           lambda t: act.mark(act.e.activation(zg[:, t, :], self.ps[:, banks[t], 256:512], ACT.Tanh, scale=0.5)))
                    for t in range(TX):
                        z = self.ps[:, banks[t], 256:512]
                        b = dve.mark(dve.e.scalar_tensor_tensor(zg[:, t, :], zg[:, t, :], 1.0, z, ALU.add, ALU.mult))
                        self.bank[banks[t]].set(b)
                    p.meet(pe, act, dve)

                    def post(t, e):
                        def f(o, s_):
                            a = dve.mark(dve.e.tensor_scalar(s_[:, 3:4], s_[:, 1:2], 2.0, None, ALU.mult))
                            dve.wait(a)
                            a = dve.mark(dve.e.reciprocal(s_[:, 4:5], s_[:, 3:4]))
                            dve.wait(a)
                            dst = orow[:, t, bass.ds(col + e * GD, GD)]
                            return dve.mark(dve.e.scalar_tensor_tensor(dst, o, s_[:, 4:5], zg[:, t, e * GD:(e + 1) * GD],
                                                                       ALU.mult, ALU.mult))
                        return f

                    units = []
                    for e in range(2):
                        for t in range(TX):
                            q = [x[:, e, t * P:(t + 1) * P] for x in (qhi, qlo)]
                            kk = [(lambda a, b, x=x: x[:, bass.ds(g, 1), a:b].rearrange("p o n -> p (o n)")) for x in (khi, klo)]
                            units.append(dict(qk=[(q[0], kk[0]), (q[0], kk[1]), (q[1], kk[0])], k0=0, w=T6, bias=None, vw=P,
                                              v=lambda k: (vhi[:, k, bass.ds(g * GD, GD)], vlo[:, k, bass.ds(g * GD, GD)]),
                                              post=post(t, e)))
                    self.attention(units, st, pbuf, pthi, ptlo, 1)
                    p.meet(pe, act, dve)
            p.meet(*self.all_engines)

        with ExitStack() as s2:
            x = self.sb(s2, "x9", [P, TX, D])
            gain = self.sb(s2, "post9", [P, D])
            junk = self.sb(s2, "junk9", [P, D])
            p.sp.wait(dve.last(), act.last(), pe.last())
            lx = [self.load(x[:, :, :], self.x_dram[:, :, :]), self.load(gain[:, :], self.row(self.gate_dram[2, :]))]
            ready = self.to_columns(orow, TX, KD, h[0], h[1], dve.last())
            for nh in range(2):
                w = self.w.push([(0, 512, ins["w_out_2"][1][:, nh * 512:(nh + 1) * 512])])
                banks = [4 * nh + t for t in range(TX)]
                done = [self.rows_product(h, w, KD, t, banks[t], 0, 512, ready) for t in range(TX)]
                w.release(done[-1])
                m = self.out_rows(done, orow, TX, nh, banks)
            dve.wait(lx)
            a = self.add_normed([x[:, t, :] for t in range(TX)], orow, [gain[:, :]] * TX, junk[:, :], m)
            out = self.outs["out"].rearrange("(t p) d -> p t d", p=P)
            for t in range(TX):
                self.store(out[:, t, :], x[:, t, :], a[t])


def constants():
    c = {"ident": np.eye(P, dtype=np.float32)}
    slopes = np.exp2(-8.0 * (np.arange(16, dtype=np.float32) + 1.0) / 16).astype(np.float32)
    pr = np.arange(P)[:, None]
    alibi = np.zeros((GROUPS, P, PER_G, NSA_BIAS_W + SWA_BIAS_W), np.float32)
    dist = pr + (S - P) - np.arange(S)[None, :]
    n = np.arange(CMP_W)
    dist_c = (np.arange(TX)[None, :, None] * P + np.arange(P)[:, None, None]) - (n * CMP_ST + CMP_L - 1)[None, None, :]
    ok_c = (dist_c >= 0) & (n < NCMP)
    dist_s = P + pr - np.arange(SWA_BIAS_W)[None, :]
    for g in range(GROUPS):
        for e in range(PER_G):
            nsa, swa = slopes[8 + g * PER_G + e], slopes[g * PER_G + e]
            alibi[g, :, e, 0:S] = np.where(dist >= 0, nsa * dist, BIG)
            alibi[g, :, e, S:NSA_BIAS_W] = np.where(ok_c, nsa * dist_c, BIG).reshape(P, TX * CMP_W)
            alibi[g, :, e, NSA_BIAS_W:] = np.where((dist_s >= 0) & (dist_s < P), swa * dist_s, BIG)
    c["alibi"] = alibi
    c["cmp_valid"] = ok_c.astype(np.float32)
    for name, hd in (("a", HD), ("b", GD)):
        axis = hd // 2
        freqs = (10000.0 ** (-np.arange(0, axis, 2, dtype=np.float32) / axis)).astype(np.float32)
        tok = np.arange(S)
        ang = np.concatenate([(tok // 64).astype(np.float32)[:, None] * freqs,
                              (tok % 64).astype(np.float32)[:, None] * freqs], axis=-1).astype(np.float32)
        cos, sin = np.cos(ang), np.sin(ang)
        for nm, v in (("cos", np.concatenate([cos, cos], -1)), ("sin", np.concatenate([-sin, sin], -1))):
            c[f"{nm}_{name}"] = np.ascontiguousarray(v.reshape(TX, P, hd).transpose(1, 0, 2).astype(np.float32))
    return c


def lay_out(a):
    by_feature = lambda v, *lead: np.ascontiguousarray(np.moveaxis(np.reshape(v, (*lead, -1, P)), -1, 0))
    o = {
        "x": a["x"][0], "p": a["p"][0, 0], "w_in": a["w_in"][0],
        "attn_pre_g": by_feature(a["attn_pre_g"][0]), "mlp_pre_g": by_feature(a["mlp_pre_g"][0]),
        "pre_g_2": by_feature(a["pre_g_2"], 2),
        "cmp_w1_k": a["cmp_w1_k"][0], "cmp_w2_k": a["cmp_w2_k"][0],
        "cmp_w1_v": a["cmp_w1_v"][0], "cmp_w2_v": a["cmp_w2_v"][0],
        "cmp_pe_k": by_feature(a["cmp_pe_k"][0]), "cmp_pe_v": by_feature(a["cmp_pe_v"][0]),
        "sinks": a["sinks"][0], "w_o": a["w_o"][0], "attn_post_g": a["attn_post_g"][0],
        "w_gate_up": a["w_gate_up"][0], "conv_w": by_feature(a["conv_w"][0], 3), "conv_b": by_feature(a["conv_b"][0]),
        "w_down": a["w_down"][0], "mlp_post_g": a["mlp_post_g"][0],
        "w_ple": a["w_ple"][0], "w_ple_gate": a["w_ple_gate"][0],
        "c_2": by_feature(a["c_2"][0]), "c_ctx_2": by_feature(a["c_ctx_2"]), "ctx_2": a["ctx_2"][0],
        "ada_w_2": a["ada_w_2"], "ada_b_2": a["ada_b_2"], "ada_b_cols": by_feature(a["ada_b_2"][:, 0:2 * D], 2),
        "post_g_2": a["post_g_2"], "w_out_2": a["w_out_2"], "a_w_in_2": a["a_w_in_2"], "b_w_in_2": a["b_w_in_2"],
        "a_lambda_2": np.reshape(a["a_lambda_2"][0], -1), "a_subln_g_2": a["a_subln_g_2"][0],
        "b_qk_g_2": np.reshape(a["b_qk_g_2"][0], -1),
    }
    o.update(constants())
    return {k: np.ascontiguousarray(v) for k, v in o.items()}


def program(nc, arrays, counts):
    ins = {n: nc.dram_tensor("in_" + n, a.shape, mybir.dt.from_np(a.dtype), kind="ExternalInput").ap()
           for n, a in arrays.items()}
    outs = {"out": nc.dram_tensor("out_0", (S, D), F32, kind="ExternalOutput").ap()}
    Kernel(nc, ins, outs, counts)


def kernel(**inputs):
    import numpy as _np
    import concourse.bacc as _bacc
    from concourse.bass_utils import run_bass_kernel_spmd as _run

    arrays = lay_out({k: _np.asarray(v) for k, v in inputs.items()})
    counts = {}
    for _ in range(2):
        nc = _bacc.Bacc("TRN2", target_bir_lowering=False, num_devices=1)
        program(nc, arrays, counts)
    r = _run(nc, [{"in_" + n: a for n, a in arrays.items()}], core_ids=[0])
    return _np.reshape(r.results[0]["out_0"], (1, S, D))
```

```python
import math
from contextlib import ExitStack, contextmanager

import numpy as np
import concourse.bass as bass
from concourse import mybir

F32 = mybir.dt.float32
F32R = mybir.dt.float32r
I32 = mybir.dt.int32
ALU = mybir.AluOpType
ACT = mybir.ActivationFunctionType
AX = mybir.AxisListType

P = 128
S = 512
C = 256
D = 1024
KD = D // P
TX, TC = S // P, C // P
TA = TX + TC
HD = 64
GD = 128
GROUPS, PER_G = 2, 4
NCMP, CMP_W = 31, 32
CMP_L, CMP_ST = 32, 16
PE_IN = 256
FF = 2816
KF = FF // P
FT = 256
EPS = 1e-6
BIG = 1e30
HEAD = 1000
LAM_INIT = 0.8 - 0.6 * math.exp(-0.3 * 0)
GELU_C = math.sqrt(2.0 / math.pi)
GELU_A = math.sqrt(0.044715)
NSA_BIAS_W = S + TX * CMP_W
SWA_BIAS_W = 2 * P


class Mark:

    def __init__(self, sem, const, coeff=0, loop=None):
        self.sem, self.const, self.coeff, self.loop = sem, const, coeff, loop

    def value(self):
        if self.loop is None or self.coeff == 0:
            return self.const
        if self.loop.active:
            return self.loop.i * self.coeff + self.const
        return self.const + self.coeff * (self.loop.n - 1)


class Counter:

    def __init__(self, prog, name, start=0):
        self.h = prog.ctx.enter_context(prog.nc.semaphore(name))
        self.name, self.const, self.coeff, self.loop = name, start, 0, None
        prog.counters.append(self)

    def inc(self, instr, by=1):
        instr.then_inc(self.h, by)
        self.const += by
        return Mark(self, self.const, self.coeff, self.loop)


class Engine:

    def __init__(self, prog, e, name, compute=True):
        self.e, self.seen = e, {}
        self.settled = prog.ctx.enter_context(prog.nc.semaphore(name + "_settled"))
        self.done = Counter(prog, name + "_done", HEAD) if compute else None
        if compute:
            e.sem_inc(self.done.h, HEAD)
        prog.engines.append(self)

    def wait(self, *marks):
        for m in marks:
            if m is None:
                continue
            if isinstance(m, (list, tuple)):
                self.wait(*m)
                continue
            fixed = m.loop is None or m.coeff == 0 or not m.loop.active
            key = (m.sem.name, fixed)
            const = m.value() if fixed else m.const
            if self.seen.get(key, -1) >= const:
                continue
            self.seen[key] = const
            self.e.wait_ge(m.sem.h, m.value())

    def mark(self, instr):
        return self.done.inc(instr)

    def settle(self):
        self.e.sem_inc(self.settled, 1)

    def last(self):
        return Mark(self.done, self.done.const, self.done.coeff, self.done.loop)


class Last:

    def __init__(self, prog, name):
        self.prog, self.name, self.marks, self.fresh = prog, name, [], False
        prog.lasts.append(self)

    def set(self, *marks):
        self.marks, self.fresh = [m for m in marks if m is not None], True

    def get(self):
        loop = self.prog.loop_now
        if loop is None or self.fresh:
            return list(self.marks)
        before = []
        for cname, off in self.prog.counts.get((loop.name, self.name), []):
            c = self.prog.by_name(cname)
            before.append(Mark(c, loop.base[cname] + off - c.coeff, c.coeff, loop))
        return list(self.marks) + before


class Loop:
    def __init__(self, name, n):
        self.name, self.n, self.active, self.i, self.base = name, n, True, None, {}


class Prog:

    def __init__(self, nc, ctx, counts):
        self.nc, self.ctx, self.counts = nc, ctx, counts
        self.counters, self.engines, self.lasts, self.loop_now = [], [], [], None
        self.pe = Engine(self, nc.tensor, "pe")
        self.act = Engine(self, nc.scalar, "act")
        self.dve = Engine(self, nc.vector, "dve")
        self.pool = Engine(self, nc.gpsimd, "pool")
        self.sp = Engine(self, nc.sync, "sp", compute=False)

    def by_name(self, name):
        return [c for c in self.counters if c.name == name][0]

    def meet(self):
        engines = (self.pe, self.act, self.dve)
        for a in engines:
            a.wait(*[b.last() for b in engines])

    @contextmanager
    def loop(self, name, n):
        loop = Loop(name, n)
        start = {c.name: c.const for c in self.counters}
        loop.base = start
        with self.nc.Fori(0, n) as i:
            loop.i = i
            for c in self.counters:
                c.coeff, c.loop = self.counts.get((name, c.name), 0), loop
            for e in self.engines:
                e.seen = {}
            for x in self.lasts:
                x.fresh = False
            self.loop_now = loop
            yield i
        for c in self.counters:
            self.counts[(name, c.name)] = c.const - start[c.name]
            c.const = start[c.name] + n * (c.const - start[c.name])
            c.coeff, c.loop = 0, None
        for x in self.lasts:
            if x.fresh:
                self.counts[(name, x.name)] = [(m.sem.name, m.const - start[m.sem.name]) for m in x.marks if m.loop is loop]
        for e in self.engines:
            e.seen = {}
        loop.active = False
        self.loop_now = None


class Weights:

    def __init__(self, prog):
        self.p = prog
        c, nc = prog.ctx, prog.nc
        self.raw = c.enter_context(nc.sbuf_tensor("w_raw", [P, 2, 2, 512], F32))
        self.hi = c.enter_context(nc.sbuf_tensor("w_hi", [P, 2, KD, 512], F32R))
        self.lo = c.enter_context(nc.sbuf_tensor("w_lo", [P, 2, KD, 512], F32R))
        self.loaded = [Counter(prog, f"w_loaded{s}") for s in range(2)]
        self.raw_read = [Last(prog, f"w_raw_read{s}") for s in range(2)]
        self.tile_read = [Last(prog, f"w_tile_read{s}") for s in range(2)]
        self.ready = [[Last(prog, f"w_ready{s}_{q}") for q in range(KD // 2)] for s in range(2)]
        self.turn = 0

    def push(self, sources, row0=0, chunks=KD):
        p, slot = self.p, self.turn
        self.turn = 1 - self.turn
        width = max(c0 + n for c0, n, _ in sources)
        for q in range(0, chunks, 2):
            r = (q // 2) % 2
            p.sp.wait(self.raw_read[r].get())
            for c0, n, src in sources:
                rows = src[row0 + q * P:row0 + (q + 2) * P, :].rearrange("(c p) n -> p c n", p=P)
                loaded = self.loaded[r].inc(p.sp.e.dma_start(self.raw[:, r, :, c0:c0 + n], rows), 16)
            raw = self.raw[:, r, :, 0:width]
            hi, lo = self.hi[:, slot, q:q + 2, 0:width], self.lo[:, slot, q:q + 2, 0:width]
            p.pool.wait(loaded, self.tile_read[slot].get())
            p.pool.settle()
            a = p.pool.mark(p.pool.e.tensor_scalar(hi, raw, 1.0, 0.0, ALU.mult, ALU.add))
            p.pool.wait(a)
            b = p.pool.mark(p.pool.e.tensor_tensor(lo, raw, hi, ALU.subtract))
            self.raw_read[r].set(b)
            self.ready[slot][q // 2].set(b)
        return Tile(self, slot)


class Tile:

    def __init__(self, w, slot):
        self.w, self.slot = w, slot

    def ready(self, k):
        return self.w.ready[self.slot][k // 2].get()

    def hl(self, k, c0, n):
        return self.w.hi[:, self.slot, k, c0:c0 + n], self.w.lo[:, self.slot, k, c0:c0 + n]

    def release(self, mark):
        self.w.tile_read[self.slot].set(mark)


def three(e, out, a, b, start, stop):
    e.matmul(out, a[0], b[0], start=start, stop=False)
    e.matmul(out, a[0], b[1], start=False, stop=False)
    return e.matmul(out, a[1], b[0], start=False, stop=stop)


def split(prog, hi, lo, ps, ready, free, scale=None, gain=None, shift=None, tmp=None, tmp_free=None, twin=None):
    act, dve = prog.act, prog.dve
    act.wait(ready, free)
    if shift is not None:
        a = act.mark(act.e.activation(hi, ps, ACT.Identity, bias=shift, scale=gain))
    else:
        k = gain if gain is not None else (1.0 if scale is None else scale)
        a = act.mark(act.e.activation(hi, ps, ACT.Copy, scale=k))
    if twin is not None:
        a = act.mark(act.e.copy(twin, ps))
    dve.wait(ready, free, a)
    if shift is not None:
        dve.wait(tmp_free)
        t = dve.mark(dve.e.tensor_scalar(tmp, ps, gain, shift, ALU.mult, ALU.add))
        dve.wait(t, a)
        b = dve.mark(dve.e.tensor_tensor(lo, tmp, hi, ALU.subtract))
    elif gain is not None or scale is not None:
        dve.wait(a)
        b = dve.mark(dve.e.scalar_tensor_tensor(lo, ps, gain if gain is not None else scale, hi, ALU.mult, ALU.subtract))
    else:
        dve.wait(a)
        b = dve.mark(dve.e.tensor_tensor(lo, ps, hi, ALU.subtract))
    return a, b


class Kernel:
    def __init__(self, nc, ins, outs, counts):
        self.nc, self.ins, self.outs = nc, ins, outs
        self.ctx = ExitStack()
        with self.ctx:
            self.p = Prog(nc, self.ctx, counts)
            self.build()

    def sb(self, ctx, name, shape, dt=F32, side="left"):
        return ctx.enter_context(self.nc.sbuf_tensor(name, shape, dt, side=side))

    def load(self, out, src, sem=None):
        self.n_loads += 1
        c = sem or Counter(self.p, f"load{self.n_loads}")
        return c.inc(self.p.act.e.dma_start(out, src), 16)

    def store(self, out, src, after):
        self.n_loads += 1
        c = Counter(self.p, f"store{self.n_loads}")
        self.p.act.wait(after)
        m = c.inc(self.p.act.e.dma_start(out, src), 16)
        self.stores.append(m)
        return m

    def row(self, v):
        return v.rearrange("(a n) -> a n", a=1).partition_broadcast(P)

    def rsqrt(self, out, ssq, count, ready):
        dve, n = self.p.dve, out.shape[-1]
        t = self.newton[:, 0:n]

        def step(instr):
            m = dve.mark(instr)
            dve.wait(m)
            return m

        dve.wait(ready, dve.last())
        step(dve.e.tensor_scalar(ssq, ssq, 1.0 / count, EPS, ALU.mult, ALU.add))
        step(dve.e.tensor_scalar(t.bitcast(I32), ssq.bitcast(I32), 1, None, ALU.logical_shift_right))
        step(dve.e.tensor_scalar(out.bitcast(I32), t.bitcast(I32), -1, 0x5F3759DF, ALU.mult, ALU.add))
        for _ in range(3):
            step(dve.e.scalar_tensor_tensor(t, out, -0.5, out, ALU.mult, ALU.mult))
            step(dve.e.tensor_tensor(t, t, ssq, ALU.mult))
            m = step(dve.e.scalar_tensor_tensor(out, t, 1.5, out, ALU.add, ALU.mult))
        return m

    def to_columns(self, rows, nt, chunks, hi, lo, ready, gains=None, shifts=None, tmp=None):
        p, w = self.p, nt * P
        banks = 2 if w > 512 else 1
        half = w // banks
        parts = gains or [(0, nt, None, None)]
        marks = []
        for k in range(chunks):
            b0 = 2 * (k % 4)
            ps = self.ps[:, b0:b0 + banks, 0:half]
            p.pe.wait(ready, self.bank[b0].get(), self.const_ready)
            for t in range(nt):
                c = t * P
                m = p.pe.e.transpose(self.ps[:, b0 + c // half, c % half:c % half + P],
                                     rows[:, t, k * P:(k + 1) * P], self.ident[:, :])
            m = p.pe.mark(m)
            ends = []
            for t0, n, gain, shift in parts:
                for c0 in range(t0 * P, (t0 + n) * P, half):
                    c1 = min((t0 + n) * P, (c0 // half + 1) * half)
                    self.split_part(c0, c1, b0, half, k, hi, lo, m, gain, shift, tmp, ends)
            self.bank[b0].set(*ends[-1])
            marks.append(ends[-1])
        return marks[-1]

    def split_part(self, c0, c1, b0, half, k, hi, lo, m, gain, shift, tmp, ends):
        src = self.ps[:, b0 + c0 // half, c0 % half:c0 % half + c1 - c0]
        i = len(ends) % 2
        t = tmp[:, i, 0:c1 - c0] if tmp is not None else None
        ends.append(split(self.p, hi[:, k, c0:c1], lo[:, k, c0:c1], src, m, ends[-1] if ends else None,
                          gain=None if gain is None else gain[:, k:k + 1],
                          shift=None if shift is None else shift[:, k:k + 1],
                          tmp=t, tmp_free=self.p.dve.last()))

    def rms_rows(self, x, xn, nt, stat, ready):
        p = self.p
        for t in range(nt):
            p.act.wait(ready[t] if isinstance(ready, list) else ready)
            m = p.act.mark(p.act.e.activation(xn[:, t, :], x[:, t, :], ACT.Square, accum_out=stat[:, 0, t:t + 1]))
        r = self.rsqrt(stat[:, 1, 0:nt], stat[:, 0, 0:nt], D, m)
        p.act.wait(r, m)
        for t in range(nt):
            m = p.act.mark(p.act.e.activation(xn[:, t, :], x[:, t, :], ACT.Copy, scale=stat[:, 1, t:t + 1]))
        return m

    def out_rows(self, jobs_ready, y, nt, nh, banks):
        p = self.p
        for t in range(nt):
            p.act.wait(jobs_ready[t])
            m = p.act.mark(p.act.e.copy(y[:, t, nh * 512:(nh + 1) * 512], self.ps[:, banks[t], :]))
            self.bank[banks[t]].set(m)
        return m

    def add_normed(self, x, y, gains, junk, ready):
        p, nt, stat = self.p, len(x), self.stat
        for t in range(nt):
            p.act.wait(ready, p.act.last())
            m = p.act.mark(p.act.e.activation(junk, y[:, t, :], ACT.Square, accum_out=stat[:, 0, t:t + 1]))
        r = self.rsqrt(stat[:, 1, 0:nt], stat[:, 0, 0:nt], D, m)
        out = []
        for t in range(nt):
            p.dve.wait(r)
            a = p.dve.mark(p.dve.e.scalar_tensor_tensor(y[:, t, :], y[:, t, :], stat[:, 1, t:t + 1], gains[t],
                                                        ALU.mult, ALU.mult))
            p.dve.wait(a)
            out.append(p.dve.mark(p.dve.e.tensor_tensor(x[t], x[t], y[:, t, :], ALU.add)))
        return out

    def rows_product(self, cols, tile, chunks, t, bank, c0, n, ready, out_c0=0, start=True, stop=True, k0=0, fresh=True):
        p = self.p
        p.pe.wait(ready, self.bank[bank].get() if start and fresh else None)
        for k in range(chunks):
            p.pe.wait(tile.ready(k))
            m = three(p.pe.e, self.ps[:, bank, out_c0:out_c0 + n],
                      (cols[0][:, k0 + k, t * P:(t + 1) * P], cols[1][:, k0 + k, t * P:(t + 1) * P]),
                      tile.hl(k, c0, n), start and k == 0, stop and k == chunks - 1)
        return p.pe.mark(m)

    def cols_product(self, cols, tile, chunks, bank, c0, ready, n=S):
        p = self.p
        p.pe.wait(ready, self.bank[bank].get())
        for k in range(chunks):
            p.pe.wait(tile.ready(k))
            m = three(p.pe.e, self.ps[:, bank, 0:n], tile.hl(k, c0, P),
                      (cols[0][:, k, 0:n], cols[1][:, k, 0:n]), k == 0, k == chunks - 1)
        return p.pe.mark(m)

    def attention(self, units, st, pbuf, ptbuf, wide, filler=None):
        p = self.p
        pe, act, dve = p.pe, p.act, p.dve
        S0, T0, O0 = 0, 2, 4
        n_p, n_pt = pbuf.shape[1], ptbuf.shape[1]
        scored, weights, turned, valued, posted = {}, {}, {}, {}, {}

        def banks(b0, n, w):
            return ([b0, b0 + 1], w // 2) if w > 512 else ([b0 if wide else b0 + n % 2], w)

        def view(bs, rows, cols):
            return self.ps[0:rows, bs[0]:bs[0] + 2, 0:cols] if len(bs) == 2 else self.ps[0:rows, bs[0], 0:cols]

        def folded(x, bs):
            return x.rearrange("p (a b) -> p a b", a=2) if len(bs) == 2 else x

        def scores(n):
            u = units[n]
            bs, cols = banks(S0, n, u["w"])
            for c, b in enumerate(bs):
                pe.wait(self.bank[b].get())
                for i, (q, k) in enumerate(u["qk"]):
                    m = pe.e.matmul(self.ps[:, b, 0:cols], q, k(u["k0"] + c * cols, u["k0"] + (c + 1) * cols),
                                    start=i == 0, stop=i == len(u["qk"]) - 1)
            scored[n] = pe.mark(m)

        def softmax(n):
            u = units[n]
            bs, cols = banks(S0, n, u["w"])
            sc, s, pr = view(bs, P, cols), st[:, n % 4, :], pbuf[:, n % n_p, 0:u["w"]]
            dve.wait(scored[n])
            if u["bias"] is not None:
                dve.wait(u.get("bias_ready"))
                dve.settle()
                a = dve.mark(dve.e.tensor_tensor_reduce(sc, sc, u["bias"], 1.0, u.get("init", 3e38), ALU.add, ALU.min,
                                                        s[:, 0:1]))
            else:
                a = dve.mark(dve.e.tensor_reduce(s[:, 0:1], sc, AX.XY if len(bs) == 2 else AX.X, ALU.min))
            act.wait(a)
            e = act.mark(act.e.activation(folded(pr, bs), sc, ACT.Exp, bias=s[:, 0:1], scale=-1.0, accum_out=s[:, 1:2]))
            for b in bs:
                self.bank[b].set(a, e)
            if u.get("sink") is not None:
                e = act.mark(act.e.activation(s[:, 2:3], s[:, 0:1], ACT.Exp, bias=u["sink"]))
            if u.get("valid") is not None:
                dve.wait(e)
                e = dve.mark(dve.e.tensor_tensor(pr, pr, u["valid"], ALU.mult))
            weights[n] = e

        def turn(n):
            u = units[n]
            nk, kw = -(-u["w"] // P), min(P, u["w"])
            bs, cols = banks(T0, n, nk * P)
            pe.wait(weights[n], [self.bank[b].get() for b in bs])
            for j in range(nk):
                c = j * P
                m = pe.e.transpose(self.ps[0:kw, bs[c // cols], c % cols:c % cols + P],
                                   pbuf[:, n % n_p, c:c + kw], self.ident[:, :])
            m = pe.mark(m)
            act.wait(m, valued.get(n - n_pt))
            turned[n] = act.mark(act.e.copy(folded(ptbuf[0:kw, n % n_pt, 0:nk * P], bs), view(bs, kw, cols)))
            for b in bs:
                self.bank[b].set(turned[n])

        def values(n):
            u = units[n]
            nk, kw, vw = -(-u["w"] // P), min(P, u["w"]), u["vw"]
            b = O0 if wide else O0 + n % 2
            o = self.ps[:, b, (n % 4) * P:(n % 4) * P + vw]
            pe.wait(turned[n], self.bank[b].get())
            for j in range(nk):
                m = pe.e.matmul(o, ptbuf[0:kw, n % n_pt, j * P:(j + 1) * P], u["v"](u["k0"] // P + j),
                                start=j == 0, stop=j == nk - 1)
            valued[n] = pe.mark(m)
            dve.wait(valued[n], weights[n])
            posted[n] = u["post"](o, st[:, n % 4, :])
            self.bank[b].set(posted[n])

        n_u = len(units)
        if wide:
            for n in range(n_u + 1):
                if n < n_u:
                    scores(n)
                    softmax(n)
                filler(n, 0)
                if n > 0:
                    values(n - 1)
                if n < n_u:
                    turn(n)
                filler(n, 1)
        else:
            for n in range(n_u + 3):
                if n < n_u:
                    scores(n)
                if 0 <= n - 2 < n_u:
                    turn(n - 2)
                if n < n_u:
                    softmax(n)
                if 0 <= n - 3:
                    values(n - 3)
        return posted[n_u - 1]

    def build(self):
        nc, p, ins, ctx = self.nc, self.p, self.ins, self.ctx
        self.n_loads, self.stores = 0, []
        self.ps = ctx.enter_context(nc.psum_tensor("ps", [P, 8, 512], F32))
        self.bank = [Last(p, f"bank{b}") for b in range(8)]
        self.w = Weights(p)
        self.ident = self.sb(ctx, "ident", [P, P])
        self.newton = self.sb(ctx, "newton", [P, 16])
        self.ones = self.sb(ctx, "ones", [P, P])
        self.gx = self.sb(ctx, "gx", [P, 4, KD])
        self.gsub = self.sb(ctx, "subln", [P, 2, KD])
        self.cvec = self.sb(ctx, "cvec", [P, 2, KD])
        self.halves = self.sb(ctx, "halves", [P, 2, 8])
        self.gate_stored = None
        self.csil = self.sb(ctx, "csil", [P, 2, KD])
        self.adab = self.sb(ctx, "adab", [P, 2, 2 * KD])
        self.mod = self.sb(ctx, "mod", [P, 4, 2, KD])
        m = [p.pool.mark(p.pool.e.memset(self.ones[:, :], 1.0))]
        loads = [self.load(self.ident[:, :], ins["ident"]),
                 self.load(self.gx[:, 0, :], ins["attn_pre_g"]), self.load(self.gx[:, 1, :], ins["mlp_pre_g"]),
                 self.load(self.gx[:, 2:4, :], ins["pre_g_2"]),
                 self.load(self.gsub[:, 0, :], ins["subln"]), self.load(self.cvec[:, 0, :], ins["c_2"]), self.load(self.cvec[:, 1, :], ins["c_ctx_2"]),
                 self.load(self.adab[:, :, :], ins["ada_b_cols"])]
        self.const_ready = m + loads
        self.x_dram = nc.dram_tensor("x_scratch", [P, TX, D], F32).ap()
        self.gate_dram = nc.dram_tensor("gate_scratch", [3, D], F32).ap()
        self.engines4 = (p.pe, p.act, p.dve, p.pool)
        self.all_engines = (*self.engines4, p.sp)

        p.act.wait(self.const_ready)
        a = p.act.mark(p.act.e.activation(self.csil[:, :, :], self.cvec[:, :, :], ACT.Tanh, scale=0.5))
        p.dve.wait(a, self.const_ready)
        a = p.dve.mark(p.dve.e.scalar_tensor_tensor(self.csil[:, :, :], self.csil[:, :, :], 1.0, self.cvec[:, :, :],
                                                    ALU.add, ALU.mult))
        p.dve.wait(a)
        self.csil_ready = p.dve.mark(p.dve.e.tensor_scalar(self.csil[:, :, :], self.csil[:, :, :], 0.5, None, ALU.mult))

        self.gsub_ready = p.dve.mark(p.dve.e.tensor_scalar(self.gsub[:, 1, :], self.gsub[:, 0, :], 0.5 * (1.0 - LAM_INIT), None,
                                                           ALU.mult))

        with ExitStack() as s:
            self.stat = self.sb(ctx, "stat", [P, 2, 8])
            h = self.sb(s, "h_hi", [P, KD, S], F32R, "right"), self.sb(s, "h_lo", [P, KD, S], F32R, "right")
            h_ready = self.block_one_attention(h)
            self.block_one_mlp(h, h_ready, s)
        with ExitStack() as s:
            x = self.sb(s, "x", [P, TX, D], F32, "right")
            self.block_one_down(x)
            self.block_one_gate(x)
        self.differential()
        for m in self.stores:
            p.sp.wait(m)

    def xin(self):
        return self.ins["x"].rearrange("(t p) d -> p t d", p=P)

    def block_one_attention(self, h):
        p, ins = self.p, self.ins
        with ExitStack() as s:
            rows = self.sb(s, "rows1", [P, TX, D])
            lx = [self.load(rows[:, t, :], self.xin()[:, t, :]) for t in range(TX)]
            m = self.rms_rows_in_place(rows, TX, self.stat, lx)
            ready = self.to_columns(rows, TX, KD, h[0], h[1], m, gains=[(0, TX, self.gx[:, 0, :], None)])
            p.meet()
            with ExitStack() as s2:
                self.attention_groups(s2, h, ready, rows)
                p.meet()
            with ExitStack() as s2:
                ready = self.project_out(s2, h, rows)
                p.meet()
        return ready

    def attention_groups(self, s, h, h_ready, orow):
        p, nc, ins = self.p, self.nc, self.ins
        pe, act, dve, pool = self.engines4
        w_in = ins["w_in"]
        sb = lambda n, sh, dt=F32: self.sb(s, n, sh, dt)
        w1 = [sb(f"cmp_w1_{n}", [P, 16, P]) for n in "kv"]
        w2 = [sb(f"cmp_w2_{n}", [P, HD]) for n in "kv"]
        pe_t = sb("cmp_pe", [P, 2, 16])
        wg = sb("wg", [P, KD, 24])
        wg_hi, wg_lo = sb("wg_hi", [P, KD, 24], F32R), sb("wg_lo", [P, KD, 24], F32R)
        sink = sb("sink", [P, 8])
        nsink = sb("nsink", [P, 8])
        gates = sb("gates", [P, TX, 24])
        valid = sb("valid", [P, TX, CMP_W])
        small = [self.load(w1[0][:, :, :], ins["cmp_w1_k"].rearrange("(l r) h -> r l h", r=P)),
                 self.load(w1[1][:, :, :], ins["cmp_w1_v"].rearrange("(l r) h -> r l h", r=P)),
                 self.load(w2[0][:, :], ins["cmp_w2_k"]), self.load(w2[1][:, :], ins["cmp_w2_v"]),
                 self.load(pe_t[:, 0, :], ins["cmp_pe_k"]), self.load(pe_t[:, 1, :], ins["cmp_pe_v"]),
                 self.load(wg[:, :, :], w_in[:, 1280:1304].rearrange("(k p) n -> p k n", p=P)),
                 self.load(sink[:, :], self.row(ins["sinks"])), self.load(valid[:, :, :], ins["cmp_valid"])]
        dve.wait(small)
        a = dve.mark(dve.e.tensor_scalar(nsink[:, :], sink[:, :], -1.0, None, ALU.mult))
        a = dve.mark(dve.e.tensor_copy(wg_hi[:, :, :], wg[:, :, :]))
        dve.wait(a)
        wg_ready = dve.mark(dve.e.tensor_tensor(wg_lo[:, :, :], wg[:, :, :], wg_hi[:, :, :], ALU.subtract))
        pe.wait(wg_ready, h_ready, self.bank[0].get(), small)
        for t in range(TX):
            for k in range(KD):
                m = three(pe.e, self.ps[:, 0, t * 24:(t + 1) * 24],
                          (h[0][:, k, t * P:(t + 1) * P], h[1][:, k, t * P:(t + 1) * P]),
                          (wg_hi[:, k, :], wg_lo[:, k, :]), k == 0, k == KD - 1)
        m = pe.mark(m)
        act.wait(m, small)
        a = act.mark(act.e.activation(gates[:, :, :], self.ps[:, 0, 0:TX * 24].rearrange("p (t n) -> p t n", t=TX),
                                      ACT.Tanh, scale=0.5))
        self.bank[0].set(a)
        dve.wait(a)
        gates_ready = dve.mark(dve.e.tensor_scalar(gates[:, :, :], gates[:, :, :], 0.5, 0.5, ALU.mult, ALU.add))

        qst = sb("q_stacked", [P, 8, S], F32R)
        khh = sb("k_hi_twice", [P, 3, S], F32R)
        klo = sb("k_lo", [HD, 3, S], F32R)
        v = sb("v", [P, TX, 192])
        blocks = sb("cmp_blocks", [P, 2, 16, NCMP])
        ckhh, cklo = sb("ck_hi_twice", [P, CMP_W], F32R), sb("ck_lo", [HD, CMP_W], F32R)
        ckz = sb("ck_zero", [P, CMP_W])
        cv = sb("cv", [CMP_W, HD])
        hid = sb("cmp_hid", [P, 3, NCMP])
        bias = sb("alibi", [P, PER_G, NSA_BIAS_W + SWA_BIAS_W])
        st = sb("st1", [P, 4, 8])
        pbuf, ptbuf = sb("p1", [P, 3, S]), sb("pt1", [P, 2, S])
        part = sb("o_part", [P, 2, HD])
        bias_loaded = Counter(p, "alibi_loaded")
        attn_end = Last(p, "attn_end1")
        sink_g = sb("sink_g", [P, 2, PER_G])
        z = dve.mark(dve.e.memset(ckz[:, :], 0.0))
        dve.wait(z)
        zeroed = [dve.mark(dve.e.tensor_copy(ckhh[:, :], ckz[:, :])), dve.mark(dve.e.tensor_copy(cklo[:, :], ckz[0:HD, :])),
              dve.mark(dve.e.memset(cv[:, :], 0.0))]

        with p.loop("groups", GROUPS) as g:
            at = (512, 640, 768, 1024, 1816, 1944, 896, 1152)
            kv = self.w.push([(HD * j, HD, w_in[:, bass.ds(g * HD + c0, HD)]) for j, c0 in enumerate(at)])
            qt = self.w.push([(0, 256, w_in[:, bass.ds(g * 256, 256)]), (256, 256, w_in[:, bass.ds(g * 256 + 1304, 256)])])
            act.wait(attn_end.get())
            bias_ready = bias_loaded.inc(act.e.dma_start(
                bias[:, :, :], ins["alibi"][bass.ds(g, 1)].rearrange("g p h n -> (g p) h n")), 16)
            ready = [self.cols_product(h, kv, KD, j, j * P, None) for j in range(3)]
            for t in range(TX):
                vm = self.rows_product(h, kv, KD, t, 3 + t // 2, 320, 192, None, out_c0=(t % 2) * 192, fresh=t % 2 == 0)
            kv.release(vm)
            dve.wait(ready[0], small)
            for j in range(2):
                for par in range(2):
                    src = self.ps[j * HD:(j + 1) * HD, 0, :]
                    src = bass.AP(src.tensor, src.offset + par, [src.ap[0], [2, 16], [CMP_ST, NCMP]])
                    vec = pe_t[par * HD:(par + 1) * HD, j, :].rearrange("p (l o) -> p l o", o=1)
                    bm = dve.mark(dve.e.tensor_tensor(blocks[par * HD:(par + 1) * HD, j, :, :], src,
                                                      vec.to_broadcast([HD, 16, NCMP]), ALU.add))
            self.bank[0].set(bm)
            for j in range(3):
                b, r0 = (1, j * HD) if j < 2 else (2, 0)
                src = self.ps[r0:r0 + HD, b, :]
                a, l = split(p, khh[0:HD, j, :], klo[:, j, :], src, ready[b], None, twin=khh[HD:P, j, :])
                self.bank[b].set(a, l)
            for b in range(2):
                src = self.ps[:, 3 + b, 0:384].rearrange("p (t n) -> p t n", t=2)
                act.wait(vm)
                self.bank[3 + b].set(act.mark(act.e.copy(v[:, 2 * b:2 * b + 2, :], src)))
            for j in range(4):
                b = 4 + j
                m = self.cols_product(h, qt, KD, b, j * P, None)
                for e in range(2):
                    a, l = split(p, qst[0:HD, 2 * j + e, :], qst[HD:P, 2 * j + e, :],
                                 self.ps[e * HD:(e + 1) * HD, b, :], m, None, scale=-(HD ** -0.5))
                self.bank[b].set(a, l)
            qt.release(m)
            for j in range(2):
                pe.wait(bm, small, self.bank[j].get())
                for l in range(16):
                    m = pe.e.matmul(self.ps[:, j, 0:NCMP], w1[j][:, l, :], blocks[:, j, l, :], start=l == 0, stop=l == 15)
                hm = self.gelu_small(hid, self.ps[:, j, 0:NCMP], pe.mark(m))
                pe.wait(hm)
                if j == 0:
                    src = self.ps[0:HD, j, 64:64 + NCMP]
                    m = pe.mark(pe.e.matmul(src, w2[0][:, :], hid[:, 0, :], start=True, stop=True))
                    a, l = split(p, ckhh[0:HD, 0:NCMP], cklo[:, 0:NCMP], src, m, zeroed, twin=ckhh[HD:P, 0:NCMP])
                else:
                    src = self.ps[0:NCMP, j, 64:128]
                    m = pe.mark(pe.e.matmul(src, hid[:, 0, :], w2[1][:, :], start=True, stop=True))
                    act.wait(m, zeroed)
                    a = act.mark(act.e.copy(cv[0:NCMP, :], src))
                    l = None
                self.bank[j].set(a, l)
            a = dve.mark(dve.e.tensor_copy(sink_g[:, 0, :], sink[:, bass.ds(g * PER_G, PER_G)]))
            dve.wait(a)
            dve.mark(dve.e.tensor_scalar(sink_g[:, 1, :], sink_g[:, 0, :], -1.0, None, ALU.mult))
            p.meet()

            def nsa_post(head, t, which):
                def post(o, s):
                    a = dve.mark(dve.e.reciprocal(s[:, 3:4], s[:, 1:2]))
                    dve.wait(a, gates_ready)
                    b = dve.mark(dve.e.tensor_tensor(s[:, 4:5], s[:, 3:4],
                                                     gates[:, t, bass.ds(g * 12 + (head * 3 + which), 1)], ALU.mult))
                    dve.wait(b)
                    if which == 0:
                        return dve.mark(dve.e.tensor_scalar(part[:, 0, :], o, s[:, 4:5], None, ALU.mult))
                    dst = part[:, 1, :] if which == 1 else orow[:, t, bass.ds(g * 256 + head * HD, HD)]
                    return dve.mark(dve.e.scalar_tensor_tensor(dst, o, s[:, 4:5], part[:, which - 1, :], ALU.mult, ALU.add))
                return post

            def swa_post(head, t):
                def post(o, s):
                    a = dve.mark(dve.e.tensor_tensor(s[:, 3:4], s[:, 1:2], s[:, 2:3], ALU.add))
                    dve.wait(a)
                    a = dve.mark(dve.e.reciprocal(s[:, 4:5], s[:, 3:4]))
                    dve.wait(a)
                    dst = orow[:, t, bass.ds(g * 256 + (512 + head * HD), HD)]
                    return dve.mark(dve.e.tensor_scalar(dst, o, s[:, 4:5], None, ALU.mult))
                return post

            def qk(head, t, hh, lo):
                return [(qst[:, head, t * P:(t + 1) * P], hh), (qst[0:HD, head, t * P:(t + 1) * P], lo)]

            units = []
            for e in range(PER_G):
                for t in range(TX):
                    units.append(dict(
                        qk=qk(e, t, lambda a, b: ckhh[:, a:b], lambda a, b: cklo[:, a:b]), k0=0, w=CMP_W,
                        bias=bias[:, e, S + t * CMP_W:S + (t + 1) * CMP_W], bias_ready=bias_ready,
                        valid=valid[:, t, :], vw=HD, v=lambda k: cv[:, :], post=nsa_post(e, t, 0)))
                    for j in range(2):
                        c = HD * (1 + j)
                        units.append(dict(
                            qk=qk(e, t, lambda a, b, j=j: khh[:, j, a:b], lambda a, b, j=j: klo[:, j, a:b]), k0=0,
                            w=(t + 1) * P, bias=bias[:, e, (TX - 1 - t) * P:S], vw=HD,
                            v=lambda k, c=c: v[:, k, c:c + HD], post=nsa_post(e, t, 1 + j)))
            for e in range(PER_G):
                for t in range(TX):
                    k0 = max(0, t - 1)
                    w = (t + 1 - k0) * P
                    units.append(dict(
                        qk=qk(4 + e, t, lambda a, b: khh[:, 2, a:b], lambda a, b: klo[:, 2, a:b]), k0=k0 * P, w=w,
                        bias=bias[:, e, NSA_BIAS_W + SWA_BIAS_W - w:NSA_BIAS_W + SWA_BIAS_W], vw=HD,
                        init=sink_g[:, 1, e:e + 1], sink=sink_g[:, 0, e:e + 1],
                        v=lambda k: v[:, k, 0:HD], post=swa_post(e, t)))
            attn_end.set(self.attention(units, st, pbuf, ptbuf, False))
            p.meet()

    def gelu_small(self, hid, x, ready):
        act, dve = self.p.act, self.p.dve
        act.wait(ready)
        a = act.mark(act.e.activation(hid[:, 1, :], x, ACT.Square, scale=GELU_A))
        dve.wait(a)
        b = dve.mark(dve.e.scalar_tensor_tensor(hid[:, 2, :], hid[:, 1, :], 1.0, x, ALU.add, ALU.mult))
        act.wait(b)
        a = act.mark(act.e.activation(hid[:, 1, :], hid[:, 2, :], ACT.Tanh, scale=GELU_C))
        dve.wait(a)
        b = dve.mark(dve.e.scalar_tensor_tensor(hid[:, 2, :], hid[:, 1, :], 1.0, x, ALU.add, ALU.mult))
        dve.wait(b, self.p.pe.last())
        return dve.mark(dve.e.tensor_scalar(hid[:, 0, :], hid[:, 2, :], 0.5, None, ALU.mult))

    def modulation_buffers(self, s, layer):
        m = dict(layer=layer, acc=self.sb(s, f"mod_acc{layer}", [P, 2, 3 * D]),
                 piece=self.sb(s, f"mod_piece{layer}", [P, 2, 3 * D]),
                 loaded=[Counter(self.p, f"mod_loaded{layer}{i}") for i in range(2)],
                 read=[Last(self.p, f"mod_read{layer}{i}") for i in range(2)])
        p = self.p
        z = p.dve.mark(p.dve.e.memset(m["acc"][:, :, :], 0.0))
        m["zero"] = z
        return m

    def modulation_step(self, m, i, k):
        p, layer = self.p, m["layer"]
        p.act.wait(m["read"][i].get())
        src = self.ins["ada_w_2"][layer].rearrange("(k p) n -> p k n", p=P)[:, bass.ds(k, 1), :]
        loaded = m["loaded"][i].inc(p.act.e.dma_start(m["piece"][:, i:i + 1, :], src), 16)
        p.dve.wait(loaded, m["zero"], self.csil_ready)
        for stream in range(2):
            n = 2 * D if (layer, stream) == (1, 1) else 3 * D
            acc = m["acc"][:, stream, 0:n]
            p.dve.wait(p.dve.last())
            r = p.dve.mark(p.dve.e.scalar_tensor_tensor(acc, m["piece"][:, i, 0:n],
                                                        self.csil[:, stream, bass.ds(k, 1)], acc, ALU.mult, ALU.add))
        m["read"][i].set(r)

    def modulation_end(self, s, m):
        p, layer, ins = self.p, m["layer"], self.ins
        rows = self.sb(s, f"mod_rows{layer}", [1, 3, D])
        lb = self.load(rows[:, 0, :], ins["ada_b_2"][layer:layer + 1, 2 * D:3 * D])
        lg = self.load(rows[:, 1, :], ins["post_g_2"][layer:layer + 1, :])
        p.pe.wait(p.dve.last(), self.const_ready)
        for stream in range(2):
            acc = m["acc"]
            b = 5 + stream
            p.pe.wait(self.bank[b].get())
            for j in range(2 * KD):
                t = p.pe.e.matmul(self.ps[:, b, j:j + 1], acc[:, stream, j * P:(j + 1) * P], self.ones[:, 0:1], start=True, stop=True)
            t = p.pe.mark(t)
            mod = self.mod[:, 2 * layer + stream, :, :]
            p.dve.wait(t)
            a = p.dve.mark(p.dve.e.tensor_tensor(mod, self.ps[:, b, 0:2 * KD].rearrange("p (a k) -> p a k", a=2),
                                                 self.adab[:, layer, :].rearrange("p (a k) -> p a k", a=2), ALU.add))
            self.bank[b].set(a)
            p.dve.wait(a)
            a = p.dve.mark(p.dve.e.scalar_tensor_tensor(mod[:, 1, :], mod[:, 1, :], 1.0, self.gx[:, 2 + layer, :], ALU.add, ALU.mult))
            if (layer, stream) == (1, 1):
                continue
            p.pe.wait(self.bank[7].get())
            for hf in range(2):
                p.pe.wait(self.bank[7].get())
                t = p.pe.mark(p.pe.e.matmul(self.ps[0:1, 7, :], self.ones[:, 0:1],
                                            acc[:, stream, 2 * D + hf * 512:2 * D + (hf + 1) * 512], start=True, stop=True))
                p.dve.wait(t, lb, lg, p.dve.last(), self.gate_stored)
                a = p.dve.mark(p.dve.e.tensor_tensor(rows[:, 2, hf * 512:(hf + 1) * 512], self.ps[0:1, 7, :],
                                                     rows[:, 0, hf * 512:(hf + 1) * 512], ALU.add))
                self.bank[7].set(a)
            p.dve.wait(a)
            a = p.dve.mark(p.dve.e.tensor_tensor(rows[:, 2, :], rows[:, 2, :], rows[:, 1, :], ALU.mult))
            self.gate_stored = self.store(self.gate_dram[2 * layer + stream:2 * layer + stream + 1, :], rows[:, 2, :], a)
        self.p.dve.wait(self.gate_stored)

    def project_out(self, s, h, rows):
        p, ins = self.p, self.ins
        x = self.sb(s, "x2", [P, TX, D])
        gain = self.sb(s, "post1", [P, D])
        junk = self.sb(s, "junk2", [P, D])
        mod = self.modulation_buffers(s, 0)
        lx = [self.load(x[:, :, :], self.xin()), self.load(gain[:, :], self.row(ins["attn_post_g"]))]
        ready = self.to_columns(rows, TX, KD, h[0], h[1], p.dve.last())
        done = []
        for nh in range(2):
            w = self.w.push([(0, 512, ins["w_o"][:, nh * 512:(nh + 1) * 512])])
            done.append([self.rows_product(h, w, KD, t, 4 * nh + t, 0, 512, ready) for t in range(TX)])
            w.release(done[-1][-1])
        with p.loop("modulation0", KD // 2) as i:
            for e in range(2):
                self.modulation_step(mod, e, i * 2 + e)
        for nh in range(2):
            m = self.out_rows(done[nh], rows, TX, nh, [4 * nh + t for t in range(TX)])
        self.modulation_end(s, mod)
        p.dve.wait(lx)
        a = self.add_normed([x[:, t, :] for t in range(TX)], rows, [gain[:, :]] * TX, junk[:, :], m)
        self.x_stored = self.store(self.x_dram[:, :, :], x[:, :, :], a[-1])
        m = self.rms_rows(x, rows, TX, self.stat, a)
        ready = self.to_columns(rows, TX, KD, h[0], h[1], m, gains=[(0, TX, self.gx[:, 1, :], None)])
        p.dve.wait(self.x_stored)
        return ready

    def block_one_mlp(self, h, h_ready, s_h):
        self.s_gated = ExitStack()
        s = self.s_gated
        self.gated = self.sb(s, "g_hi", [P, KF, S], F32R), self.sb(s, "g_lo", [P, KF, S], F32R)
        with ExitStack() as s2:
            self.gate_up(s2, h, h_ready, *self.gated)
            self.p.meet()

    def block_one_down(self, x):
        p, ins = self.p, self.ins
        pe, act, dve, pool = self.engines4
        with self.s_gated as s:
            y = self.sb(s, "y4", [P, TX, D])
            gain = self.sb(s, "post2", [P, D])
            junk = self.sb(s, "junk4", [P, D])
            act.wait(dve.last(), pe.last(), self.x_stored)
            lx = [self.load(x[:, :, :], self.x_dram[:, :, :]), self.load(gain[:, :], self.row(ins["mlp_post_g"]))]
            parts = (8, 6, 4, 4)
            with p.loop("w_down", 2) as nh:
                k0 = 0
                for c in parts:
                    w = self.w.push([(0, 512, ins["w_down"][:, bass.ds(nh * 512, 512)])], row0=k0 * P, chunks=c)
                    done = [self.rows_product(self.gated, w, c, t, t, 0, 512, None, start=k0 == 0, stop=k0 + c == KF, k0=k0)
                            for t in range(TX)]
                    w.release(done[-1])
                    k0 += c
                for t in range(TX):
                    act.wait(done[t])
                    m = act.mark(act.e.copy(y[:, t, bass.ds(nh * 512, 512)], self.ps[:, t, :]))
                    self.bank[t].set(m)
            dve.wait(lx)
            self.x_ready = self.add_normed([x[:, t, :] for t in range(TX)], y, [gain[:, :]] * TX, junk[:, :], act.last())
            p.meet()

    def rms_rows_in_place(self, x, nt, stat, ready):
        p = self.p
        act = p.act
        act.wait(ready)
        for t in range(nt):
            for hf in range(2):
                act.wait(self.bank[hf].get())
                m = act.mark(act.e.activation(self.ps[:, hf, :], x[:, t, hf * 512:(hf + 1) * 512], ACT.Square,
                                              accum_out=self.halves[:, hf, t:t + 1]))
                self.bank[hf].set(m)
        p.dve.wait(m)
        a = p.dve.mark(p.dve.e.tensor_tensor(stat[:, 0, 0:nt], self.halves[:, 0, 0:nt], self.halves[:, 1, 0:nt], ALU.add))
        r = self.rsqrt(stat[:, 1, 0:nt], stat[:, 0, 0:nt], D, a)
        act.wait(r, m)
        for t in range(nt):
            m = act.mark(act.e.activation(x[:, t, :], x[:, t, :], ACT.Copy, scale=stat[:, 1, t:t + 1]))
        return m

    def gate_up(self, s, h, h_ready, ghi, glo):
        p, ins = self.p, self.ins
        pe, act, dve, pool = self.engines4
        conv = self.sb(s, "conv_wb", [P, 4, KF])
        lc = [self.load(conv[:, 0:3, :], ins["conv_w"]), self.load(conv[:, 3, :], ins["conv_b"])]
        c = self.sb(s, "conv_out", [P, 2, S])
        v = self.sb(s, "gelu_mid", [P, S])
        g = self.sb(s, "gated", [P, S])
        g_read = Last(p, "gated_read")
        c_read = [Last(p, f"conv_read{i}") for i in range(2)]
        n_tiles = FF // FT
        act.wait(lc)
        dve.wait(lc)
        pe.wait(h_ready)

        def tile(col, col_u, j, b0):
            w = self.w.push([(0, FT, ins["w_gate_up"][:, col]), (FT, FT, ins["w_gate_up"][:, col_u])])
            m = [self.cols_product(h, w, KD, b0 + i, (i % 2) * FT + (i // 2) * P, None) for i in range(4)]
            w.release(m[-1])
            for e in range(2):
                a_ps, u_ps = self.ps[:, b0 + 2 * e, :], self.ps[:, b0 + 2 * e + 1, :]
                je = j + e
                col1 = (lambda r: conv[:, r, bass.ds(je, 1)]) if not isinstance(je, int) else (lambda r: conv[:, r, je:je + 1])
                row = (lambda x: x[:, bass.ds(je, 1), :].rearrange("p a n -> p (a n)")) if not isinstance(je, int) else (lambda x: x[:, je, :])
                ce = c[:, e, :]
                act.wait(m[2 * e], c_read[e].get())
                a = act.mark(act.e.activation(ce, a_ps, ACT.Identity, bias=col1(3), scale=col1(2)))
                for r in (1, 0):
                    d = 2 - r
                    dve.wait(a, dve.last())
                    b = dve.mark(dve.e.scalar_tensor_tensor(ce[:, d:S], a_ps[:, 0:S - d], col1(r), ce[:, d:S], ALU.mult, ALU.add))
                act.wait(b, g_read.get())
                a = act.mark(act.e.activation(v[:, :], ce, ACT.Square, scale=GELU_A))
                dve.wait(a)
                b = dve.mark(dve.e.scalar_tensor_tensor(v[:, :], v[:, :], 1.0, ce, ALU.add, ALU.mult))
                act.wait(b)
                a = act.mark(act.e.activation(v[:, :], v[:, :], ACT.Tanh, scale=GELU_C))
                dve.wait(a)
                b = dve.mark(dve.e.scalar_tensor_tensor(ce, v[:, :], 1.0, ce, ALU.add, ALU.mult))
                dve.wait(b, m[2 * e + 1], g_read.get())
                b = dve.mark(dve.e.scalar_tensor_tensor(g[:, :], ce, 0.5, u_ps, ALU.mult, ALU.mult))
                self.bank[b0 + 2 * e].set(b)
                self.bank[b0 + 2 * e + 1].set(b)
                c_read[e].set(b)
                act.wait(b)
                a = act.mark(act.e.copy(row(ghi), g[:, :]))
                dve.wait(a)
                b = dve.mark(dve.e.tensor_tensor(row(glo), g[:, :], row(ghi), ALU.subtract))
                g_read.set(b)

        with p.loop("gate_up", n_tiles // 2) as i:
            for e in range(2):
                tile(bass.ds(i * (2 * FT) + e * FT, FT), bass.ds(i * (2 * FT) + (FF + e * FT), FT), i * 4 + 2 * e, 4 * e)
        for t in range(n_tiles // 2 * 2, n_tiles):
            tile(slice(t * FT, (t + 1) * FT), slice(FF + t * FT, FF + (t + 1) * FT), 2 * t, 0)

    def block_one_gate(self, x):
        p, ins = self.p, self.ins
        pe, act, dve, pool = self.engines4
        KP = PE_IN // P
        with ExitStack() as s:
            hi, lo = self.sb(s, "x5_hi", [P, KD, S], F32R), self.sb(s, "x5_lo", [P, KD, S], F32R)
            phi, plo = self.sb(s, "p_hi", [P, KP, S], F32R), self.sb(s, "p_lo", [P, KP, S], F32R)
            prow = self.sb(s, "p_rows", [P, TX, PE_IN])
            th = self.sb(s, "gate_tanh", [P, 2, 512])
            mod = self.modulation_buffers(s, 1)
            lx = self.x_ready
            act.wait(dve.last(), pe.last())
            lp = self.load(prow[:, :, :], ins["p"].rearrange("(t p) d -> p t d", p=P))
            r1 = self.to_columns(x, TX, KD, hi, lo, lx)
            r2 = self.to_columns(prow, TX, KP, phi, plo, lp)
            th_read = [Last(p, f"tanh_read{i}") for i in range(2)]
            with p.loop("ple", 2) as nh:
                w = self.w.push([(0, 512, ins["w_ple_gate"][:, bass.ds(nh * 512, 512)])])
                we = self.w.push([(0, 512, ins["w_ple"][:, bass.ds(nh * 512, 512)])], chunks=KP)
                mg = [self.rows_product((hi, lo), w, KD, t, t, 0, 512, [r1, r2]) for t in range(TX)]
                w.release(mg[-1])
                me = [self.rows_product((phi, plo), we, KP, t, 4 + t, 0, 512, None) for t in range(TX)]
                we.release(me[-1])
                for k in range(4):
                    self.modulation_step(mod, k % 2, nh * 4 + k)
                for t in range(TX):
                    tt = th[:, t % 2, :]
                    act.wait(mg[t], th_read[t % 2].get())
                    a = act.mark(act.e.activation(tt, self.ps[:, t, :], ACT.Tanh, scale=0.5))
                    self.bank[t].set(a)
                    dve.wait(a, me[t])
                    b = dve.mark(dve.e.scalar_tensor_tensor(tt, tt, 1.0, self.ps[:, 4 + t, :], ALU.add, ALU.mult))
                    self.bank[4 + t].set(b)
                    dve.wait(b)
                    xs = x[:, t, bass.ds(nh * 512, 512)]
                    b = dve.mark(dve.e.scalar_tensor_tensor(xs, tt, 0.5, xs, ALU.mult, ALU.add))
                    th_read[t % 2].set(b)
            self.x_stored = self.store(self.x_dram[:, :, :], x[:, :, :], dve.last())
            self.modulation_end(s, mod)
            dve.wait(self.x_stored)
            p.meet()

    def differential(self):
        p, ins = self.p, self.ins
        pe, act, dve, pool = self.engines4
        with ExitStack() as s:
            h = (self.sb(s, "h6_hi", [P, KD, TA * P], F32R), self.sb(s, "h6_lo", [P, KD, TA * P], F32R))
            rows = self.sb(s, "rows6", [P, TA, D])
            stat = self.stat
            act.wait(self.x_stored)
            ctx_in = ins["ctx_2"].rearrange("(t p) d -> p t d", p=P)
            lx = [self.load(rows[:, 0:TX, :], self.x_dram[:, :, :]), self.load(rows[:, TX:TA, :], ctx_in)]
            m = self.rms_rows_in_place(rows, TA, stat, lx)
            mod = lambda layer: [(0, TX, self.mod[:, 2 * layer, 1, :], self.mod[:, 2 * layer, 0, :]),
                                 (TX, TC, self.mod[:, 2 * layer + 1, 1, :], self.mod[:, 2 * layer + 1, 0, :])]
            with ExitStack() as s2:
                tmp = self.sb(s2, "shift_tmp6", [P, 2, 384])
                ready = self.to_columns(rows, TA, KD, h[0], h[1], m, gains=mod(0), tmp=tmp)
                p.meet()
            with ExitStack() as s2:
                self.differential_heads(s2, h, ready, rows)
                p.meet()
            with ExitStack() as s2:
                x, c = self.sb(s2, "x7", [P, TX, D]), self.sb(s2, "c7", [P, TC, D])
                gain = self.sb(s2, "post7", [P, 2, D])
                junk = self.sb(s2, "junk7", [P, D])
                tmp = self.sb(s2, "shift_tmp7", [P, 2, 384])
                act.wait(dve.last(), pe.last())
                lx = [self.load(x[:, :, :], self.x_dram[:, :, :]), self.load(c[:, :, :], ctx_in),
                      self.load(gain[:, 0, :], self.row(self.gate_dram[0, :])),
                      self.load(gain[:, 1, :], self.row(self.gate_dram[1, :]))]
                ready = self.to_columns(rows, TA, KD, h[0], h[1], [dve.last(), self.gsub_ready],
                                        gains=[(0, TA, self.gsub[:, 1, :], None)])
                for nh in range(2):
                    w = self.w.push([(0, 512, ins["w_out_2"][0][:, nh * 512:(nh + 1) * 512])])
                    banks = [(TA * nh + t) % 8 for t in range(TA)]
                    done = [self.rows_product(h, w, KD, t, banks[t], 0, 512, ready) for t in range(TA)]
                    w.release(done[-1])
                    m = self.out_rows(done, rows, TA, nh, banks)
                gains = [gain[:, 0, :]] * TX + [gain[:, 1, :]] * TC
                xc = [x[:, t, :] for t in range(TX)] + [c[:, t, :] for t in range(TC)]
                dve.wait(lx)
                a = self.add_normed(xc, rows, gains, junk[:, :], m)
                self.x_stored = self.store(self.x_dram[:, :, :], x[:, :, :], a[-1])
                for t in range(TA):
                    act.wait(a[t])
                    m = act.mark(act.e.activation(rows[:, t, :], xc[t], ACT.Square, accum_out=stat[:, 0, t:t + 1]))
                r = self.rsqrt(stat[:, 1, 0:TA], stat[:, 0, 0:TA], D, m)
                act.wait(r, m)
                for t in range(TA):
                    m = act.mark(act.e.activation(rows[:, t, :], xc[t], ACT.Copy, scale=stat[:, 1, t:t + 1]))
                ready = self.to_columns(rows, TA, KD, h[0], h[1], m, gains=mod(1), tmp=tmp)
                dve.wait(self.x_stored)
                p.meet()
            self.grouped(s, h, ready, rows, stat)
            p.meet()

    def rope(self, out, t2, x, cos, sin, half, ready):
        dve = self.p.dve
        n = x.shape[1]
        shape = [P, n, half]
        dve.wait(ready, dve.last())
        dve.mark(dve.e.tensor_tensor(out.rearrange("p v (a n) -> p (v a) n", a=2), x.rearrange("p v (a n) -> p (v a) n", a=2),
                                     cos.rearrange("p (o n) -> p o n", o=1).to_broadcast([P, 2 * n, half]), ALU.mult))
        a = sin.rearrange("p (o n) -> p o n", o=1)
        dve.mark(dve.e.tensor_tensor(t2[:, :, 0:half], x[:, :, half:2 * half], a[:, :, 0:half].to_broadcast(shape), ALU.mult))
        m = dve.mark(dve.e.tensor_tensor(t2[:, :, half:2 * half], x[:, :, 0:half], a[:, :, half:2 * half].to_broadcast(shape), ALU.mult))
        dve.wait(m)
        return dve.mark(dve.e.tensor_tensor(out, out, t2, ALU.add)), m

    def differential_heads(self, s, h, h_ready, orow):
        p, ins = self.p, self.ins
        pe, act, dve, pool = self.engines4
        sb = lambda n, sh, dt=F32: self.sb(s, n, sh, dt)
        w_in = ins["a_w_in_2"][0]
        T6 = TA * P
        cos, sin = sb("cos_a", [P, TX, HD // 2]), sb("sin_a", [P, TX, HD])
        lam = sb("lam", [P, 4])
        qst, khh = sb("q6", [P, 2, 2, T6], F32R), sb("k6_hi", [P, 2, 2, T6], F32R)
        klo = sb("k6_lo", [P, 2, T6], F32R)
        v = sb("v6", [P, 2, TA, P])
        zg = sb("z6", [P, 2, TA, P])
        rot, rot2 = sb("rot6", [P, 4, HD]), sb("rot6b", [P, 4, HD])
        st = sb("st6", [P, 4, 8])
        ss = sb("ss6", [P, 2, 8])
        o1, osq = sb("o1_6", [P, P]), sb("o_squares6", [P, P])
        pbuf, ptbuf = sb("p6", [P, 1, T6]), sb("pt6", [P, 2, T6])
        rot_read = Last(p, "rot_read6")
        prepared = [Last(p, f"head_prepared{b}") for b in range(2)]
        attended = [Last(p, f"head_attended{b}") for b in range(2)]
        lamb = pbuf[:, 0, 0:4 * HD]
        small = [self.load(cos[:, :, :], ins["cos_a"]), self.load(sin[:, :, :], ins["sin_a"]),
                 self.load(lamb, self.row(ins["a_lambda_2"]))]
        dve.wait(small)
        for j in range(2):
            m = dve.mark(dve.e.tensor_tensor_reduce(o1[:, j * HD:(j + 1) * HD], lamb[:, 2 * j * HD:(2 * j + 1) * HD],
                                                    lamb[:, (2 * j + 1) * HD:(2 * j + 2) * HD], 1.0, 0.0,
                                                    ALU.mult, ALU.add, lam[:, j:j + 1]))
        act.wait(m)
        a = act.mark(act.e.activation(lam[:, 2:4], lam[:, 0:2], ACT.Exp))
        dve.wait(a)
        lam_ready = dve.mark(dve.e.tensor_scalar(lam[:, 0:1], lam[:, 3:4], LAM_INIT, lam[:, 2:3], ALU.subtract, ALU.subtract))
        GB, TB = 5, 7

        def push(hd):
            return self.w.push([(P * j, P, w_in[:, bass.ds(hd * P + j * D, P)]) for j in range(4)])

        def prepare(b, tile):
            def turn(t):
                e = t % 2
                pe.wait(roped[t], self.bank[TB].get() if e == 0 else None)
                for j in range(2):
                    m = pe.e.transpose(self.ps[:, TB, j * 256 + e * P:j * 256 + (e + 1) * P],
                                       rot[:, 2 * j:2 * j + 2, :].rearrange("p a n -> p (a n)"), self.ident[:, :])
                m = pe.mark(m)
                rot_read.set(m)
                if e == 1:
                    c0, c1 = (t - 1) * P, (t + 1) * P
                    for sub in range(2):
                        hi, lo = (slice(0, HD), slice(HD, P)) if sub == 0 else (slice(HD, P), slice(0, HD))
                        q = self.ps[sub * HD:(sub + 1) * HD, TB, 0:256]
                        k = self.ps[sub * HD:(sub + 1) * HD, TB, 256:512]
                        _, l = split(p, qst[hi, b, sub, c0:c1], qst[lo, b, sub, c0:c1], q, m, None, scale=-(HD ** -0.5))
                        split(p, khh[hi, b, sub, c0:c1], klo[hi, b, c0:c1], k, m, l, twin=khh[lo, b, sub, c0:c1])
                    self.bank[TB].set(act.last(), dve.last())

            roped = {}
            act.wait(attended[b].get())
            dve.wait(attended[b].get())
            for t in range(TA):
                bank = GB + t % 2
                pe.wait(h_ready, self.bank[bank].get())
                for k in range(KD):
                    pe.wait(tile.ready(k))
                    m = three(pe.e, self.ps[:, bank, :], (h[0][:, k, t * P:(t + 1) * P], h[1][:, k, t * P:(t + 1) * P]),
                              tile.hl(k, 0, 512), k == 0, k == KD - 1)
                    if k == KD - 1:
                        m = pe.mark(m)
                    if k == 3 and t > 0:
                        turn(t - 1)
                    yield
                x = self.ps[:, bank, 0:256].rearrange("p (v n) -> p v n", v=4)
                z = self.ps[:, bank, 384:512]
                r = rot[:, :, :]
                act.wait(m)
                act.mark(act.e.activation(zg[:, b, t, :], z, ACT.Tanh, scale=0.5))
                if t >= TX:
                    act.wait(rot_read.get())
                    a = act.mark(act.e.copy(r, x))
                va = act.mark(act.e.copy(v[:, b, t, :], self.ps[:, bank, 256:384]))
                if t < TX:
                    a, _ = self.rope(r, rot2[:, :, :], x, cos[:, t, :], sin[:, t, :], HD // 2, [va, rot_read.get()])
                dve.wait(va)
                d = dve.mark(dve.e.scalar_tensor_tensor(zg[:, b, t, :], zg[:, b, t, :], 1.0, z, ALU.add, ALU.mult))
                self.bank[bank].set(va, d)
                roped[t] = a
            tile.release(m)
            yield
            turn(TA - 1)
            prepared[b].set(act.last(), dve.last())

        def attend(hd, b, filler):
            def post(t, sub):
                def f(o, s_):
                    a = dve.mark(dve.e.reciprocal(s_[:, 3:4], s_[:, 1:2]))
                    dve.wait(a, lam_ready)
                    if sub == 0:
                        return dve.mark(dve.e.tensor_scalar(o1[:, :], o, s_[:, 3:4], None, ALU.mult))
                    a = dve.mark(dve.e.tensor_tensor(s_[:, 4:5], s_[:, 3:4], lam[:, 0:1], ALU.mult))
                    dve.wait(a)
                    dst = orow[:, t, bass.ds(hd * P, P)]
                    a = dve.mark(dve.e.scalar_tensor_tensor(dst, o, s_[:, 4:5], o1[:, :], ALU.mult, ALU.add))
                    act.wait(a, act.last())
                    act.mark(act.e.activation(osq[:, :], dst, ACT.Square, accum_out=ss[:, 0, t:t + 1]))
                    return a
                return f

            units = []
            for t in range(TA):
                for sub in range(2):
                    q0, hi = t * P, slice(sub * HD, (sub + 1) * HD)
                    units.append(dict(
                        qk=[(qst[:, b, sub, q0:q0 + P], lambda a0, a1, sub=sub: khh[:, b, sub, a0:a1]),
                            (qst[hi, b, sub, q0:q0 + P], lambda a0, a1, hi=hi: klo[hi, b, a0:a1])],
                        k0=0 if t < TX else S, w=T6 if t < TX else C, bias=None, vw=P,
                        v=lambda k: v[:, b, k, :], post=post(t, sub)))
            pe.wait(prepared[b].get())
            steps = iter(()) if filler is None else filler

            def fill(n, part):
                for _ in range((3 - part) if n < 2 * TX else 2 - part):
                    next(steps, None)

            self.attention(units, st, pbuf, ptbuf, True, fill)
            for _ in steps:
                pass
            r = self.rsqrt(ss[:, 1, 0:TA], ss[:, 0, 0:TA], P, act.last())
            dve.wait(r)
            for t in range(TA):
                o = orow[:, t, bass.ds(hd * P, P)]
                m = dve.mark(dve.e.scalar_tensor_tensor(o, o, ss[:, 1, t:t + 1], zg[:, b, t, :], ALU.mult, ALU.mult))
            attended[b].set(m, pe.last())

        tiles = [push(0), push(1)]
        for _ in prepare(0, tiles[0]):
            pass
        with p.loop("diff_heads", 3) as i:
            for e in range(2):
                push(i * 2 + (2 + e))
                attend(i * 2 + e, e, prepare(1 - e, tiles[1 - e]))
        attend(6, 0, prepare(1, tiles[1]))
        attend(7, 1, None)

    def grouped(self, s, h, h_ready, orow, stat):
        p, ins = self.p, self.ins
        pe, act, dve, pool = self.engines4
        w_in = ins["b_w_in_2"][0]
        T6 = TA * P
        with ExitStack() as s2:
            sb = lambda n, sh, dt=F32: self.sb(s2, n, sh, dt)
            cos, sin = sb("cos_b", [P, TX, GD // 2]), sb("sin_b", [P, TX, GD])
            gq, gk = sb("gq", [P, GD]), sb("gk", [P, GD])
            khi, klo = sb("k8_hi", [P, 2, T6], F32R), sb("k8_lo", [P, 2, T6], F32R)
            v = sb("v8", [P, TA, 256])
            qhi, qlo = sb("q8_hi", [P, 2, 2, S], F32R), sb("q8_lo", [P, 2, 2, S], F32R)
            raw, rot = sb("raw8", [P, 2, 2, GD]), sb("rot8", [P, 2, 2, GD])
            rot2 = sb("rot8b", [P, 2, GD])
            st = sb("st8", [P, 4, 8])
            ss = sb("ss8", [P, 2, 4])
            junk = sb("junk8", [P, GD])
            pbuf, ptbuf = sb("p8", [P, 1, T6]), sb("pt8", [P, 2, T6])
            small = [self.load(cos[:, :, :], ins["cos_b"]), self.load(sin[:, :, :], ins["sin_b"]),
                     self.load(gq[:, :], self.row(ins["b_qk_g_2"][0:GD])),
                     self.load(gk[:, :], self.row(ins["b_qk_g_2"][GD:2 * GD]))]
            dve.wait(small)
            g_ready = dve.mark(dve.e.tensor_scalar(gq[:, :], gq[:, :], -(GD ** -0.5), None, ALU.mult))
            GB, TB = 5, 7
            raw_read, rot_read = Last(p, "raw_read8"), Last(p, "rot_read8")
            attended = [None, None]

            def prepare(tile, nt, gain, hi, lo, free, second):
                def norm_rope(t):
                    r = self.rsqrt(ss[:, 1, :], ss[:, 0, :], GD, [act.last(), rot_read.get()])
                    dve.wait(r, g_ready)
                    for e in range(2):
                        u = t - 1 + e
                        for a in range(2):
                            dst = raw if u < TX else rot
                            m = dve.mark(dve.e.scalar_tensor_tensor(dst[:, e, a, :], raw[:, e, a, :], ss[:, 1, 2 * e + a:2 * e + a + 1],
                                                                    gain[:, :], ALU.mult, ALU.mult))
                        if u < TX:
                            m, _ = self.rope(rot[:, e, :, :], rot2[:, :, :], raw[:, e, :, :], cos[:, u, :], sin[:, u, :], GD // 2, m)
                    raw_read.set(m)
                    return m

                def turn(t, roped):
                    pe.wait(roped, self.bank[TB].get())
                    for e in range(2):
                        for a in range(2):
                            m = pe.e.transpose(self.ps[:, TB, (2 * e + a) * P:(2 * e + a + 1) * P], rot[:, e, a, :], self.ident[:, :])
                    m = pe.mark(m)
                    rot_read.set(m)
                    src = self.ps[:, TB, :].rearrange("p (e a n) -> p a e n", e=2, a=2)
                    h_, l_ = (x[:, :, (t - 1) * P:(t + 1) * P].rearrange("p a (e n) -> p a e n", e=2) for x in (hi, lo))
                    self.bank[TB].set(*split(p, h_, l_, src, m, free))

                roped = None
                for t in range(nt):
                    bank = GB + t % 2
                    pe.wait(h_ready, self.bank[bank].get())
                    for k in range(KD):
                        pe.wait(tile.ready(k))
                        m = three(pe.e, self.ps[:, bank, :], (h[0][:, k, t * P:(t + 1) * P], h[1][:, k, t * P:(t + 1) * P]),
                                  tile.hl(k, 0, 512), k == 0, k == KD - 1)
                        if k == KD - 1:
                            m = pe.mark(m)
                        if k == 5 and t % 2 == 0 and t > 0:
                            turn(t - 1, roped)
                        yield
                    e = t % 2
                    act.wait(m, raw_read.get())
                    c = act.mark(act.e.copy(raw[:, e, :, :], self.ps[:, bank, 0:256].rearrange("p (a n) -> p a n", a=2)))
                    for a in range(2):
                        act.wait(act.last(), dve.last() if a + e == 0 else None)
                        c = act.mark(act.e.activation(junk[:, :], self.ps[:, bank, a * GD:(a + 1) * GD], ACT.Square,
                                                      accum_out=ss[:, 0, 2 * e + a:2 * e + a + 1]))
                    self.bank[bank].set(*second(t, bank, m))
                    if e == 1:
                        roped = norm_rope(t)
                tile.release(m)
                yield
                turn(nt - 1, roped)

            def values(t, bank, done):
                return [act.mark(act.e.copy(v[:, t, :], self.ps[:, bank, 256:512]))]

            def silu(pair):
                def f(t, bank, done):
                    z, dst = self.ps[:, bank, 256:512], orow[:, t, pair * 256:(pair + 1) * 256]
                    a = act.mark(act.e.activation(dst, z, ACT.Tanh, scale=0.5))
                    dve.wait(a)
                    return a, dve.mark(dve.e.scalar_tensor_tensor(dst, dst, 1.0, z, ALU.add, ALU.mult))
                return f

            def push(pair):
                c = pair * 256
                return self.w.push([(0, 256, w_in[:, c:c + 256]), (256, 256, w_in[:, c + D + 512:c + D + 768])])

            def prepare_pair(pair, tile):
                b = pair % 2
                return prepare(tile, TX, gq, qhi[:, b, :, :], qlo[:, b, :, :], attended[b], silu(pair))

            def attend(pair, filler):
                g, b = pair // 2, pair % 2

                def post(t, e):
                    def f(o, s_):
                        a = dve.mark(dve.e.tensor_scalar(s_[:, 3:4], s_[:, 1:2], 2.0, None, ALU.mult))
                        dve.wait(a)
                        a = dve.mark(dve.e.reciprocal(s_[:, 4:5], s_[:, 3:4]))
                        dve.wait(a)
                        dst = orow[:, t, pair * 256 + e * GD:pair * 256 + (e + 1) * GD]
                        return dve.mark(dve.e.scalar_tensor_tensor(dst, o, s_[:, 4:5], dst, ALU.mult, ALU.mult))
                    return f

                units = []
                for e in range(2):
                    for t in range(TX):
                        q = [x[:, b, e, t * P:(t + 1) * P] for x in (qhi, qlo)]
                        kk = [(lambda a0, a1, x=x: x[:, g, a0:a1]) for x in (khi, klo)]
                        units.append(dict(qk=[(q[0], kk[0]), (q[0], kk[1]), (q[1], kk[0])], k0=0, w=T6, bias=None, vw=P,
                                          v=lambda k: v[:, k, g * GD:(g + 1) * GD],
                                          post=post(t, e)))
                pe.wait(act.last(), dve.last())
                steps = iter(()) if filler is None else filler

                def fill(n, part):
                    for _ in range(3 if part == 0 and n % 2 == 0 else 2):
                        next(steps, None)

                self.attention(units, st, pbuf, ptbuf, True, fill)
                for _ in steps:
                    pass
                attended[b] = pe.last()

            kv = prepare(self.w.push([(0, 512, w_in[:, D:D + 512])]), TA, gk, khi, klo, None, values)
            for _ in range(TA * KD + 1):
                next(kv)
            first = prepare_pair(0, push(0))
            for _ in range(KD):
                next(first)
            for gen in (kv, first):
                for _ in gen:
                    pass
            n_pairs = D // 256
            for pair in range(n_pairs):
                attend(pair, prepare_pair(pair + 1, push(pair + 1)) if pair + 1 < n_pairs else None)
            p.meet()

        with ExitStack() as s2:
            x = self.sb(s2, "x9", [P, TX, D])
            gain = self.sb(s2, "post9", [P, D])
            junk = self.sb(s2, "junk9", [P, D])
            act.wait(dve.last(), pe.last())
            lx = [self.load(x[:, :, :], self.x_dram[:, :, :]), self.load(gain[:, :], self.row(self.gate_dram[2, :]))]
            ready = self.to_columns(orow, TX, KD, h[0], h[1], dve.last())
            for nh in range(2):
                w = self.w.push([(0, 512, ins["w_out_2"][1][:, nh * 512:(nh + 1) * 512])])
                banks = [4 * nh + t for t in range(TX)]
                done = [self.rows_product(h, w, KD, t, banks[t], 0, 512, ready) for t in range(TX)]
                w.release(done[-1])
                m = self.out_rows(done, orow, TX, nh, banks)
            dve.wait(lx)
            a = self.add_normed([x[:, t, :] for t in range(TX)], orow, [gain[:, :]] * TX, junk[:, :], m)
            out = self.outs["out"].rearrange("(t p) d -> p t d", p=P)
            for t in range(TX):
                self.store(out[:, t, :], x[:, t, :], a[t])


def constants():
    c = {"ident": np.eye(P, dtype=np.float32)}
    slopes = np.exp2(-8.0 * (np.arange(16, dtype=np.float32) + 1.0) / 16).astype(np.float32)
    pr = np.arange(P)[:, None]
    alibi = np.zeros((GROUPS, P, PER_G, NSA_BIAS_W + SWA_BIAS_W), np.float32)
    dist = pr + (S - P) - np.arange(S)[None, :]
    n = np.arange(CMP_W)
    dist_c = (np.arange(TX)[None, :, None] * P + np.arange(P)[:, None, None]) - (n * CMP_ST + CMP_L - 1)[None, None, :]
    ok_c = (dist_c >= 0) & (n < NCMP)
    dist_s = P + pr - np.arange(SWA_BIAS_W)[None, :]
    for g in range(GROUPS):
        for e in range(PER_G):
            nsa, swa = slopes[8 + g * PER_G + e], slopes[g * PER_G + e]
            alibi[g, :, e, 0:S] = np.where(dist >= 0, nsa * dist, BIG)
            alibi[g, :, e, S:NSA_BIAS_W] = np.where(ok_c, nsa * dist_c, BIG).reshape(P, TX * CMP_W)
            alibi[g, :, e, NSA_BIAS_W:] = np.where((dist_s >= 0) & (dist_s < P), swa * dist_s, BIG)
    c["alibi"] = alibi
    c["cmp_valid"] = ok_c.astype(np.float32)
    for name, hd in (("a", HD), ("b", GD)):
        axis = hd // 2
        freqs = (10000.0 ** (-np.arange(0, axis, 2, dtype=np.float32) / axis)).astype(np.float32)
        tok = np.arange(S)
        ang = np.concatenate([(tok // 64).astype(np.float32)[:, None] * freqs,
                              (tok % 64).astype(np.float32)[:, None] * freqs], axis=-1).astype(np.float32)
        cos, sin = np.cos(ang), np.sin(ang)
        for nm, v in (("cos", cos), ("sin", np.concatenate([-sin, sin], -1))):
            c[f"{nm}_{name}"] = np.ascontiguousarray(v.reshape(TX, P, -1).transpose(1, 0, 2).astype(np.float32))
    return c


def lay_out(a):
    by_feature = lambda v, *lead: np.ascontiguousarray(np.moveaxis(np.reshape(v, (*lead, -1, P)), -1, 0))
    o = {
        "x": a["x"][0], "p": a["p"][0, 0], "w_in": a["w_in"][0],
        "attn_pre_g": by_feature(a["attn_pre_g"][0]), "mlp_pre_g": by_feature(a["mlp_pre_g"][0]),
        "pre_g_2": by_feature(a["pre_g_2"], 2),
        "cmp_w1_k": a["cmp_w1_k"][0], "cmp_w2_k": a["cmp_w2_k"][0],
        "cmp_w1_v": a["cmp_w1_v"][0], "cmp_w2_v": a["cmp_w2_v"][0],
        "cmp_pe_k": by_feature(a["cmp_pe_k"][0]), "cmp_pe_v": by_feature(a["cmp_pe_v"][0]),
        "sinks": a["sinks"][0], "w_o": a["w_o"][0], "attn_post_g": a["attn_post_g"][0],
        "w_gate_up": a["w_gate_up"][0], "conv_w": by_feature(a["conv_w"][0], 3), "conv_b": by_feature(a["conv_b"][0]),
        "w_down": a["w_down"][0], "mlp_post_g": a["mlp_post_g"][0],
        "w_ple": a["w_ple"][0], "w_ple_gate": a["w_ple_gate"][0],
        "c_2": by_feature(a["c_2"][0]), "c_ctx_2": by_feature(a["c_ctx_2"]), "ctx_2": a["ctx_2"][0],
        "ada_w_2": a["ada_w_2"], "ada_b_2": a["ada_b_2"], "ada_b_cols": by_feature(a["ada_b_2"][:, 0:2 * D], 2),
        "post_g_2": a["post_g_2"], "w_out_2": a["w_out_2"], "a_w_in_2": a["a_w_in_2"], "b_w_in_2": a["b_w_in_2"],
        "a_lambda_2": np.reshape(a["a_lambda_2"][0], -1), "subln": np.repeat(a["a_subln_g_2"][0][:, None], KD, 1),
        "b_qk_g_2": np.reshape(a["b_qk_g_2"][0], -1),
    }
    o.update(constants())
    return {k: np.ascontiguousarray(v) for k, v in o.items()}


def program(nc, arrays, counts):
    ins = {n: nc.dram_tensor("in_" + n, a.shape, mybir.dt.from_np(a.dtype), kind="ExternalInput").ap()
           for n, a in arrays.items()}
    outs = {"out": nc.dram_tensor("out_0", (S, D), F32, kind="ExternalOutput").ap()}
    Kernel(nc, ins, outs, counts)


def kernel(**inputs):
    import numpy as _np
    import concourse.bacc as _bacc
    from concourse.bass_utils import run_bass_kernel_spmd as _run

    arrays = lay_out({k: _np.asarray(v) for k, v in inputs.items()})
    counts = {}
    for _ in range(2):
        nc = _bacc.Bacc("TRN2", target_bir_lowering=False, num_devices=1)
        program(nc, arrays, counts)
    r = _run(nc, [{"in_" + n: a for n, a in arrays.items()}], core_ids=[0])
    return _np.reshape(r.results[0]["out_0"], (1, S, D))
```

```python
import math
from contextlib import ExitStack, contextmanager

import numpy as np
import concourse.bass as bass
from concourse import mybir

F32 = mybir.dt.float32
F32R = mybir.dt.float32r
I32 = mybir.dt.int32
ALU = mybir.AluOpType
ACT = mybir.ActivationFunctionType
AX = mybir.AxisListType

P = 128
S = 512
C = 256
D = 1024
KD = D // P
TX, TC = S // P, C // P
TA = TX + TC
HD = 64
GD = 128
GROUPS, PER_G = 2, 4
NCMP, CMP_W = 31, 32
CMP_L, CMP_ST = 32, 16
PE_IN = 256
FF = 2816
KF = FF // P
FT = 256
EPS = 1e-6
BIG = 1e30
HEAD = 1000
LAM_INIT = 0.8 - 0.6 * math.exp(-0.3 * 0)
GELU_C = math.sqrt(2.0 / math.pi)
GELU_A = math.sqrt(0.044715)
NSA_BIAS_W = S + TX * CMP_W
SWA_BIAS_W = 2 * P


class Mark:

    def __init__(self, sem, const, coeff=0, loop=None):
        self.sem, self.const, self.coeff, self.loop = sem, const, coeff, loop

    def value(self):
        if self.loop is None or self.coeff == 0:
            return self.const
        if self.loop.active:
            return self.loop.i * self.coeff + self.const
        return self.const + self.coeff * (self.loop.n - 1)


class Counter:

    def __init__(self, prog, name, start=0):
        self.h = prog.ctx.enter_context(prog.nc.semaphore(name))
        self.name, self.const, self.coeff, self.loop = name, start, 0, None
        prog.counters.append(self)

    def inc(self, instr, by=1):
        instr.then_inc(self.h, by)
        self.const += by
        return Mark(self, self.const, self.coeff, self.loop)


class Engine:

    def __init__(self, prog, e, name, compute=True):
        self.e, self.seen = e, {}
        self.settled = prog.ctx.enter_context(prog.nc.semaphore(name + "_settled"))
        self.done = Counter(prog, name + "_done", HEAD) if compute else None
        if compute:
            e.sem_inc(self.done.h, HEAD)
        prog.engines.append(self)

    def wait(self, *marks):
        for m in marks:
            if m is None:
                continue
            if isinstance(m, (list, tuple)):
                self.wait(*m)
                continue
            fixed = m.loop is None or m.coeff == 0 or not m.loop.active
            key = (m.sem.name, fixed)
            const = m.value() if fixed else m.const
            if self.seen.get(key, -1) >= const:
                continue
            self.seen[key] = const
            self.e.wait_ge(m.sem.h, m.value())

    def mark(self, instr):
        return self.done.inc(instr)

    def settle(self):
        self.e.sem_inc(self.settled, 1)

    def last(self):
        return Mark(self.done, self.done.const, self.done.coeff, self.done.loop)


class Last:

    def __init__(self, prog, name):
        self.prog, self.name, self.marks, self.fresh = prog, name, [], False
        prog.lasts.append(self)

    def set(self, *marks):
        self.marks, self.fresh = [m for m in marks if m is not None], True

    def get(self):
        loop = self.prog.loop_now
        if loop is None or self.fresh:
            return list(self.marks)
        before = []
        for cname, off in self.prog.counts.get((loop.name, self.name), []):
            c = self.prog.by_name(cname)
            before.append(Mark(c, loop.base[cname] + off - c.coeff, c.coeff, loop))
        return list(self.marks) + before


class Loop:
    def __init__(self, name, n):
        self.name, self.n, self.active, self.i, self.base = name, n, True, None, {}


class Prog:

    def __init__(self, nc, ctx, counts):
        self.nc, self.ctx, self.counts = nc, ctx, counts
        self.counters, self.engines, self.lasts, self.loop_now = [], [], [], None
        self.pe = Engine(self, nc.tensor, "pe")
        self.act = Engine(self, nc.scalar, "act")
        self.dve = Engine(self, nc.vector, "dve")
        self.pool = Engine(self, nc.gpsimd, "pool")
        self.sp = Engine(self, nc.sync, "sp", compute=False)

    def by_name(self, name):
        return [c for c in self.counters if c.name == name][0]

    def meet(self):
        engines = (self.pe, self.act, self.dve)
        for a in engines:
            a.wait(*[b.last() for b in engines])

    @contextmanager
    def loop(self, name, n):
        loop = Loop(name, n)
        start = {c.name: c.const for c in self.counters}
        loop.base = start
        with self.nc.Fori(0, n) as i:
            loop.i = i
            for c in self.counters:
                c.coeff, c.loop = self.counts.get((name, c.name), 0), loop
            for e in self.engines:
                e.seen = {}
            for x in self.lasts:
                x.fresh = False
            self.loop_now = loop
            yield i
        for c in self.counters:
            self.counts[(name, c.name)] = c.const - start[c.name]
            c.const = start[c.name] + n * (c.const - start[c.name])
            c.coeff, c.loop = 0, None
        for x in self.lasts:
            if x.fresh:
                self.counts[(name, x.name)] = [(m.sem.name, m.const - start[m.sem.name]) for m in x.marks if m.loop is loop]
        for e in self.engines:
            e.seen = {}
        loop.active = False
        self.loop_now = None


class Weights:

    def __init__(self, prog):
        self.p = prog
        c, nc = prog.ctx, prog.nc
        self.raw = c.enter_context(nc.sbuf_tensor("w_raw", [P, 2, 2, 512], F32))
        self.hi = c.enter_context(nc.sbuf_tensor("w_hi", [P, 2, KD, 512], F32R))
        self.lo = c.enter_context(nc.sbuf_tensor("w_lo", [P, 2, KD, 512], F32R))
        self.loaded = [Counter(prog, f"w_loaded{s}") for s in range(2)]
        self.raw_read = [Last(prog, f"w_raw_read{s}") for s in range(2)]
        self.tile_read = [Last(prog, f"w_tile_read{s}") for s in range(2)]
        self.ready = [[Last(prog, f"w_ready{s}_{q}") for q in range(KD // 2)] for s in range(2)]
        self.turn = 0

    def push(self, sources, row0=0, chunks=KD, gain=None):
        p, slot = self.p, self.turn
        self.turn = 1 - self.turn
        width = max(c0 + n for c0, n, _ in sources)
        for q in range(0, chunks, 2):
            r = (q // 2) % 2
            p.sp.wait(self.raw_read[r].get())
            for c0, n, src in sources:
                rows = src[row0 + q * P:row0 + (q + 2) * P, :].rearrange("(c p) n -> p c n", p=P)
                loaded = self.loaded[r].inc(p.sp.e.dma_start(self.raw[:, r, :, c0:c0 + n], rows), 16)
            raw = self.raw[:, r, :, 0:width]
            hi, lo = self.hi[:, slot, q:q + 2, 0:width], self.lo[:, slot, q:q + 2, 0:width]
            p.pool.wait(loaded, self.tile_read[slot].get())
            p.pool.settle()
            if gain is not None:
                p.pool.wait(gain[1])
                a = p.pool.mark(p.pool.e.tensor_scalar(raw, raw, gain[0], None, ALU.mult))
                p.pool.wait(a)
            a = p.pool.mark(p.pool.e.tensor_scalar(hi, raw, 1.0, 0.0, ALU.mult, ALU.add))
            p.pool.wait(a)
            b = p.pool.mark(p.pool.e.tensor_tensor(lo, raw, hi, ALU.subtract))
            self.raw_read[r].set(b)
            self.ready[slot][q // 2].set(b)
        return Tile(self, slot)


class Tile:

    def __init__(self, w, slot):
        self.w, self.slot = w, slot

    def ready(self, k):
        return self.w.ready[self.slot][k // 2].get()

    def hl(self, k, c0, n):
        return self.w.hi[:, self.slot, k, c0:c0 + n], self.w.lo[:, self.slot, k, c0:c0 + n]

    def release(self, mark):
        self.w.tile_read[self.slot].set(mark)


def three(e, out, a, b, start, stop):
    e.matmul(out, a[0], b[0], start=start, stop=False)
    e.matmul(out, a[0], b[1], start=False, stop=False)
    return e.matmul(out, a[1], b[0], start=False, stop=stop)


def split(prog, hi, lo, ps, ready, free=None, scale=None, twin=None):
    act, dve = prog.act, prog.dve
    act.wait(ready, free)
    a = act.mark(act.e.activation(hi, ps, ACT.Copy, scale=1.0 if scale is None else scale))
    if twin is not None:
        a = act.mark(act.e.copy(twin, ps))
    dve.wait(a)
    if scale is not None:
        b = dve.mark(dve.e.scalar_tensor_tensor(lo, ps, scale, hi, ALU.mult, ALU.subtract))
    else:
        b = dve.mark(dve.e.tensor_tensor(lo, ps, hi, ALU.subtract))
    return a, b


class Kernel:
    def __init__(self, nc, ins, outs, counts):
        self.nc, self.ins, self.outs = nc, ins, outs
        self.ctx = ExitStack()
        with self.ctx:
            self.p = Prog(nc, self.ctx, counts)
            self.build()

    def sb(self, ctx, name, shape, dt=F32, side="left"):
        return ctx.enter_context(self.nc.sbuf_tensor(name, shape, dt, side=side))

    def load(self, out, src, sem=None):
        self.n_loads += 1
        c = sem or Counter(self.p, f"load{self.n_loads}")
        return c.inc(self.p.act.e.dma_start(out, src), 16)

    def store(self, out, src, after):
        self.n_loads += 1
        c = Counter(self.p, f"store{self.n_loads}")
        self.p.act.wait(after)
        m = c.inc(self.p.act.e.dma_start(out, src), 16)
        self.stores.append(m)
        return m

    def row(self, v):
        return v.rearrange("(a n) -> a n", a=1).partition_broadcast(P)

    def rsqrt(self, out, ssq, count, ready):
        dve, n = self.p.dve, out.shape[-1]
        t = self.newton[:, 0:n]

        def step(instr):
            m = dve.mark(instr)
            dve.wait(m)
            return m

        dve.wait(ready, dve.last())
        step(dve.e.tensor_scalar(ssq, ssq, 1.0 / count, EPS, ALU.mult, ALU.add))
        step(dve.e.tensor_scalar(t.bitcast(I32), ssq.bitcast(I32), 1, None, ALU.logical_shift_right))
        step(dve.e.tensor_scalar(out.bitcast(I32), t.bitcast(I32), -1, 0x5F3759DF, ALU.mult, ALU.add))
        for _ in range(3):
            step(dve.e.scalar_tensor_tensor(t, out, -0.5, out, ALU.mult, ALU.mult))
            step(dve.e.tensor_tensor(t, t, ssq, ALU.mult))
            m = step(dve.e.scalar_tensor_tensor(out, t, 1.5, out, ALU.add, ALU.mult))
        return m

    def turn_tile(self, row, t, cols, banks, ready, gain=None, shift=None, tmp=None):
        p = self.p
        pe, act, dve = p.pe, p.act, p.dve
        hi, lo = (x[:, :, t * P:(t + 1) * P] for x in cols)
        per = KD // 2
        for g, b in enumerate(banks):
            pe.wait(ready, self.bank[b].get(), self.const_ready)
            for k in range(per):
                m = pe.e.transpose(self.ps[:, b, k * P:(k + 1) * P], row[:, (per * g + k) * P:(per * g + k + 1) * P],
                                   self.ident[:, :])
            m = pe.mark(m)
            ks = slice(per * g, per * (g + 1))
            src = self.ps[:, b, :].rearrange("p (k n) -> p k n", k=per)
            if gain is None:
                a, l = split(p, hi[:, ks, :], lo[:, ks, :], src, m)
                self.bank[b].set(a, l)
                continue
            act.wait(m, self.tmp_read[g] if shift is not None else None)
            chunks = [(per * g + k, self.ps[:, b, k * P:(k + 1) * P], tmp[:, g, k * P:(k + 1) * P] if shift is not None else None)
                      for k in range(per)]
            if shift is None:
                for f, i, _ in chunks:
                    a = act.mark(act.e.activation(hi[:, f, :], i, ACT.Copy, scale=gain[:, f:f + 1]))
                dve.wait(a)
                for f, i, _ in chunks:
                    l = dve.mark(dve.e.scalar_tensor_tensor(lo[:, f, :], i, gain[:, f:f + 1], hi[:, f, :], ALU.mult, ALU.subtract))
                self.bank[b].set(a, l)
            else:
                for f, i, o in chunks:
                    a = act.mark(act.e.activation(o, i, ACT.Identity, bias=shift[:, f:f + 1], scale=gain[:, f:f + 1]))
                self.bank[b].set(a)
                a, l = split(p, hi[:, ks, :], lo[:, ks, :], tmp[:, g, :].rearrange("p (k n) -> p k n", k=per), a)
                self.tmp_read[g] = l
        return [a, l]

    def squares(self, halves, junk, i, ready):
        act = self.p.act
        act.wait(ready)
        for hf in range(2):
            m = act.mark(act.e.activation(junk[:, hf * 512:(hf + 1) * 512], halves[hf], ACT.Square,
                                          accum_out=self.halves[:, hf, i:i + 1]))
        return m

    def inverse_rms(self, i0, i1, ready):
        dve = self.p.dve
        dve.wait(ready)
        m = dve.mark(dve.e.tensor_tensor(self.stat[:, 0, i0:i1], self.halves[:, 0, i0:i1], self.halves[:, 1, i0:i1], ALU.add))
        return self.rsqrt(self.stat[:, 1, i0:i1], self.stat[:, 0, i0:i1], D, m)

    def scale_rows(self, out, x, i, ready):
        act = self.p.act
        act.wait(ready)
        return act.mark(act.e.activation(out, x, ACT.Copy, scale=self.stat[:, 1, i:i + 1]))

    def normed_adder(self, x, gain, y, loaded, rows, store):
        p = self.p
        act, dve = p.act, p.dve
        xs, normed, y_read = {}, {}, {}

        def squares_of_x(t):
            return self.squares((x[:, t, 0:512], x[:, t, 512:D]), rows[:, t, :], 2 * t + 3, xs[t])

        def add(t, banks, done):
            before = rows is not None and t > 0
            m = squares_of_x(t - 1) if before else None
            v = [self.ps[:, b, :] for b in banks]
            yt = y[:, t % 2, :]
            m = self.squares(v, yt, 2 * t, [m, done, y_read.get(t % 2)])
            r = self.inverse_rms(2 * t, 2 * t + (2 if before else 1), m)
            if before:
                normed[t - 1] = self.scale_rows(rows[:, t - 1, :], x[:, t - 1, :], 2 * t + 1, r)
            dve.wait(r, loaded[t])
            for hf in range(2):
                c = slice(hf * 512, (hf + 1) * 512)
                a = dve.mark(dve.e.scalar_tensor_tensor(yt[:, c], v[hf], self.stat[:, 1, 2 * t:2 * t + 1], gain(t)[:, c],
                                                        ALU.mult, ALU.mult))
                self.bank[banks[hf]].set(a)
            dve.wait(a)
            xs[t] = y_read[t % 2] = dve.mark(dve.e.tensor_tensor(x[:, t, :], x[:, t, :], yt, ALU.add))
            store(t, xs[t])

        def last():
            t = max(xs)
            m = squares_of_x(t)
            r = self.inverse_rms(2 * t + 3, 2 * t + 4, m)
            normed[t] = self.scale_rows(rows[:, t, :], x[:, t, :], 2 * t + 3, r)

        return add, last, normed

    def tiles_product(self, nt, cols, weights, turn_in, add, last, turn_out, beside=None, ahead=None):
        ready = {0: turn_in(0)}
        for t in range(nt):
            if t + 1 < nt:
                ready[t + 1] = turn_in(t + 1)
            banks = [2 * (t % 2) + nh if beside is None else nh for nh in range(2)]
            done = []
            for nh in range(2):
                done.append(self.rows_product(cols, weights[nh], KD, t, banks[nh], 0, 512, ready[t]))
                weights[nh].release(done[nh])
                if beside is not None:
                    beside(t, nh, banks[nh], done[nh])
                if t >= 2 and nh == 0:
                    turn_out(t - 2)
            add(t, banks, done)
        if last is not None:
            turn_out(nt - 2)
            early = ahead() if ahead is not None else None
            last()
            turn_out(nt - 1)
            return early

    def products_ahead(self, cols, tile, where, ready):
        return {t: (b, self.rows_product(cols, tile, KD, t, b, 0, 512, ready[t])) for t, b in where}

    def head_tile(self, hd):
        w_in = self.ins["a_w_in_2"][0]
        return self.w.push([(P * j, P, w_in[:, bass.ds(hd * P + j * D, P)]) for j in range(4)])

    def rows_product(self, cols, tile, chunks, t, bank, c0, n, ready, out_c0=0, start=True, stop=True, k0=0, fresh=True):
        p = self.p
        p.pe.wait(ready, self.bank[bank].get() if start and fresh else None)
        for k in range(chunks):
            p.pe.wait(tile.ready(k))
            m = three(p.pe.e, self.ps[:, bank, out_c0:out_c0 + n],
                      (cols[0][:, k0 + k, t * P:(t + 1) * P], cols[1][:, k0 + k, t * P:(t + 1) * P]),
                      tile.hl(k, c0, n), start and k == 0, stop and k == chunks - 1)
        return p.pe.mark(m)

    def cols_product(self, cols, tile, chunks, bank, c0, ready, n=S):
        p = self.p
        p.pe.wait(ready, self.bank[bank].get())
        for k in range(chunks):
            p.pe.wait(tile.ready(k))
            m = three(p.pe.e, self.ps[:, bank, 0:n], tile.hl(k, c0, P),
                      (cols[0][:, k, 0:n], cols[1][:, k, 0:n]), k == 0, k == chunks - 1)
        return p.pe.mark(m)

    def attention(self, units, st, pbuf, ptbuf, wide, filler=None):
        p = self.p
        pe, act, dve = p.pe, p.act, p.dve
        S0, T0, O0 = 0, 2, 4
        n_p, n_pt = pbuf.shape[1], ptbuf.shape[1]
        scored, weights, turned, valued, posted = {}, {}, {}, {}, {}

        def banks(step, n, w):
            if not wide:
                b0 = (S0 if step == "scores" else T0) + n % 2
            elif step == "scores":
                b0 = S0 if filler is not None or n % 2 == 0 else 5
            else:
                b0 = T0
            return ([b0, b0 + 1], w // 2) if w > 512 else ([b0], w)

        def out_bank(n):
            return (O0, 7)[n % 2 if filler is None else 0] if wide else O0 + n % 2

        def view(bs, rows, cols):
            return self.ps[0:rows, bs[0]:bs[0] + 2, 0:cols] if len(bs) == 2 else self.ps[0:rows, bs[0], 0:cols]

        def folded(x, bs):
            return x.rearrange("p (a b) -> p a b", a=2) if len(bs) == 2 else x

        def scores(n):
            u = units[n]
            bs, cols = banks("scores", n, u["w"])
            pe.wait(u.get("ready"))
            for c, b in enumerate(bs):
                pe.wait(self.bank[b].get())
                for i, (q, k) in enumerate(u["qk"]):
                    m = pe.e.matmul(self.ps[:, b, 0:cols], q, k(u["k0"] + c * cols, u["k0"] + (c + 1) * cols),
                                    start=i == 0, stop=i == len(u["qk"]) - 1)
            scored[n] = pe.mark(m)

        def softmax(n):
            u = units[n]
            bs, cols = banks("scores", n, u["w"])
            sc, s, pr = view(bs, P, cols), st[:, n % 4, :], pbuf[:, n % n_p, 0:u["w"]]
            dve.wait(scored[n])
            if u["bias"] is not None:
                dve.wait(u.get("bias_ready"))
                dve.settle()
                a = dve.mark(dve.e.tensor_tensor_reduce(sc, sc, u["bias"], 1.0, u.get("init", 3e38), ALU.add, ALU.min,
                                                        s[:, 0:1]))
            else:
                a = dve.mark(dve.e.tensor_reduce(s[:, 0:1], sc, AX.XY if len(bs) == 2 else AX.X, ALU.min))
            act.wait(a)
            e = act.mark(act.e.activation(folded(pr, bs), sc, ACT.Exp, bias=s[:, 0:1], scale=-1.0, accum_out=s[:, 1:2]))
            for b in bs:
                self.bank[b].set(a, e)
            if u.get("sink") is not None:
                e = act.mark(act.e.activation(s[:, 2:3], s[:, 0:1], ACT.Exp, bias=u["sink"]))
            if u.get("valid") is not None:
                dve.wait(e)
                e = dve.mark(dve.e.tensor_tensor(pr, pr, u["valid"], ALU.mult))
            weights[n] = e

        def turn(n):
            u = units[n]
            nk, kw = -(-u["w"] // P), min(P, u["w"])
            bs, cols = banks("turned", n, nk * P)
            pe.wait(weights[n], [self.bank[b].get() for b in bs])
            for j in range(nk):
                c = j * P
                m = pe.e.transpose(self.ps[0:kw, bs[c // cols], c % cols:c % cols + P],
                                   pbuf[:, n % n_p, c:c + kw], self.ident[:, :])
            m = pe.mark(m)
            act.wait(m, valued.get(n - n_pt))
            turned[n] = act.mark(act.e.copy(folded(ptbuf[0:kw, n % n_pt, 0:nk * P], bs), view(bs, kw, cols)))
            for b in bs:
                self.bank[b].set(turned[n])

        def values(n):
            u = units[n]
            nk, kw, vw = -(-u["w"] // P), min(P, u["w"]), u["vw"]
            b = out_bank(n)
            o = self.ps[:, b, (n % 4) * P:(n % 4) * P + vw]
            pe.wait(turned[n], self.bank[b].get())
            for j in range(nk):
                m = pe.e.matmul(o, ptbuf[0:kw, n % n_pt, j * P:(j + 1) * P], u["v"](u["k0"] // P + j),
                                start=j == 0, stop=j == nk - 1)
            valued[n] = pe.mark(m)
            dve.wait(valued[n], weights[n])
            posted[n] = u["post"](o, st[:, n % 4, :])
            self.bank[b].set(posted[n])

        n_u = len(units)
        if wide and filler is None:
            for n in range(n_u + 2):
                if n < n_u:
                    scores(n)
                    softmax(n)
                if 0 <= n - 1 < n_u:
                    turn(n - 1)
                if 0 <= n - 2:
                    values(n - 2)
        elif wide:
            for n in range(n_u + 1):
                if n < n_u:
                    scores(n)
                    softmax(n)
                filler(n)
                if n > 0:
                    values(n - 1)
                if n < n_u:
                    turn(n)
        else:
            for n in range(n_u + 3):
                if n < n_u:
                    scores(n)
                if 0 <= n - 2 < n_u:
                    turn(n - 2)
                if n < n_u:
                    softmax(n)
                if 0 <= n - 3:
                    values(n - 3)
        return posted[n_u - 1]

    def build(self):
        nc, p, ins, ctx = self.nc, self.p, self.ins, self.ctx
        self.n_loads, self.stores = 0, []
        self.ps = ctx.enter_context(nc.psum_tensor("ps", [P, 8, 512], F32))
        self.bank = [Last(p, f"bank{b}") for b in range(8)]
        self.w = Weights(p)
        self.ident = self.sb(ctx, "ident", [P, P])
        self.newton = self.sb(ctx, "newton", [P, 16])
        self.ones = self.sb(ctx, "ones", [P, 1])
        self.gx = self.sb(ctx, "gx", [P, 4, KD])
        self.gsub = self.sb(ctx, "subln", [P, 2])
        self.cvec = self.sb(ctx, "cvec", [P, 2, KD])
        self.halves = self.sb(ctx, "halves", [P, 2, 20])
        self.stat = self.sb(ctx, "stat", [P, 2, 20])
        self.squares_y = self.sb(ctx, "squares_y", [P, TX, 2])
        self.tmp_read = [None, None]
        self.csil = self.sb(ctx, "csil", [P, 2, KD])
        self.adab = self.sb(ctx, "adab", [P, 2, 3 * KD])
        self.postg = self.sb(ctx, "post_gains", [P, 2, KD])
        self.mod = self.sb(ctx, "mod", [P, 4, 3 * KD])
        m = [p.pool.mark(p.pool.e.memset(self.ones[:, :], 1.0))]
        self.s_rows = ExitStack()
        self.rows1 = self.sb(self.s_rows, "rows1", [P, TX, D])
        self.x_loaded = [self.load(self.rows1[:, t, :], self.xin()[:, t, :]) for t in range(TX)]
        loads = [self.load(self.ident[:, :], ins["ident"]),
                 self.load(self.gx[:, 0, :], ins["attn_pre_g"]), self.load(self.gx[:, 1, :], ins["mlp_pre_g"]),
                 self.load(self.gx[:, 2:4, :], ins["pre_g_2"]),
                 self.load(self.gsub[:, 0:1], ins["subln"]), self.load(self.cvec[:, 0, :], ins["c_2"]), self.load(self.cvec[:, 1, :], ins["c_ctx_2"]),
                 self.load(self.adab[:, :, :], ins["ada_b_cols"]), self.load(self.postg[:, :, :], ins["post_g_cols"])]
        self.const_ready = m + loads
        self.x_dram = nc.dram_tensor("x_scratch", [P, TX, D], F32).ap()
        self.gate_dram = nc.dram_tensor("gate_scratch", [3, D], F32).ap()
        self.engines4 = (p.pe, p.act, p.dve, p.pool)
        self.all_engines = (*self.engines4, p.sp)

        p.act.wait(self.const_ready)
        a = p.act.mark(p.act.e.activation(self.csil[:, :, :], self.cvec[:, :, :], ACT.Tanh, scale=0.5))
        p.dve.wait(a, self.const_ready)
        a = p.dve.mark(p.dve.e.scalar_tensor_tensor(self.csil[:, :, :], self.csil[:, :, :], 1.0, self.cvec[:, :, :],
                                                    ALU.add, ALU.mult))
        p.dve.wait(a)
        self.csil_ready = p.dve.mark(p.dve.e.tensor_scalar(self.csil[:, :, :], self.csil[:, :, :], 0.5, None, ALU.mult))

        self.gsub_ready = p.dve.mark(p.dve.e.tensor_scalar(self.gsub[:, 1:2], self.gsub[:, 0:1], 0.5 * (1.0 - LAM_INIT), None,
                                                           ALU.mult))

        self.piece_loaded = [Counter(p, f"mod_loaded{i}") for i in range(4)]
        self.piece_read = [Last(p, f"mod_piece_read{i}") for i in range(4)]
        self.acc_read, self.acc_ready = Last(p, "mod_acc_read"), Last(p, "mod_acc_ready")
        with ExitStack() as s_mod:
            with ExitStack() as s:
                h = self.sb(s, "h_hi", [P, KD, S], F32R, "right"), self.sb(s, "h_lo", [P, KD, S], F32R, "right")
                h_ready = self.block_one_attention(h, s)
                self.block_one_mlp(h, h_ready)
            s = s_mod.enter_context(ExitStack())
            self.modulation_buffers(s, 3, 2)
            x, y = self.sb(s, "x4", [P, TX, D], F32, "right"), self.sb(s, "y4", [P, TX, D], F32, "right")
            lx, gain = self.block_one_down(x, y, s)
            h6_stack = ExitStack()
            h = (self.sb(h6_stack, "h6_hi", [P, KD, TA * P], F32R), self.sb(h6_stack, "h6_lo", [P, KD, TA * P], F32R))
            h_ready = self.block_one_gate(x, y, lx, gain, h)
        with h6_stack:
            self.second_block(h, h_ready)
        for m in self.stores:
            p.sp.wait(m)

    def xin(self):
        return self.ins["x"].rearrange("(t p) d -> p t d", p=P)

    def modulated(self, layer, t):
        m = self.mod[:, 2 * layer + (t >= TX), :]
        return m[:, KD:2 * KD], m[:, 0:KD]

    def block_one_attention(self, h, s_h):
        p, ins = self.p, self.ins
        with self.s_rows:
            rows = self.rows1
            with ExitStack() as s2:
                self.attention_groups(s2, h, rows)
                p.meet()
            self.modulation_buffers(s_h, 2, 1)
            with ExitStack() as s2:
                ready = self.project_out(s2, h, rows)
                p.meet()
        return ready

    def attention_groups(self, s, h, orow):
        p, nc, ins = self.p, self.nc, self.ins
        pe, act, dve, pool = self.engines4
        w_in = ins["w_in"]
        sb = lambda n, sh, dt=F32: self.sb(s, n, sh, dt)
        w1 = [sb(f"cmp_w1_{n}", [P, 16, P]) for n in "kv"]
        w2 = [sb(f"cmp_w2_{n}", [P, HD]) for n in "kv"]
        pe_t = sb("cmp_pe", [P, 2, 16])
        khh = sb("k_hi_twice", [P, 3, S], F32R)
        pbuf = sb("p1", [P, 3, S])
        wg, wg_hi, wg_lo = (x.rearrange("p (k n) -> p k n", k=KD)
                            for x in (pbuf[:, 0, 0:KD * 24], khh[:, 0, 0:KD * 24], khh[:, 1, 0:KD * 24]))
        sink = sb("sink", [P, 8])
        gates = sb("gates", [P, TX, 24])
        valid = sb("valid", [P, TX, CMP_W])
        wg_loaded = self.load(wg, w_in[:, 1280:1304].rearrange("(k p) n -> p k n", p=P))
        small = [self.load(w1[0][:, :, :], ins["cmp_w1_k"].rearrange("(l r) h -> r l h", r=P)),
                 self.load(w1[1][:, :, :], ins["cmp_w1_v"].rearrange("(l r) h -> r l h", r=P)),
                 self.load(w2[0][:, :], ins["cmp_w2_k"]), self.load(w2[1][:, :], ins["cmp_w2_v"]),
                 self.load(pe_t[:, 0, :], ins["cmp_pe_k"]), self.load(pe_t[:, 1, :], ins["cmp_pe_v"]),
                 self.load(sink[:, :], self.row(ins["sinks"])), self.load(valid[:, :, :], ins["cmp_valid"])]
        junk = pbuf[:, 1:3, :].rearrange("p a n -> p (a n)")
        scaled = {}
        for t in range(TX):
            m = self.squares((orow[:, t, 0:512], orow[:, t, 512:D]), junk, t, [self.x_loaded[t], act.last()])
            if t % 2:
                r = self.inverse_rms(t - 1, t + 1, m)
                for u in (t - 1, t):
                    scaled[u] = r
        for t in range(TX):
            m = self.scale_rows(orow[:, t, :], orow[:, t, :], t, scaled[t])
            h_ready = self.turn_tile(orow[:, t, :], t, h, (4 + 2 * (t % 2), 5 + 2 * (t % 2)), m, gain=self.gx[:, 0, :])
        dve.wait(wg_loaded)
        a = dve.mark(dve.e.tensor_copy(wg_hi, wg))
        dve.wait(a)
        wg_ready = dve.mark(dve.e.tensor_tensor(wg_lo, wg, wg_hi, ALU.subtract))
        pe.wait(wg_ready, h_ready, self.bank[0].get())
        for k in range(KD):
            m = three(pe.e, self.ps[0:24, 0, :], (wg_hi[:, k, :], wg_lo[:, k, :]), (h[0][:, k, :], h[1][:, k, :]),
                      k == 0, k == KD - 1)
        gcol = pbuf[0:24, 1, :]
        act.wait(pe.mark(m))
        a = act.mark(act.e.copy(gcol, self.ps[0:24, 0, :]))
        pe.wait(a)
        for t in range(TX):
            m = pe.e.transpose(self.ps[:, 0, t * 24:(t + 1) * 24], gcol[:, t * P:(t + 1) * P], self.ident[0:24, 0:24])
        act.wait(pe.mark(m))
        a = act.mark(act.e.activation(gates[:, :, :], self.ps[:, 0, 0:TX * 24].rearrange("p (t n) -> p t n", t=TX),
                                      ACT.Tanh, scale=0.5))
        self.bank[0].set(a)
        dve.wait(a)
        gates_ready = dve.mark(dve.e.tensor_scalar(gates[:, :, :], gates[:, :, :], 0.5, 0.5, ALU.mult, ALU.add))

        qst = sb("q_stacked", [P, 8, S], F32R)
        klo = sb("k_lo", [P, 2, S], F32R)
        v = sb("v", [P, TX, 192])
        blocks = sb("cmp_blocks", [P, 2, 16, NCMP])
        ckhh, cklo = sb("ck_hi_twice", [P, CMP_W], F32R), sb("ck_lo", [HD, CMP_W], F32R)
        ckz = sb("ck_zero", [P, CMP_W])
        cv = sb("cv", [CMP_W, HD])
        hid = sb("cmp_hid", [P, 3, NCMP])
        bias = sb("alibi", [P, PER_G, NSA_BIAS_W + SWA_BIAS_W])
        st = sb("st1", [P, 4, 8])
        ptbuf = sb("pt1", [P, 2, S])
        part = sb("o_part", [P, 2, HD])
        bias_loaded = Counter(p, "alibi_loaded")
        attn_end = Last(p, "attn_end1")
        sink_g = sb("sink_g", [P, 2, PER_G])
        z = dve.mark(dve.e.memset(ckz[:, :], 0.0))
        dve.wait(z)
        zeroed = [dve.mark(dve.e.tensor_copy(ckhh[:, :], ckz[:, :])), dve.mark(dve.e.tensor_copy(cklo[:, :], ckz[0:HD, :])),
              dve.mark(dve.e.memset(cv[:, :], 0.0))]

        with p.loop("groups", GROUPS) as g:
            at = (512, 640, 768, 1024, 1816, 1944, 896, 1152)
            kv = self.w.push([(HD * j, HD, w_in[:, bass.ds(g * HD + c0, HD)]) for j, c0 in enumerate(at)])
            qt = self.w.push([(0, 256, w_in[:, bass.ds(g * 256, 256)]), (256, 256, w_in[:, bass.ds(g * 256 + 1304, 256)])])
            act.wait(attn_end.get())
            bias_ready = bias_loaded.inc(act.e.dma_start(
                bias[:, :, :], ins["alibi"][bass.ds(g, 1)].rearrange("g p h n -> (g p) h n")), 16)
            ready = [self.cols_product(h, kv, KD, j, j * P, None) for j in range(3)]
            for t in range(TX):
                vm = self.rows_product(h, kv, KD, t, 3 + t // 2, 320, 192, None, out_c0=(t % 2) * 192, fresh=t % 2 == 0)
            kv.release(vm)
            dve.wait(ready[0], small)
            for j in range(2):
                for par in range(2):
                    src = self.ps[j * HD:(j + 1) * HD, 0, :]
                    src = bass.AP(src.tensor, src.offset + par, [src.ap[0], [2, 16], [CMP_ST, NCMP]])
                    vec = pe_t[par * HD:(par + 1) * HD, j, :].rearrange("p (l o) -> p l o", o=1)
                    bm = dve.mark(dve.e.tensor_tensor(blocks[par * HD:(par + 1) * HD, j, :, :], src,
                                                      vec.to_broadcast([HD, 16, NCMP]), ALU.add))
            self.bank[0].set(bm)
            for j in range(3):
                b, r0 = (1, j * HD) if j < 2 else (2, 0)
                src = self.ps[r0:r0 + HD, b, :]
                top, other = (slice(0, HD), slice(HD, P)) if j < 2 else (slice(HD, P), slice(0, HD))
                a, l = split(p, khh[top, j, :], klo[top, j % 2, :], src, ready[b], None, twin=khh[other, j, :])
                self.bank[b].set(a, l)
            for b in range(2):
                src = self.ps[:, 3 + b, 0:384].rearrange("p (t n) -> p t n", t=2)
                act.wait(vm)
                self.bank[3 + b].set(act.mark(act.e.copy(v[:, 2 * b:2 * b + 2, :], src)))
            for j in range(4):
                b = 4 + j
                m = self.cols_product(h, qt, KD, b, j * P, None)
                for e in range(2):
                    top, other = (slice(0, HD), slice(HD, P)) if j < 2 else (slice(HD, P), slice(0, HD))
                    a, l = split(p, qst[top, 2 * j + e, :], qst[other, 2 * j + e, :],
                                 self.ps[e * HD:(e + 1) * HD, b, :], m, None, scale=-(HD ** -0.5))
                self.bank[b].set(a, l)
            qt.release(m)
            for j in range(2):
                pe.wait(bm, small, self.bank[j].get())
                for l in range(16):
                    m = pe.e.matmul(self.ps[:, j, 0:NCMP], w1[j][:, l, :], blocks[:, j, l, :], start=l == 0, stop=l == 15)
                hm = self.gelu_small(hid, self.ps[:, j, 0:NCMP], pe.mark(m))
                pe.wait(hm)
                if j == 0:
                    src = self.ps[0:HD, j, 64:64 + NCMP]
                    m = pe.mark(pe.e.matmul(src, w2[0][:, :], hid[:, 0, :], start=True, stop=True))
                    a, l = split(p, ckhh[0:HD, 0:NCMP], cklo[:, 0:NCMP], src, m, zeroed, twin=ckhh[HD:P, 0:NCMP])
                else:
                    src = self.ps[0:NCMP, j, 64:128]
                    m = pe.mark(pe.e.matmul(src, hid[:, 0, :], w2[1][:, :], start=True, stop=True))
                    act.wait(m, zeroed)
                    a = act.mark(act.e.copy(cv[0:NCMP, :], src))
                    l = None
                self.bank[j].set(a, l)
            a = dve.mark(dve.e.tensor_copy(sink_g[:, 0, :], sink[:, bass.ds(g * PER_G, PER_G)]))
            dve.wait(a)
            dve.mark(dve.e.tensor_scalar(sink_g[:, 1, :], sink_g[:, 0, :], -1.0, None, ALU.mult))
            p.meet()

            def nsa_post(head, t, which):
                def post(o, s):
                    a = dve.mark(dve.e.reciprocal(s[:, 3:4], s[:, 1:2]))
                    dve.wait(a, gates_ready)
                    b = dve.mark(dve.e.tensor_tensor(s[:, 4:5], s[:, 3:4],
                                                     gates[:, t, bass.ds(g * 12 + (head * 3 + which), 1)], ALU.mult))
                    dve.wait(b)
                    if which == 0:
                        return dve.mark(dve.e.tensor_scalar(part[:, 0, :], o, s[:, 4:5], None, ALU.mult))
                    dst = part[:, 1, :] if which == 1 else orow[:, t, bass.ds(g * 256 + head * HD, HD)]
                    return dve.mark(dve.e.scalar_tensor_tensor(dst, o, s[:, 4:5], part[:, which - 1, :], ALU.mult, ALU.add))
                return post

            def swa_post(head, t):
                def post(o, s):
                    a = dve.mark(dve.e.tensor_tensor(s[:, 3:4], s[:, 1:2], s[:, 2:3], ALU.add))
                    dve.wait(a)
                    a = dve.mark(dve.e.reciprocal(s[:, 4:5], s[:, 3:4]))
                    dve.wait(a)
                    dst = orow[:, t, bass.ds(g * 256 + (512 + head * HD), HD)]
                    return dve.mark(dve.e.tensor_scalar(dst, o, s[:, 4:5], None, ALU.mult))
                return post

            def qk(head, t, hh, lo):
                top = slice(0, HD) if head < 4 else slice(HD, P)
                return [(qst[:, head, t * P:(t + 1) * P], hh), (qst[top, head, t * P:(t + 1) * P], lo)]

            units = []
            for e in range(PER_G):
                for t in range(TX):
                    units.append(dict(
                        qk=qk(e, t, lambda a, b: ckhh[:, a:b], lambda a, b: cklo[:, a:b]), k0=0, w=CMP_W,
                        bias=bias[:, e, S + t * CMP_W:S + (t + 1) * CMP_W], bias_ready=bias_ready,
                        valid=valid[:, t, :], vw=HD, v=lambda k: cv[:, :], post=nsa_post(e, t, 0)))
                    for j in range(2):
                        c = HD * (1 + j)
                        units.append(dict(
                            qk=qk(e, t, lambda a, b, j=j: khh[:, j, a:b], lambda a, b, j=j: klo[0:HD, j, a:b]), k0=0,
                            w=(t + 1) * P, bias=bias[:, e, (TX - 1 - t) * P:S], vw=HD,
                            v=lambda k, c=c: v[:, k, c:c + HD], post=nsa_post(e, t, 1 + j)))
            for e in range(PER_G):
                for t in range(TX):
                    k0 = max(0, t - 1)
                    w = (t + 1 - k0) * P
                    units.append(dict(
                        qk=qk(4 + e, t, lambda a, b: khh[:, 2, a:b], lambda a, b: klo[HD:P, 0, a:b]), k0=k0 * P, w=w,
                        bias=bias[:, e, NSA_BIAS_W + SWA_BIAS_W - w:NSA_BIAS_W + SWA_BIAS_W], vw=HD,
                        init=sink_g[:, 1, e:e + 1], sink=sink_g[:, 0, e:e + 1],
                        v=lambda k: v[:, k, 0:HD], post=swa_post(e, t)))
            attn_end.set(self.attention(units, st, pbuf, ptbuf, False))
            p.meet()

    def gelu_small(self, hid, x, ready):
        act, dve = self.p.act, self.p.dve
        act.wait(ready)
        a = act.mark(act.e.activation(hid[:, 1, :], x, ACT.Square, scale=GELU_A))
        dve.wait(a)
        b = dve.mark(dve.e.scalar_tensor_tensor(hid[:, 2, :], hid[:, 1, :], 1.0, x, ALU.add, ALU.mult))
        act.wait(b)
        a = act.mark(act.e.activation(hid[:, 1, :], hid[:, 2, :], ACT.Tanh, scale=GELU_C))
        dve.wait(a)
        b = dve.mark(dve.e.scalar_tensor_tensor(hid[:, 2, :], hid[:, 1, :], 1.0, x, ALU.add, ALU.mult))
        dve.wait(b, self.p.pe.last())
        return dve.mark(dve.e.tensor_scalar(hid[:, 0, :], hid[:, 2, :], 0.5, None, ALU.mult))

    def modulation_buffers(self, s, n, layer):
        self.acc = self.sb(s, f"mod_acc{layer}", [P, 2, 512], F32, "right")
        self.piece = self.sb(s, f"mod_piece{layer}", [P, n, 512], F32, "right")
        self.n_pieces = n

    def modulation_block(self, layer, j):
        act, dve = self.p.act, self.p.dve
        src = self.ins["ada_w_2"][layer].rearrange("(k p) n -> p k n", p=P)
        loaded = {}

        def load(k):
            if k < KD:
                i = k % self.n_pieces
                act.wait(self.piece_read[i].get())
                loaded[k] = self.piece_loaded[i].inc(
                    act.e.dma_start(self.piece[:, i, :], src[:, k, bass.ds(j * 512, 512)]), 16)

        for k in range(self.n_pieces - 1):
            load(k)
        yield
        for k in range(KD):
            load(k + self.n_pieces - 1)
            i = k % self.n_pieces
            dve.wait(loaded[k], self.csil_ready, self.acc_read.get() if k == 0 else dve.last())
            for stream in range(2):
                acc, c = self.acc[:, stream, :], self.csil[:, stream, k:k + 1]
                if k == 0:
                    r = dve.mark(dve.e.tensor_scalar(acc, self.piece[:, i, :], c, None, ALU.mult))
                else:
                    r = dve.mark(dve.e.scalar_tensor_tensor(acc, self.piece[:, i, :], c, acc, ALU.mult, ALU.add))
            self.piece_read[i].set(r)
            self.acc_ready.set(r)
            yield

    def modulation_sum(self, layer, j, bank):
        pe, dve = self.p.pe, self.p.dve
        pe.wait(self.acc_ready.get(), self.bank[bank].get(), self.const_ready)
        for stream in range(2):
            for c in range(4):
                m = pe.e.matmul(self.ps[:, bank, 4 * stream + c:4 * stream + c + 1], self.acc[:, stream, c * P:(c + 1) * P],
                                self.ones[:, 0:1], start=True, stop=True)
        m = pe.mark(m)
        self.acc_read.set(m)
        dve.wait(m)
        b = dve.mark(dve.e.tensor_tensor(self.mod[:, 2 * layer:2 * layer + 2, bass.ds(j * 4, 4)],
                                         self.ps[:, bank, 0:8].rearrange("p (s c) -> p s c", s=2),
                                         self.adab[:, layer:layer + 1, bass.ds(j * 4, 4)].to_broadcast([P, 2, 4]), ALU.add))
        self.bank[bank].set(b)

    def modulation_end(self, layer, bank):
        pe, dve = self.p.pe, self.p.dve
        stored = []
        for stream in range(2):
            m, n = self.mod[:, 2 * layer + stream, :], 2 * layer + stream
            dve.wait(dve.last())
            dve.mark(dve.e.scalar_tensor_tensor(m[:, KD:2 * KD], m[:, KD:2 * KD], 1.0, self.gx[:, 2 + layer, :], ALU.add, ALU.mult))
            a = dve.mark(dve.e.tensor_tensor(m[:, 2 * KD:3 * KD], m[:, 2 * KD:3 * KD], self.postg[:, layer, :], ALU.mult))
            if n == 3:
                continue
            pe.wait(a, self.bank[bank].get())
            t = pe.mark(pe.e.transpose(self.ps[0:KD, bank, 0:P], m[:, 2 * KD:3 * KD], self.ident[:, :]))
            dve.wait(t, self.acc_read.get())
            turned = self.acc[0:KD, stream, 0:P]
            a = dve.mark(dve.e.tensor_copy(turned, self.ps[0:KD, bank, 0:P]))
            self.bank[bank].set(a)
            stored.append(self.store(self.gate_dram[n, :].rearrange("(k p) -> k p", k=KD), turned, a))
        self.acc_read.set(*stored)

    def project_out(self, s, h, rows):
        p, ins = self.p, self.ins
        act, dve = p.act, p.dve
        x = self.sb(s, "x2", [P, TX, D])
        gain = self.sb(s, "post1", [P, D])
        y = self.sb(s, "y2", [P, 2, D])
        lx = [self.load(gain[:, :], self.row(ins["attn_post_g"]))]
        lx += [self.load(x[:, t, :], self.xin()[:, t, :]) for t in range(TX)]
        w = [self.w.push([(0, 512, ins["w_o"][:, nh * 512:(nh + 1) * 512])]) for nh in range(2)]
        start = dve.last()
        mod = self.modulation_block(0, 0)
        out = {}

        def store(t, ready):
            self.store(self.x_dram[:, t, :], x[:, t, :], ready)
            for _ in range(3):
                next(mod, None)

        add, last, normed = self.normed_adder(x, lambda t: gain, y, [[lx[0], m] for m in lx[1:]], rows, store)

        def turn_in(t):
            return self.turn_tile(rows[:, t, :], t, h, (4, 5), start)

        def turn_out(t):
            out[t] = self.turn_tile(rows[:, t, :], t, h, (6, 7), normed[t], gain=self.gx[:, 1, :])

        self.tiles_product(TX, h, w, turn_in, add, last, turn_out)
        for _ in mod:
            pass
        dve.wait(self.stores)
        return out[TX - 1]

    def block_one_mlp(self, h, h_ready):
        self.s_gated = ExitStack()
        s = self.s_gated
        self.gated = self.sb(s, "g_hi", [P, KF, S], F32R), self.sb(s, "g_lo", [P, KF, S], F32R)
        with ExitStack() as s2:
            self.gate_up(s2, h, h_ready, *self.gated)
            self.p.meet()

    def block_one_down(self, x, y, s_x):
        p, ins = self.p, self.ins
        act = p.act
        self.modulation_end(0, 4)
        gain = self.sb(s_x, "post4", [P, D], F32, "right")
        lx = [self.load(gain[:, :], self.row(ins["mlp_post_g"]))]
        lx += [self.load(x[:, t, :], self.x_dram[:, t, :]) for t in range(TX)]
        square = self.squares_y
        with self.s_gated as s:
            parts = (8, 6, 4, 4)
            with p.loop("w_down", 2) as nh:
                k0 = 0
                for i, c in enumerate(parts):
                    w = self.w.push([(0, 512, ins["w_down"][:, bass.ds(nh * 512, 512)])], row0=k0 * P, chunks=c)
                    done = []
                    for t in range(TX):
                        done.append(self.rows_product(self.gated, w, c, t, t, 0, 512, None, start=k0 == 0,
                                                      stop=k0 + c == KF, k0=k0))
                        if t == 0 and i > 0:
                            self.modulation_sum(1, nh * 3 + (i - 1), 4)
                        if t == 0 and i < 3:
                            for _ in self.modulation_block(1, nh * 3 + i):
                                pass
                    w.release(done[-1])
                    k0 += c
                for t in range(TX):
                    act.wait(done[t])
                    half = y[:, t, bass.ds(nh * 512, 512)]
                    act.settle()
                    act.mark(act.e.activation(half, self.ps[:, t, :], ACT.Square, accum_out=square[:, t, bass.ds(nh, 1)]))
                    act.wait(act.last())
                    act.settle()
                    m = act.mark(act.e.activation(half, self.ps[:, t, :], ACT.Copy))
                    self.bank[t].set(m)
            p.dve.wait(act.last())
            y0 = TA + 2
            a = p.dve.mark(p.dve.e.tensor_tensor(self.stat[:, 0, y0:y0 + TX], square[:, :, 0], square[:, :, 1], ALU.add))
            self.rsqrt(self.stat[:, 1, y0:y0 + TX], self.stat[:, 0, y0:y0 + TX], D, a)
            p.meet()
        return lx, gain

    def gate_up(self, s, h, h_ready, ghi, glo):
        p, ins = self.p, self.ins
        pe, act, dve, pool = self.engines4
        conv = self.sb(s, "conv_wb", [P, 4, KF])
        lc = [self.load(conv[:, 0:3, :], ins["conv_w"]), self.load(conv[:, 3, :], ins["conv_b"])]
        c = self.sb(s, "conv_out", [P, 2, S])
        c_read = [Last(p, f"conv_read{i}") for i in range(2)]
        n_tiles = FF // FT
        act.wait(lc)
        dve.wait(lc)
        pe.wait(h_ready)

        def tile(col, col_u, j, b0, mod=None, steps=(0, 0), summed=None):
            w = self.w.push([(0, FT, ins["w_gate_up"][:, col]), (FT, FT, ins["w_gate_up"][:, col_u])])
            m = []
            for i in range(4):
                if i == 3 and summed is not None:
                    self.modulation_sum(0, summed, 3)
                m.append(self.cols_product(h, w, KD, b0 + i, (i % 2) * FT + (i // 2) * P, None))
            w.release(m[-1])
            for e in range(2):
                a_ps, u_ps = self.ps[:, b0 + 2 * e, :], self.ps[:, b0 + 2 * e + 1, :]
                je = j + e
                col1 = (lambda r: conv[:, r, bass.ds(je, 1)]) if not isinstance(je, int) else (lambda r: conv[:, r, je:je + 1])
                row = (lambda x: x[:, bass.ds(je, 1), :].rearrange("p a n -> p (a n)")) if not isinstance(je, int) else (lambda x: x[:, je, :])
                ce = c[:, e, :]
                act.wait(m[2 * e], c_read[e].get())
                a = act.mark(act.e.activation(ce, a_ps, ACT.Identity, bias=col1(3), scale=col1(2)))
                for r in (1, 0):
                    d = 2 - r
                    dve.wait(a, dve.last())
                    b = dve.mark(dve.e.scalar_tensor_tensor(ce[:, d:S], a_ps[:, 0:S - d], col1(r), ce[:, d:S], ALU.mult, ALU.add))
                act.wait(b)
                a = act.mark(act.e.activation(a_ps, ce, ACT.Square, scale=GELU_A))
                dve.wait(a)
                b = dve.mark(dve.e.scalar_tensor_tensor(a_ps, a_ps, 1.0, ce, ALU.add, ALU.mult))
                act.wait(b)
                a = act.mark(act.e.activation(a_ps, a_ps, ACT.Tanh, scale=GELU_C))
                dve.wait(a)
                b = dve.mark(dve.e.scalar_tensor_tensor(ce, a_ps, 1.0, ce, ALU.add, ALU.mult))
                self.bank[b0 + 2 * e].set(b)
                dve.wait(b, m[2 * e + 1])
                b = dve.mark(dve.e.scalar_tensor_tensor(u_ps, ce, 0.5, u_ps, ALU.mult, ALU.mult))
                c_read[e].set(b)
                act.wait(b)
                a = act.mark(act.e.copy(row(ghi), u_ps))
                dve.wait(a)
                b = dve.mark(dve.e.tensor_tensor(row(glo), u_ps, row(ghi), ALU.subtract))
                self.bank[b0 + 2 * e + 1].set(b)
                for _ in range(steps[e]):
                    next(mod)

        with p.loop("gate_up", n_tiles // 2) as i:
            mod = self.modulation_block(0, i + 1)
            for e in range(2):
                tile(bass.ds(i * (2 * FT) + e * FT, FT), bass.ds(i * (2 * FT) + (FF + e * FT), FT), i * 4 + 2 * e, 4 * e,
                     *((mod, (1, 3), i) if e == 0 else (mod, (3, 2), None)))
        t = n_tiles - 1
        if n_tiles % 2:
            tile(slice(t * FT, (t + 1) * FT), slice(FF + t * FT, FF + (t + 1) * FT), 2 * t, 0, summed=n_tiles // 2)

    def block_one_gate(self, x, y, lx, gain, h):
        p, ins = self.p, self.ins
        pe, act, dve = p.pe, p.act, p.dve
        KP = PE_IN // P
        with ExitStack() as s:
            prow, pcol = self.sb(s, "p_rows", [P, TX, PE_IN]), self.sb(s, "p_cols", [P, KP, S])
            wp = self.sb(s, "w_ple", [P, KP, D])
            th = self.sb(s, "gate_tanh", [P, 2, 512])
            ctx = self.sb(s, "ctx5", [P, TC, D])
            junk, tmp = self.sb(s, "junk5", [P, D]), self.sb(s, "tmp5", [P, 2, 512])
            lp = [self.load(prow[:, :, :], ins["p"].rearrange("(t p) d -> p t d", p=P)),
                  self.load(wp[:, :, :], ins["w_ple"].rearrange("(k p) n -> p k n", p=P))]
            lc = self.load(ctx[:, :, :], self.ctx_in())
            w = [self.w.push([(0, 512, ins["w_ple_gate"][:, nh * 512:(nh + 1) * 512])]) for nh in range(2)]
            pcol_ready = []

            def turn_p():
                for k in range(KP):
                    pe.wait(lp, self.bank[6 + k].get())
                    for t in range(TX):
                        m = pe.e.transpose(self.ps[:, 6 + k, t * P:(t + 1) * P], prow[:, t, k * P:(k + 1) * P], self.ident[:, :])
                    act.wait(pe.mark(m))
                    pcol_ready.append(act.mark(act.e.copy(pcol[:, k, :], self.ps[:, 6 + k, :])))
                    self.bank[6 + k].set(pcol_ready[-1])
                self.modulation_end(1, 6)

            def norm_context():
                for t in range(TC):
                    i = TX + t
                    m = self.squares((ctx[:, t, 0:512], ctx[:, t, 512:D]), junk, i, [lc, act.last()])
                r = self.inverse_rms(TX, TA, m)
                for t in range(TC):
                    normed[TX + t] = self.scale_rows(ctx[:, t, :], ctx[:, t, :], TX + t, [r, act.last()])

            normed, out, xs = {}, {}, {}
            th_read = [Last(p, f"tanh_read{i}") for i in range(2)]
            y0 = TA + 2

            added = {}

            def add_y(t):
                dve.wait(lx[0], lx[1 + t])
                a = dve.mark(dve.e.scalar_tensor_tensor(y[:, t, :], y[:, t, :], self.stat[:, 1, y0 + t:y0 + t + 1], gain[:, :],
                                                        ALU.mult, ALU.mult))
                dve.wait(a)
                added[t] = dve.mark(dve.e.tensor_tensor(x[:, t, :], x[:, t, :], y[:, t, :], ALU.add))

            def turn_in(t):
                if t < 2:
                    add_y(t)
                if t == 1:
                    turn_p()
                return self.turn_tile(x[:, t, :], t, h, (4, 5), added[t])

            def beside(t, nh, bank, done):
                if nh == 0 and t + 2 < TX:
                    add_y(t + 2)
                pe.wait(pcol_ready, self.bank[2 + nh].get())
                for k in range(KP):
                    m = pe.e.matmul(self.ps[:, 2 + nh, :], pcol[:, k, t * P:(t + 1) * P], wp[:, k, nh * 512:(nh + 1) * 512],
                                    start=k == 0, stop=k == KP - 1)
                m = pe.mark(m)
                act.wait(done, th_read[nh].get())
                a = act.mark(act.e.activation(th[:, nh, :], self.ps[:, bank, :], ACT.Tanh, scale=0.5))
                self.bank[bank].set(a)
                dve.wait(a, m)
                b = dve.mark(dve.e.scalar_tensor_tensor(th[:, nh, :], th[:, nh, :], 1.0, self.ps[:, 2 + nh, :], ALU.add, ALU.mult))
                self.bank[2 + nh].set(b)
                dve.wait(b)
                half = x[:, t, nh * 512:(nh + 1) * 512]
                dve.wait(done)
                xs[t] = dve.mark(dve.e.scalar_tensor_tensor(half, th[:, nh, :], 0.5, half, ALU.mult, ALU.add))
                th_read[nh].set(xs[t])
                if t >= 2 and nh == 1:
                    turn_out(TX + t - 2)

            def norm_x(t):
                m = self.squares((x[:, t, 0:512], x[:, t, 512:D]), y[:, t, :], t, xs[t])
                r = self.inverse_rms(t, t + 1, m)
                normed[t] = self.scale_rows(y[:, t, :], x[:, t, :], t, r)

            def add(t, banks, done):
                self.store(self.x_dram[:, t, :], x[:, t, :], xs[t])
                if t > 0:
                    norm_x(t - 1)
                else:
                    norm_context()

            def turn_out(t):
                row = y[:, t, :] if t < TX else ctx[:, t - TX, :]
                gain, shift = self.modulated(0, t)
                out[t] = self.turn_tile(row, t, h, (6, 7), normed[t], gain=gain, shift=shift, tmp=tmp)

            def ahead():
                self.first_head = self.head_tile(0)
                return self.products_ahead(h, self.first_head, [(0, 0), (1, 1), (2, 2), (TX, 3), (TX + 1, 4)], out)

            self.ahead = self.tiles_product(TX, h, w, turn_in, add, lambda: norm_x(TX - 1), turn_out, beside, ahead)
            dve.wait(self.stores)
            p.meet()
        return out[TX - 1]

    def ctx_in(self):
        return self.ins["ctx_2"].rearrange("(t p) d -> p t d", p=P)

    def second_block(self, h, h_ready):
        p, ins = self.p, self.ins
        act, dve = p.act, p.dve
        with ExitStack() as s:
            rows = self.sb(s, "rows6", [P, TA, D])
            with ExitStack() as s2:
                self.differential_heads(s2, h, h_ready, rows)
                p.meet()
            with ExitStack() as s2:
                x, gain = self.sb(s2, "x7", [P, TA, D]), self.sb(s2, "post7", [P, 2, D])
                y, tmp = self.sb(s2, "y7", [P, 2, D]), self.sb(s2, "tmp7", [P, 2, 512])
                act.wait(self.stores)
                lg = [self.load(gain[:, i, :], self.row(self.gate_dram[i, :])) for i in range(2)]
                lx = [self.load(x[:, t, :], self.x_dram[:, t, :]) for t in range(TX)]
                lx += [self.load(x[:, TX:TA, :], self.ctx_in())] * TC
                w = [self.w.push([(0, 512, ins["w_out_2"][0][:, nh * 512:(nh + 1) * 512])],
                                 gain=(self.gsub[:, 1:2], self.gsub_ready)) for nh in range(2)]
                start = dve.last()
                out = {}

                def store(t, ready):
                    if t < TX:
                        self.store(self.x_dram[:, t, :], x[:, t, :], ready)

                add, last, normed = self.normed_adder(x, lambda t: gain[:, t // TX, :], y, [[lg, m] for m in lx], rows, store)

                def turn_in(t):
                    return self.turn_tile(rows[:, t, :], t, h, (4, 5), start)

                def turn_out(t):
                    g, shift = self.modulated(1, t)
                    out[t] = self.turn_tile(rows[:, t, :], t, h, (6, 7), normed[t], gain=g, shift=shift, tmp=tmp)

                def ahead():
                    self.kv_tile = self.w.push([(0, 512, ins["b_w_in_2"][0][:, D:D + 512])])
                    return self.products_ahead(h, self.kv_tile, [(t, t) for t in range(TX)], out)

                done = self.tiles_product(TA, h, w, turn_in, add, last, turn_out, None, ahead)
                dve.wait(self.stores)
                p.meet()
            self.grouped(s, h, out[TA - 1], rows, self.kv_tile, done)
            p.meet()

    def rope(self, out, t2, x, cos, sin, half, ready):
        dve = self.p.dve
        n = x.shape[1]
        shape = [P, n, half]
        dve.wait(ready, dve.last())
        dve.mark(dve.e.tensor_tensor(out.rearrange("p v (a n) -> p (v a) n", a=2), x.rearrange("p v (a n) -> p (v a) n", a=2),
                                     cos.rearrange("p (o n) -> p o n", o=1).to_broadcast([P, 2 * n, half]), ALU.mult))
        a = sin.rearrange("p (o n) -> p o n", o=1)
        dve.mark(dve.e.tensor_tensor(t2[:, :, 0:half], x[:, :, half:2 * half], a[:, :, 0:half].to_broadcast(shape), ALU.mult))
        m = dve.mark(dve.e.tensor_tensor(t2[:, :, half:2 * half], x[:, :, 0:half], a[:, :, half:2 * half].to_broadcast(shape), ALU.mult))
        dve.wait(m)
        return dve.mark(dve.e.tensor_tensor(out, out, t2, ALU.add)), m

    def differential_heads(self, s, h, h_ready, orow):
        p, ins = self.p, self.ins
        pe, act, dve, pool = self.engines4
        sb = lambda n, sh, dt=F32: self.sb(s, n, sh, dt)
        T6 = TA * P
        cos, sin = sb("cos_a", [P, TX, HD // 2]), sb("sin_a", [P, TX, HD])
        lam = sb("lam", [P, 4])
        qst, khh = sb("q6", [P, 2, 2, T6], F32R), sb("k6_hi", [P, 2, 2, T6], F32R)
        klo = sb("k6_lo", [P, 2, T6], F32R)
        v = sb("v6", [P, 2, TA, P])
        zg = sb("z6", [P, 2, TA, P])
        rot, rot2 = sb("rot6", [P, 4, HD]), sb("rot6b", [P, 4, HD])
        st = sb("st6", [P, 4, 8])
        ss = sb("ss6", [P, 2, 8])
        o1, osq = sb("o1_6", [P, P]), sb("o_squares6", [P, P])
        pbuf, ptbuf = sb("p6", [P, 2, T6]), sb("pt6", [P, 2, T6])
        rot_read = Last(p, "rot_read6")
        prepared = [Last(p, f"head_prepared{b}") for b in range(2)]
        attended = [Last(p, f"head_attended{b}") for b in range(2)]
        lamb = pbuf[:, 0, 0:4 * HD]
        small = [self.load(cos[:, :, :], ins["cos_a"]), self.load(sin[:, :, :], ins["sin_a"]),
                 self.load(lamb, self.row(ins["a_lambda_2"]))]
        dve.wait(small)
        for j in range(2):
            m = dve.mark(dve.e.tensor_tensor_reduce(o1[:, j * HD:(j + 1) * HD], lamb[:, 2 * j * HD:(2 * j + 1) * HD],
                                                    lamb[:, (2 * j + 1) * HD:(2 * j + 2) * HD], 1.0, 0.0,
                                                    ALU.mult, ALU.add, lam[:, j:j + 1]))
        act.wait(m)
        a = act.mark(act.e.activation(lam[:, 2:4], lam[:, 0:2], ACT.Exp))
        dve.wait(a)
        lam_ready = dve.mark(dve.e.tensor_scalar(lam[:, 0:1], lam[:, 3:4], LAM_INIT, lam[:, 2:3], ALU.subtract, ALU.subtract))
        GB, TB = 5, 7

        def prepare(b, tile, early=()):
            def turn(t):
                e = t % 2
                pe.wait(roped[t], self.bank[TB].get() if e == 0 else None)
                for j in range(2):
                    m = pe.e.transpose(self.ps[:, TB, j * 256 + e * P:j * 256 + (e + 1) * P],
                                       rot[:, 2 * j:2 * j + 2, :].rearrange("p a n -> p (a n)"), self.ident[:, :])
                m = pe.mark(m)
                rot_read.set(m)
                if e == 1:
                    c0, c1 = (t - 1) * P, (t + 1) * P
                    for sub in range(2):
                        hi, lo = (slice(0, HD), slice(HD, P)) if sub == 0 else (slice(HD, P), slice(0, HD))
                        q = self.ps[sub * HD:(sub + 1) * HD, TB, 0:256]
                        k = self.ps[sub * HD:(sub + 1) * HD, TB, 256:512]
                        _, l = split(p, qst[hi, b, sub, c0:c1], qst[lo, b, sub, c0:c1], q, m, None, scale=-(HD ** -0.5))
                        split(p, khh[hi, b, sub, c0:c1], klo[hi, b, c0:c1], k, m, l, twin=khh[lo, b, sub, c0:c1])
                    self.bank[TB].set(act.last(), dve.last())

            roped = {}
            act.wait(attended[b].get())
            dve.wait(attended[b].get())
            for t in range(TA):
                bank = GB + t % 2
                if t in early:
                    bank, m = early[t]
                    if t > 0:
                        turn(t - 1)
                else:
                    pe.wait(h_ready, self.bank[bank].get())
                for k in range(KD if t not in early else 0):
                    pe.wait(tile.ready(k))
                    m = three(pe.e, self.ps[:, bank, :], (h[0][:, k, t * P:(t + 1) * P], h[1][:, k, t * P:(t + 1) * P]),
                              tile.hl(k, 0, 512), k == 0, k == KD - 1)
                    if k == KD - 1:
                        m = pe.mark(m)
                    if k == 3 and t > 0:
                        turn(t - 1)
                    yield
                x = self.ps[:, bank, 0:256].rearrange("p (v n) -> p v n", v=4)
                z = self.ps[:, bank, 384:512]
                r = rot[:, :, :]
                act.wait(m)
                act.mark(act.e.activation(zg[:, b, t, :], z, ACT.Tanh, scale=0.5))
                if t >= TX:
                    act.wait(rot_read.get())
                    a = act.mark(act.e.copy(r, x))
                va = act.mark(act.e.copy(v[:, b, t, :], self.ps[:, bank, 256:384]))
                if t < TX:
                    a, _ = self.rope(r, rot2[:, :, :], x, cos[:, t, :], sin[:, t, :], HD // 2, [va, rot_read.get()])
                dve.wait(va)
                d = dve.mark(dve.e.scalar_tensor_tensor(zg[:, b, t, :], zg[:, b, t, :], 1.0, z, ALU.add, ALU.mult))
                self.bank[bank].set(va, d)
                roped[t] = a
            tile.release(pe.last())
            yield
            turn(TA - 1)
            prepared[b].set(act.last(), dve.last())

        def attend(hd, b, filler):
            def post(t, sub):
                def f(o, s_):
                    a = dve.mark(dve.e.reciprocal(s_[:, 3:4], s_[:, 1:2]))
                    dve.wait(a, lam_ready)
                    if sub == 0:
                        return dve.mark(dve.e.tensor_scalar(o1[:, :], o, s_[:, 3:4], None, ALU.mult))
                    a = dve.mark(dve.e.tensor_tensor(s_[:, 4:5], s_[:, 3:4], lam[:, 0:1], ALU.mult))
                    dve.wait(a)
                    dst = orow[:, t, bass.ds(hd * P, P)]
                    a = dve.mark(dve.e.scalar_tensor_tensor(dst, o, s_[:, 4:5], o1[:, :], ALU.mult, ALU.add))
                    act.wait(a, act.last())
                    act.mark(act.e.activation(osq[:, :], dst, ACT.Square, accum_out=ss[:, 0, t:t + 1]))
                    return a
                return f

            units = []
            for t in (0, 4, 1, 5, 2, 3):
                for sub in range(2):
                    q0, hi = t * P, slice(sub * HD, (sub + 1) * HD)
                    units.append(dict(
                        qk=[(qst[:, b, sub, q0:q0 + P], lambda a0, a1, sub=sub: khh[:, b, sub, a0:a1]),
                            (qst[hi, b, sub, q0:q0 + P], lambda a0, a1, hi=hi: klo[hi, b, a0:a1])],
                        k0=0 if t < TX else S, w=T6 if t < TX else C, bias=None, vw=P,
                        v=lambda k: v[:, b, k, :], post=post(t, sub)))
            pe.wait(prepared[b].get())
            steps = () if filler is None else filler

            def fill(n):
                for _ in range(7 if n == 0 else 4 if n < 2 * TA - 1 else 2 if n < 2 * TA else KD):
                    next(steps, None)

            self.attention(units, st, pbuf, ptbuf, True, None if filler is None else fill)
            for _ in steps:
                pass
            r = self.rsqrt(ss[:, 1, 0:TA], ss[:, 0, 0:TA], P, act.last())
            dve.wait(r)
            for t in range(TA):
                o = orow[:, t, bass.ds(hd * P, P)]
                m = dve.mark(dve.e.scalar_tensor_tensor(o, o, ss[:, 1, t:t + 1], zg[:, b, t, :], ALU.mult, ALU.mult))
            attended[b].set(m, pe.last())

        tiles = [self.first_head, self.head_tile(1)]
        for _ in prepare(0, tiles[0], self.ahead):
            pass
        with p.loop("diff_heads", 3) as i:
            for e in range(2):
                self.head_tile(i * 2 + (2 + e))
                attend(i * 2 + e, e, prepare(1 - e, tiles[1 - e]))
        attend(6, 0, prepare(1, tiles[1]))
        attend(7, 1, None)

    def grouped(self, s, h, h_ready, orow, kv_tile, kv_done):
        p, ins = self.p, self.ins
        pe, act, dve, pool = self.engines4
        w_in = ins["b_w_in_2"][0]
        T6 = TA * P
        with ExitStack() as s2:
            sb = lambda n, sh, dt=F32: self.sb(s2, n, sh, dt)
            cos, sin = sb("cos_b", [P, TX, GD // 2]), sb("sin_b", [P, TX, GD])
            gq, gk = sb("gq", [P, GD]), sb("gk", [P, GD])
            khi, klo = sb("k8_hi", [P, 2, T6], F32R), sb("k8_lo", [P, 2, T6], F32R)
            v = sb("v8", [P, TA, 256])
            qhi, qlo = sb("q8_hi", [P, 2, 2, S], F32R), sb("q8_lo", [P, 2, 2, S], F32R)
            raw, rot = sb("raw8", [P, 2, 2, GD]), sb("rot8", [P, 2, 2, GD])
            rot2 = sb("rot8b", [P, 2, GD])
            st = sb("st8", [P, 4, 8])
            ss = sb("ss8", [P, 2, 4])
            junk = sb("junk8", [P, GD])
            pbuf, ptbuf = sb("p8", [P, 2, T6]), sb("pt8", [P, 2, T6])
            small = [self.load(cos[:, :, :], ins["cos_b"]), self.load(sin[:, :, :], ins["sin_b"]),
                     self.load(gq[:, :], self.row(ins["b_qk_g_2"][0:GD])),
                     self.load(gk[:, :], self.row(ins["b_qk_g_2"][GD:2 * GD]))]
            dve.wait(small)
            g_ready = dve.mark(dve.e.tensor_scalar(gq[:, :], gq[:, :], -(GD ** -0.5), None, ALU.mult))
            GB, TB = 5, 7
            raw_read, rot_read = Last(p, "raw_read8"), Last(p, "rot_read8")
            attended, made = [None, None], [{}, {}]

            def prepare(tile, order, gain, hi, lo, free, second, early=(), made=None):
                def norm(t):
                    return self.rsqrt(ss[:, 1, :], ss[:, 0, :], GD, [act.last(), rot_read.get()])

                def rope(t, e, r):
                    dve.wait(r, g_ready)
                    u = t - 1 + e
                    for a in range(2):
                        dst = raw if u < TX else rot
                        m = dve.mark(dve.e.scalar_tensor_tensor(dst[:, e, a, :], raw[:, e, a, :], ss[:, 1, 2 * e + a:2 * e + a + 1],
                                                                gain[:, :], ALU.mult, ALU.mult))
                    if u < TX:
                        m, _ = self.rope(rot[:, e, :, :], rot2[:, :, :], raw[:, e, :, :], cos[:, u, :], sin[:, u, :], GD // 2, m)
                    raw_read.set(m)
                    return m

                def turn(t, roped):
                    pe.wait(roped, self.bank[TB].get())
                    for e in range(2):
                        for a in range(2):
                            m = pe.e.transpose(self.ps[:, TB, (2 * e + a) * P:(2 * e + a + 1) * P], rot[:, e, a, :], self.ident[:, :])
                    m = pe.mark(m)
                    rot_read.set(m)
                    src = self.ps[:, TB, :].rearrange("p (e a n) -> p a e n", e=2, a=2)
                    h_, l_ = (x[:, :, (t - 1) * P:(t + 1) * P].rearrange("p a (e n) -> p a e n", e=2) for x in (hi, lo))
                    parts = split(p, h_, l_, src, m, free)
                    self.bank[TB].set(*parts)
                    if made is not None:
                        made[t - 1] = made[t] = parts

                pair = [None, 0, None]

                def beside():
                    t, j, r = pair
                    if t is not None:
                        if j == 0:
                            r = norm(t)
                        elif j in (3, 6):
                            r = rope(t, j // 3 - 1, r)
                        elif j == 11:
                            turn(t, r)
                        pair[1:] = j + 1, r

                for t in order:
                    bank = GB + t % 2
                    if t in early:
                        bank, m = early[t]
                        if t % 2 == 0:
                            while pair[0] is not None and pair[1] < 12:
                                beside()
                                yield
                    else:
                        pe.wait(h_ready, self.bank[bank].get())
                    for k in range(KD if t not in early else 0):
                        pe.wait(tile.ready(k))
                        m = three(pe.e, self.ps[:, bank, :], (h[0][:, k, t * P:(t + 1) * P], h[1][:, k, t * P:(t + 1) * P]),
                                  tile.hl(k, 0, 512), k == 0, k == KD - 1)
                        if k == KD - 1:
                            m = pe.mark(m)
                            tile.release(m)
                        beside()
                        yield
                    e = t % 2
                    act.wait(m, raw_read.get())
                    c = act.mark(act.e.copy(raw[:, e, :, :], self.ps[:, bank, 0:256].rearrange("p (a n) -> p a n", a=2)))
                    for a in range(2):
                        act.wait(act.last(), dve.last() if a + e == 0 else None)
                        c = act.mark(act.e.activation(junk[:, :], self.ps[:, bank, a * GD:(a + 1) * GD], ACT.Square,
                                                      accum_out=ss[:, 0, 2 * e + a:2 * e + a + 1]))
                    self.bank[bank].set(*second(t, bank, m))
                    if e == 1:
                        pair[:] = t, 0, None
                while pair[1] < 12:
                    beside()
                    yield

            def values(t, bank, done):
                return [act.mark(act.e.copy(v[:, t, :], self.ps[:, bank, 256:512]))]

            def silu(pair):
                def f(t, bank, done):
                    z, dst = self.ps[:, bank, 256:512], orow[:, t, pair * 256:(pair + 1) * 256]
                    a = act.mark(act.e.activation(dst, z, ACT.Tanh, scale=0.5))
                    dve.wait(a)
                    return a, dve.mark(dve.e.scalar_tensor_tensor(dst, dst, 1.0, z, ALU.add, ALU.mult))
                return f

            def push(pair):
                c = pair * 256
                return self.w.push([(0, 256, w_in[:, c:c + 256]), (256, 256, w_in[:, c + D + 512:c + D + 768])])

            def prepare_pair(pair, tile):
                b = pair % 2
                return prepare(tile, range(TX), gq, qhi[:, b, :, :], qlo[:, b, :, :], attended[b], silu(pair), made=made[b])

            def attend(pair, filler):
                g, b = pair // 2, pair % 2

                def post(t, e):
                    def f(o, s_):
                        a = dve.mark(dve.e.tensor_scalar(s_[:, 3:4], s_[:, 1:2], 2.0, None, ALU.mult))
                        dve.wait(a)
                        a = dve.mark(dve.e.reciprocal(s_[:, 4:5], s_[:, 3:4]))
                        dve.wait(a)
                        dst = orow[:, t, pair * 256 + e * GD:pair * 256 + (e + 1) * GD]
                        return dve.mark(dve.e.scalar_tensor_tensor(dst, o, s_[:, 4:5], dst, ALU.mult, ALU.mult))
                    return f

                units = []
                for e in range(2):
                    for t in range(TX):
                        q = [x[:, b, e, t * P:(t + 1) * P] for x in (qhi, qlo)]
                        kk = [(lambda a0, a1, x=x: x[:, g, a0:a1]) for x in (khi, klo)]
                        units.append(dict(qk=[(q[0], kk[0]), (q[0], kk[1]), (q[1], kk[0])], ready=made[b][t], k0=0, w=T6, bias=None, vw=P,
                                          v=lambda k: v[:, k, g * GD:(g + 1) * GD],
                                          post=post(t, e)))
                pe.wait(kv_made)
                steps = () if filler is None else filler

                def fill(n):
                    for _ in range(6 if n < 5 else 3 if n < 2 * TX else 12):
                        next(steps, None)

                self.attention(units, st, pbuf, ptbuf, True, None if filler is None else fill)
                for _ in steps:
                    pass
                attended[b] = pe.last()

            kv = prepare(kv_tile, (0, 1, TX, TX + 1, 2, 3), gk, khi, klo, None, values, kv_done)
            first = prepare_pair(0, push(0))
            for _ in range(2 * KD + 12):
                next(kv)
            for _ in range(KD):
                next(kv)
                next(first)
            for _ in kv:
                pass
            kv_made = [act.last(), dve.last()]
            for _ in first:
                pass
            n_pairs = D // 256
            for pair in range(n_pairs):
                attend(pair, prepare_pair(pair + 1, push(pair + 1)) if pair + 1 < n_pairs else None)
            p.meet()

        with ExitStack() as s2:
            x, gain = self.sb(s2, "x9", [P, TX, D]), self.sb(s2, "post9", [P, D])
            y = self.sb(s2, "y9", [P, 2, D])
            lg = self.load(gain[:, :], self.row(self.gate_dram[2, :]))
            lx = [self.load(x[:, t, :], self.x_dram[:, t, :]) for t in range(TX)]
            w = [self.w.push([(0, 512, ins["w_out_2"][1][:, nh * 512:(nh + 1) * 512])]) for nh in range(2)]
            start = dve.last()
            out = self.outs["out"].rearrange("(t p) d -> p t d", p=P)

            def turn_in(t):
                return self.turn_tile(orow[:, t, :], t, h, (4 + 2 * (t % 2), 5 + 2 * (t % 2)), start)

            def store(t, ready):
                self.store(out[:, t, :], x[:, t, :], ready)

            add, _, _ = self.normed_adder(x, lambda t: gain, y, [[lg, m] for m in lx], None, store)
            self.tiles_product(TX, h, w, turn_in, add, None, lambda t: None)


def constants():
    c = {"ident": np.eye(P, dtype=np.float32)}
    slopes = np.exp2(-8.0 * (np.arange(16, dtype=np.float32) + 1.0) / 16).astype(np.float32)
    pr = np.arange(P)[:, None]
    alibi = np.zeros((GROUPS, P, PER_G, NSA_BIAS_W + SWA_BIAS_W), np.float32)
    dist = pr + (S - P) - np.arange(S)[None, :]
    n = np.arange(CMP_W)
    dist_c = (np.arange(TX)[None, :, None] * P + np.arange(P)[:, None, None]) - (n * CMP_ST + CMP_L - 1)[None, None, :]
    ok_c = (dist_c >= 0) & (n < NCMP)
    dist_s = P + pr - np.arange(SWA_BIAS_W)[None, :]
    for g in range(GROUPS):
        for e in range(PER_G):
            nsa, swa = slopes[8 + g * PER_G + e], slopes[g * PER_G + e]
            alibi[g, :, e, 0:S] = np.where(dist >= 0, nsa * dist, BIG)
            alibi[g, :, e, S:NSA_BIAS_W] = np.where(ok_c, nsa * dist_c, BIG).reshape(P, TX * CMP_W)
            alibi[g, :, e, NSA_BIAS_W:] = np.where((dist_s >= 0) & (dist_s < P), swa * dist_s, BIG)
    c["alibi"] = alibi
    c["cmp_valid"] = ok_c.astype(np.float32)
    for name, hd in (("a", HD), ("b", GD)):
        axis = hd // 2
        freqs = (10000.0 ** (-np.arange(0, axis, 2, dtype=np.float32) / axis)).astype(np.float32)
        tok = np.arange(S)
        ang = np.concatenate([(tok // 64).astype(np.float32)[:, None] * freqs,
                              (tok % 64).astype(np.float32)[:, None] * freqs], axis=-1).astype(np.float32)
        cos, sin = np.cos(ang), np.sin(ang)
        for nm, v in (("cos", cos), ("sin", np.concatenate([-sin, sin], -1))):
            c[f"{nm}_{name}"] = np.ascontiguousarray(v.reshape(TX, P, -1).transpose(1, 0, 2).astype(np.float32))
    return c


def lay_out(a):
    by_feature = lambda v, *lead: np.ascontiguousarray(np.moveaxis(np.reshape(v, (*lead, -1, P)), -1, 0))
    o = {
        "x": a["x"][0], "p": a["p"][0, 0], "w_in": a["w_in"][0],
        "attn_pre_g": by_feature(a["attn_pre_g"][0]), "mlp_pre_g": by_feature(a["mlp_pre_g"][0]),
        "pre_g_2": by_feature(a["pre_g_2"], 2),
        "cmp_w1_k": a["cmp_w1_k"][0], "cmp_w2_k": a["cmp_w2_k"][0],
        "cmp_w1_v": a["cmp_w1_v"][0], "cmp_w2_v": a["cmp_w2_v"][0],
        "cmp_pe_k": by_feature(a["cmp_pe_k"][0]), "cmp_pe_v": by_feature(a["cmp_pe_v"][0]),
        "sinks": a["sinks"][0], "w_o": a["w_o"][0], "attn_post_g": a["attn_post_g"][0],
        "w_gate_up": a["w_gate_up"][0], "conv_w": by_feature(a["conv_w"][0], 3), "conv_b": by_feature(a["conv_b"][0]),
        "w_down": a["w_down"][0], "mlp_post_g": a["mlp_post_g"][0],
        "w_ple": a["w_ple"][0], "w_ple_gate": a["w_ple_gate"][0],
        "c_2": by_feature(a["c_2"][0]), "c_ctx_2": by_feature(a["c_ctx_2"]), "ctx_2": a["ctx_2"][0],
        "ada_w_2": a["ada_w_2"], "ada_b_cols": by_feature(a["ada_b_2"], 2),
        "post_g_cols": by_feature(a["post_g_2"], 2), "w_out_2": a["w_out_2"], "a_w_in_2": a["a_w_in_2"], "b_w_in_2": a["b_w_in_2"],
        "a_lambda_2": np.reshape(a["a_lambda_2"][0], -1), "subln": a["a_subln_g_2"][0][:, None],
        "b_qk_g_2": np.reshape(a["b_qk_g_2"][0], -1),
    }
    o.update(constants())
    return {k: np.ascontiguousarray(v) for k, v in o.items()}


def program(nc, arrays, counts):
    ins = {n: nc.dram_tensor("in_" + n, a.shape, mybir.dt.from_np(a.dtype), kind="ExternalInput").ap()
           for n, a in arrays.items()}
    outs = {"out": nc.dram_tensor("out_0", (S, D), F32, kind="ExternalOutput").ap()}
    Kernel(nc, ins, outs, counts)


def kernel(**inputs):
    import numpy as _np
    import concourse.bacc as _bacc
    from concourse.bass_utils import run_bass_kernel_spmd as _run

    arrays = lay_out({k: _np.asarray(v) for k, v in inputs.items()})
    counts = {}
    for _ in range(2):
        nc = _bacc.Bacc("TRN2", target_bir_lowering=False, num_devices=1)
        program(nc, arrays, counts)
    r = _run(nc, [{"in_" + n: a for n, a in arrays.items()}], core_ids=[0])
    return _np.reshape(r.results[0]["out_0"], (1, S, D))
```
